# Optimizing a Trainium2 kernel written in Bass

```python
import math
import jax, jax.numpy as jnp
from jax import lax
import numpy as np

D_MODEL = 2048
BATCH = 1
SEQ = 512
DEPTH = 1
DEC_BATCH = 8
DEC_SEQ = 1
PAST_LEN = 4096
PAGE_SIZE = 128

EPS = 1e-6
NEG_INF = -1e30
MIX_WIDTH = D_MODEL
A_GROUPS = 4
A_DIM = 128
A_WIDTH = A_GROUPS * A_DIM
CHUNK = 128
B_HEADS = 16
B_KV_HEADS = 2
B_HEAD_DIM = 64
GQA = B_HEADS // B_KV_HEADS
B_WIDTH = B_HEADS * B_HEAD_DIM
B_KV_WIDTH = B_KV_HEADS * B_HEAD_DIM
WINDOW = 128
N_BUCKETS = 32
MAX_DISTANCE = 128
C_HEADS = 4
C_QK_DIM = 64
C_V_DIM = 128
C_QK_WIDTH = C_HEADS * C_QK_DIM
C_WIDTH = C_HEADS * C_V_DIM
MLSTM_CHUNK = 64
IN_SPLITS = (A_WIDTH, A_WIDTH, B_WIDTH, B_KV_WIDTH, B_KV_WIDTH,
             C_QK_WIDTH, C_QK_WIDTH, C_WIDTH, C_WIDTH, C_HEADS, C_HEADS)
IN_WIDTH = sum(IN_SPLITS)
IN_OFFSETS = tuple(int(o) for o in np.cumsum(IN_SPLITS)[:-1])
D_FF = 5632
CONV_W = 3

kernel_name = "hybrid_sgu_swa_mlstm_convffn_step"

def rmsnorm(x, g):
    xf = x.astype(jnp.float32)
    y = xf * lax.rsqrt(jnp.mean(xf * xf, axis=-1, keepdims=True) + EPS)
    return (y * g.astype(jnp.float32)).astype(x.dtype)

def t5_bucket(dist):
    n = jnp.maximum(dist, 0)
    max_exact = N_BUCKETS // 2
    nf = jnp.maximum(n, 1).astype(jnp.float32)
    large = max_exact + (jnp.log(nf / max_exact) / math.log(MAX_DISTANCE / max_exact)
                         * (N_BUCKETS - max_exact)).astype(jnp.int32)
    return jnp.where(n < max_exact, n, jnp.minimum(large, N_BUCKETS - 1))

def rel_bias_logits(rel_bias, dist):
    b = jnp.take(rel_bias, t5_bucket(dist), axis=0).astype(jnp.float32)
    return jnp.moveaxis(b, -1, 0).reshape(B_KV_HEADS, GQA, *dist.shape)

def sink_attn(q, k, v, bias, valid, sink):
    s = jnp.einsum('...qhgd,...shd->...hgqs', q, k,
                   preferred_element_type=jnp.float32) * (B_HEAD_DIM ** -0.5) + bias
    s = jnp.where(valid, s, NEG_INF)
    sk = sink.astype(jnp.float32).reshape(B_KV_HEADS, GQA, 1, 1)
    mx = jnp.maximum(jnp.max(s, axis=-1, keepdims=True), sk)
    p = jnp.exp(s - mx)
    p = p / (jnp.sum(p, axis=-1, keepdims=True) + jnp.exp(sk - mx))
    return jnp.einsum('...hgqs,...shd->...qhgd', p.astype(v.dtype), v)

def swa_prompt(q, k, v, rel_bias, sink):
    Bn, T = q.shape[:2]
    nb = T // WINDOW
    qb = q.reshape(Bn, nb, WINDOW, B_KV_HEADS, GQA, B_HEAD_DIM)

    def band(a):
        ap = jnp.pad(a, ((0, 0), (WINDOW, 0), (0, 0), (0, 0))).reshape(
            Bn, nb + 1, WINDOW, B_KV_HEADS, B_HEAD_DIM)
        return jnp.concatenate([ap[:, :-1], ap[:, 1:]], axis=2)

    qi = jnp.arange(WINDOW)[:, None]
    kj = jnp.arange(2 * WINDOW)[None, :]
    dist = WINDOW + qi - kj
    kpos = jnp.arange(nb)[:, None, None] * WINDOW - WINDOW + kj
    valid = (dist >= 0) & (dist < WINDOW) & (kpos >= 0)
    o = sink_attn(qb, band(k), band(v), rel_bias_logits(rel_bias, dist),
                  valid[:, None, None], sink)
    return o.reshape(Bn, T, B_WIDTH)

def swa_sample(q, k, v, k_past, v_past, rel_bias, sink):
    Bn, T = q.shape[:2]
    kc = jnp.concatenate([k_past.astype(k.dtype), k], axis=1)
    vc = jnp.concatenate([v_past.astype(v.dtype), v], axis=1)
    qi = jnp.arange(T)[:, None]
    kpos = jnp.concatenate([jnp.arange(WINDOW) - WINDOW, jnp.arange(T)])[None, :]
    dist = qi - kpos
    valid = (dist >= 0) & (dist < WINDOW)
    o = sink_attn(q.reshape(Bn, T, B_KV_HEADS, GQA, B_HEAD_DIM), kc, vc,
                  rel_bias_logits(rel_bias, dist), valid, sink)
    return o.reshape(Bn, T, B_WIDTH)

def chunk_mlp(u, v, v_gain, w_s, b_s):
    Bn, T, _ = u.shape
    L = min(T, CHUNK)
    nc = T // L
    vn = rmsnorm(v.reshape(Bn, T, A_GROUPS, A_DIM), v_gain.reshape(A_GROUPS, A_DIM))
    ws = jnp.tril(w_s[:, :L, :L])
    mixv = jnp.einsum('gts,bnsgd->bntgd', ws, vn.reshape(Bn, nc, L, A_GROUPS, A_DIM)) \
        + jnp.transpose(b_s[:, :L])[:, :, None]
    out = u.reshape(Bn, nc, L, A_GROUPS, A_DIM) * mixv
    return out.reshape(Bn, T, A_WIDTH), vn.reshape(Bn, T, A_WIDTH)

def mlstm(q, k, v, ig, fg, C0, n0, m0):
    f32 = jnp.float32
    q, k, v, ig = q.astype(f32), k.astype(f32), v.astype(f32), ig.astype(f32)
    Bn, T, H, dk = q.shape
    dv = v.shape[-1]
    k = k * (dk ** -0.5)
    logf = jax.nn.log_sigmoid(fg.astype(f32))
    L = math.gcd(T, MLSTM_CHUNK)
    nc = T // L

    def chunks(a):
        return jnp.moveaxis(a.reshape(Bn, nc, L, *a.shape[2:]), 1, 0)

    causal = jnp.tril(jnp.ones((L, L), dtype=bool))[None, :, :, None]

    def step(carry, xs):
        C, n, m = carry
        qc, kc, vc, ic, lfc = xs
        b = jnp.cumsum(lfc, axis=1)
        dlog = b[:, :, None, :] - b[:, None, :, :] + ic[:, None, :, :]
        dlog = jnp.where(causal, dlog, -jnp.inf)
        inter = b + m[:, None, :]
        mt = jnp.maximum(inter, jnp.max(dlog, axis=2))
        s = jnp.einsum('bthd,bshd->btsh', qc, kc) * jnp.exp(dlog - mt[:, :, None, :])
        iw = jnp.exp(inter - mt)
        num = iw[..., None] * jnp.einsum('bthd,bhde->bthe', qc, C) \
            + jnp.einsum('btsh,bshe->bthe', s, vc)
        qn = iw * jnp.einsum('bthd,bhd->bth', qc, n) + jnp.sum(s, axis=2)
        h = num / jnp.maximum(jnp.abs(qn), jnp.exp(-mt))[..., None]
        bL = b[:, -1]
        m_new = mt[:, -1]
        wc = jnp.exp(bL[:, None] - b + ic - m_new[:, None])
        decay = jnp.exp(bL + m - m_new)
        C = decay[..., None, None] * C + jnp.einsum('bsh,bshd,bshe->bhde', wc, kc, vc)
        n = decay[..., None] * n + jnp.einsum('bsh,bshd->bhd', wc, kc)
        return (C, n, m_new), h

    (C, n, m), hs = lax.scan(step, (C0.astype(f32), n0.astype(f32), m0.astype(f32)),
                             (chunks(q), chunks(k), chunks(v), chunks(ig), chunks(logf)))
    h = jnp.moveaxis(hs, 0, 1).reshape(Bn, T, H, dv)
    return h, C, n, m

def conv_ffn(h, w_up, conv_w, conv_b, w_down, buf):
    z = h @ w_up
    T = z.shape[1]
    zp = jnp.concatenate([buf.astype(z.dtype), z], axis=1)
    zc = conv_b + sum(zp[:, j:j + T] * conv_w[j] for j in range(CONV_W))
    g, a = jnp.split(zc, 2, axis=-1)
    y = (jax.nn.silu(g) * a) @ w_down
    return y, zp[:, -(CONV_W - 1):]

def trunk_layer(x, norm1, w_in, a_v_gain, a_spatial_w, a_spatial_b, b_q_gain, b_k_gain,
                b_sinks, c_gate_bias, c_h_gain, w_out, norm2, w_up, ffn_conv_w, ffn_conv_b,
                w_down, rel_bias, k_past, v_past, C0, n0, m0, conv_buf):
    Bn, T, _ = x.shape
    dt = x.dtype
    h = rmsnorm(x, norm1)
    z = h @ w_in
    au, av, bq, bk, bv, cq, ck, cv, co, ci, cf = jnp.split(z, IN_OFFSETS, axis=-1)
    a_out, a_vrows = chunk_mlp(jax.nn.gelu(au, approximate=False), jax.nn.gelu(av, approximate=False),
                               a_v_gain, a_spatial_w, a_spatial_b)
    q = rmsnorm(bq.reshape(Bn, T, B_HEADS, B_HEAD_DIM), b_q_gain)
    k = rmsnorm(bk.reshape(Bn, T, B_KV_HEADS, B_HEAD_DIM), b_k_gain)
    v = bv.reshape(Bn, T, B_KV_HEADS, B_HEAD_DIM)
    if k_past is None:
        b_out = swa_prompt(q, k, v, rel_bias, b_sinks)
        k_new, v_new = k[:, -WINDOW:], v[:, -WINDOW:]
    else:
        b_out = swa_sample(q, k, v, k_past, v_past, rel_bias, b_sinks)
        k_new, v_new = k, v
    ig = ci + c_gate_bias[:C_HEADS]
    fg = cf + c_gate_bias[C_HEADS:]
    ch, C1, n1, m1 = mlstm(cq.reshape(Bn, T, C_HEADS, C_QK_DIM), ck.reshape(Bn, T, C_HEADS, C_QK_DIM),
                           cv.reshape(Bn, T, C_HEADS, C_V_DIM), ig, fg, C0, n0, m0)
    ch = rmsnorm(ch, c_h_gain.reshape(C_HEADS, C_V_DIM)).reshape(Bn, T, C_WIDTH)
    c_out = ch * jax.nn.sigmoid(co.astype(jnp.float32))
    mix = jnp.concatenate([a_out.astype(dt), b_out.astype(dt), c_out.astype(dt)], axis=-1) @ w_out
    x = x + mix.astype(dt)
    f, new_buf = conv_ffn(rmsnorm(x, norm2), w_up, ffn_conv_w, ffn_conv_b, w_down, conv_buf)
    x = x + f.astype(dt)
    return x, a_vrows, k_new, v_new, C1, n1, m1, new_buf

def setup_inputs(seed: int = 0) -> dict:
    key = jax.random.key(seed)
    ks = jax.random.split(key, 32)
    nrm = lambda k, s, sc: jax.random.normal(k, s, jnp.float32) * sc
    F2 = 2 * D_FF
    gate_b = jnp.concatenate([nrm(ks[15], (DEPTH, C_HEADS), 0.1),
                              3.0 + nrm(ks[16], (DEPTH, C_HEADS), 0.5)], axis=-1)
    return {
        "x_prompt": nrm(ks[0], (BATCH, SEQ, D_MODEL), 1.0),
        "x_sample": nrm(ks[1], (DEC_BATCH, DEC_SEQ, D_MODEL), 1.0),
        "cache_swa_k": nrm(ks[2], (DEPTH, DEC_BATCH, WINDOW, B_KV_HEADS, B_HEAD_DIM), 1.0),
        "cache_swa_v": nrm(ks[3], (DEPTH, DEC_BATCH, WINDOW, B_KV_HEADS, B_HEAD_DIM), 1.0),
        "state_mlstm_C": nrm(ks[4], (DEPTH, DEC_BATCH, C_HEADS, C_QK_DIM, C_V_DIM), 0.1),
        "state_mlstm_n": nrm(ks[5], (DEPTH, DEC_BATCH, C_HEADS, C_QK_DIM), 0.1),
        "state_mlstm_m": nrm(ks[6], (DEPTH, DEC_BATCH, C_HEADS), 0.5),
        "state_ffn_conv": nrm(ks[7], (DEPTH, DEC_BATCH, CONV_W - 1, F2), 1.0),
        "rel_bias": nrm(ks[8], (N_BUCKETS, B_HEADS), 0.5),
        "norm1": 1.0 + nrm(ks[9], (DEPTH, D_MODEL), 0.02),
        "w_in": nrm(ks[10], (DEPTH, D_MODEL, IN_WIDTH), D_MODEL ** -0.5),
        "a_v_gain": 1.0 + nrm(ks[11], (DEPTH, A_WIDTH), 0.02),
        "a_spatial_w": nrm(ks[12], (DEPTH, A_GROUPS, CHUNK, CHUNK), 0.5 * CHUNK ** -0.5),
        "a_spatial_b": 1.0 + nrm(ks[13], (DEPTH, A_GROUPS, CHUNK), 0.1),
        "b_q_gain": 1.0 + nrm(ks[14], (DEPTH, B_HEAD_DIM), 0.02),
        "b_k_gain": 1.0 + nrm(ks[17], (DEPTH, B_HEAD_DIM), 0.02),
        "b_sinks": nrm(ks[18], (DEPTH, B_HEADS), 0.5),
        "c_gate_bias": gate_b,
        "c_h_gain": 1.0 + nrm(ks[19], (DEPTH, C_WIDTH), 0.02),
        "w_out": nrm(ks[20], (DEPTH, MIX_WIDTH, D_MODEL), MIX_WIDTH ** -0.5),
        "norm2": 1.0 + nrm(ks[21], (DEPTH, D_MODEL), 0.02),
        "w_up": nrm(ks[22], (DEPTH, D_MODEL, F2), D_MODEL ** -0.5),
        "ffn_conv_w": nrm(ks[23], (DEPTH, CONV_W, F2), CONV_W ** -0.5),
        "ffn_conv_b": nrm(ks[24], (DEPTH, F2), 0.02),
        "w_down": nrm(ks[25], (DEPTH, D_FF, D_MODEL), D_FF ** -0.5),
    }

def reference(x_prompt, x_sample, cache_swa_k, cache_swa_v, state_mlstm_C, state_mlstm_n,
              state_mlstm_m, state_ffn_conv, rel_bias, norm1, w_in, a_v_gain, a_spatial_w,
              a_spatial_b, b_q_gain, b_k_gain, b_sinks, c_gate_bias, c_h_gain, w_out, norm2,
              w_up, ffn_conv_w, ffn_conv_b, w_down):
    Bp = x_prompt.shape[0]
    C0p = jnp.zeros((Bp, C_HEADS, C_QK_DIM, C_V_DIM), jnp.float32)
    n0p = jnp.zeros((Bp, C_HEADS, C_QK_DIM), jnp.float32)
    m0p = jnp.zeros((Bp, C_HEADS), jnp.float32)
    buf0p = jnp.zeros((Bp, CONV_W - 1, 2 * D_FF), x_prompt.dtype)
    xp, xs = x_prompt, x_sample
    P = [[] for _ in range(7)]
    S = [[] for _ in range(7)]
    for l in range(DEPTH):
        w = (norm1[l], w_in[l], a_v_gain[l], a_spatial_w[l], a_spatial_b[l], b_q_gain[l],
             b_k_gain[l], b_sinks[l], c_gate_bias[l], c_h_gain[l], w_out[l], norm2[l], w_up[l],
             ffn_conv_w[l], ffn_conv_b[l], w_down[l], rel_bias)
        outp = trunk_layer(xp, *w, None, None, C0p, n0p, m0p, buf0p)
        outs = trunk_layer(xs, *w, cache_swa_k[l], cache_swa_v[l], state_mlstm_C[l],
                           state_mlstm_n[l], state_mlstm_m[l], state_ffn_conv[l])
        xp, xs = outp[0], outs[0]
        for i in range(7):
            P[i].append(outp[i + 1])
            S[i].append(outs[i + 1])
    st = lambda lst: jnp.stack(lst, axis=0)
    return (xp, xs,
            st(P[1]), st(P[2]), st(S[1]), st(S[2]),
            st(P[3]), st(P[4]), st(P[5]),
            st(S[3]), st(S[4]), st(S[5]),
            st(P[6]), st(S[6]),
            st(S[0]))


_drawn_inputs = setup_inputs


def setup_inputs(seed=0):
    import zlib

    import numpy as np

    out = dict(_drawn_inputs(seed))
    spreads = {}
    factors = {'a_v_gain': 7.442,
     'b_q_gain': 8.0,
     'b_k_gain': 2.782,
     'b_sinks': 64.0,
     'c_h_gain': 8.0,
     'norm2': 2.716,
     'ffn_conv_b': 4.024,
     'a_spatial_b': 3.259}
    for name, (base, spread) in spreads.items():
        noise = np.random.default_rng([zlib.crc32(name.encode()), seed]).standard_normal(out[name].shape)
        drawn = base * np.exp(spread * noise) if base else spread * noise
        out[name] = __import__('jax').numpy.asarray(drawn.astype(out[name].dtype))
    for name, factor in factors.items():
        out[name] = (out[name] * factor).astype(out[name].dtype)
    return out
```

```python
from contextlib import ExitStack

import numpy as np

import concourse.bass as bass
from concourse import mybir

F32 = mybir.dt.float32
F32R = mybir.dt.float32r
ACT = mybir.ActivationFunctionType
ALU = mybir.AluOpType
AX_X = mybir.AxisListType.X

P = 128
D = 2048
KC = D // P
T = 512
S = 8
N = T + S
NH = N // 2
NB = T // P
EPS = 1e-6
NEG = -1e30
IN_W = 3848
FF = 5632
F2 = 2 * FF
FC = FF // P
GC = 4
NG = FC // GC
WINDOW = 128
NBUCKET = 32

Z_CQ, Z_CK, Z_CV, Z_CO, Z_BQ, Z_BK, Z_BV, Z_AU, Z_AV, Z_N = 0, 2, 4, 8, 12, 20, 21, 22, 26, 30
COL_C, COL_B, COL_A, COL_G = 2304, 1024, 0, 3840
K_ORDER = [4 * c + k for k in range(4) for c in range(4)]
MIX_TILES = [Z_AU + i for i in range(4)] + [Z_BQ + i for i in range(8)] + [Z_CO + i for i in range(4)]

U_OUT = Z_N
U_FFN = U_OUT + KC
U_GRP = 2 * GC
U_ALL = U_FFN + NG * (U_GRP + GC)


def bucket_of(dist):
    n = max(dist, 0)
    if n < NBUCKET // 2:
        return n
    large = NBUCKET // 2 + int(np.float32(np.log(np.float32(n) / np.float32(16))) / np.log(8.0) * 16)
    return min(large, NBUCKET - 1)


def bucket_table():
    e = np.zeros((NBUCKET + 1, 384), np.float32)
    for w in range(384):
        dist = 255 - w
        e[bucket_of(dist) if 0 <= dist < WINDOW else NBUCKET, w] = 1.0
    return e


def hybrid_layer(nc, io):
    ctx = ExitStack()
    base = (nc.sbuf_base + 31) // 32 * 32
    limit = nc.sbuf_usable_end // 32 * 32

    class Region:

        def __init__(self, start, size):
            self.start, self.end, self.at = start, start + size, start

        def again(self):
            return Region(self.start, self.end - self.start)

        def take(self, name, shape, dt=F32):
            size = int(np.prod(shape[1:])) * 4
            size = (size + 31) // 32 * 32
            assert self.at + size <= self.end, (name, self.at + size - self.end)
            t = nc.alloc_sbuf_tensor_at(name, shape, dt, offset=self.at)
            self.at += size
            return t

    ACTB = 2 * KC * N * 4
    XB = KC * N * 4
    keep = Region(base, limit - base - 2 * ACTB - XB)
    r_act = Region(keep.end, ACTB)
    r_z = Region(r_act.end, ACTB)
    r_x = Region(r_z.end, XB)

    ident = keep.take("ident", [P, P])
    ones = keep.take("ones", [P, P])
    pairones = keep.take("pairones", [P, P])
    causal = keep.take("causal", [P, P])
    vrow = keep.take("vrow", [48, P])
    vecs = keep.take("vecs", [P, 48])
    G1, G2, GAV, GCH, GBQ, GBK = 0, 16, 32, 36, 40, 41
    sel = keep.take("sel", [4, 4, P])
    rs1 = keep.take("rs1", [P, N])
    rs2 = keep.take("rs2", [P, N])
    small = keep.take("small", [P, 64])
    gbi = keep.take("gbi", [4, 1])
    gbf = keep.take("gbf", [36, 1])
    gain2 = keep.take("gain2", [P, 2])
    raw = keep.take("raw", [P, 2, KC * P])
    whi = keep.take("whi", [P, 4, 4, P], F32R)
    wlo = keep.take("wlo", [P, 4, 4, P], F32R)

    act_hi = r_act.take("act_hi", [P, KC, N], F32R)
    act_lo = r_act.take("act_lo", [P, KC, N], F32R)

    z0 = r_z.again()
    xtok = z0.take("xtok", [P, 5, D])
    xjunk = z0.take("xjunk", [P, D])
    wg_raw = z0.take("wg_raw", [P, KC, S])
    z1 = r_z.again()
    zT = z1.take("zT", [P, Z_N, N])
    z2 = r_z.again()
    h2_hi = z2.take("h2_hi", [P, KC, N], F32R)
    h2_lo = z2.take("h2_lo", [P, KC, N], F32R)
    xT = r_x.take("xT", [P, KC, N])

    ctx.enter_context(nc.allow_non_contiguous_dma(reason="small states, a few hundred elements"))
    ps = ctx.enter_context(nc.psum_tensor("ps", [P, 8, 512], F32))

    spill = nc.dram_tensor("x_spill", [P, KC * N], F32, kind="Internal").ap()
    BIAS_PITCH = (P + 1) * 384
    bias_rows = nc.dram_tensor("bias_rows", [16, P + 1, 384], F32, kind="Internal").ap()
    conv_rows = nc.dram_tensor("conv_rows", [P, 2 * FC, 20], F32, kind="Internal").ap()

    def sem(name):
        return ctx.enter_context(nc.semaphore(name))

    out_done = sem("out_done")
    stores = [0]

    def stored():
        stores[0] += 16
        return 16

    raw_in = [sem("raw_in0"), sem("raw_in1")]
    w_hi = sem("w_hi")
    w_lo = sem("w_lo")
    w_used = sem("w_used")
    z_free = sem("z_free")
    stage = sem("stage")
    chain_v, chain_a, chain_p = sem("chain_v"), sem("chain_a"), sem("chain_p")

    x_in = [sem(f"x_in{i}") for i in range(5)]
    vec_in, misc_in, wg_in = sem("vec_in"), sem("misc_in"), sem("wg_in")
    const_made = sem("const_made")
    ring_zero = sem("ring_zero")
    x_tr, x_ev_a, x_ev_v = sem("x_tr"), sem("x_ev_a"), sem("x_ev_v")
    vec_tr, vec_ev, rs_diag, rs_mm, rs_ready = (sem(n) for n in ("vec_tr", "vec_ev", "rs_diag", "rs_mm", "rs_ready"))
    var_v, var_a = sem("var_v"), sem("var_a")
    h_hi, h_lo = sem("h_hi"), sem("h_lo")
    wg_hi, wg_lo = sem("wg_hi"), sem("wg_lo")
    spilled = sem("spilled")

    def qslot(t, k):
        return t[:, k, :, :]

    def rawq(k, s):
        return raw[:, s, :].rearrange("p (c k n) -> p c k n", c=4, k=4)[:, :, k, :]

    def pair(b):
        return ps[:, b:b + 2, 0:NH]

    def halves(ap):
        return ap.rearrange("p (h n) -> p h n", h=2)

    w_in, w_out, w_up, w_down = io["w_in"], io["w_out"], io["w_up"], io["w_down"]

    def cols_of(w, col):
        return w[:, bass.ds(col, P)].rearrange("(c p) n -> p c n", p=P)

    def down_of(row, m):
        return w_down[bass.ds(row, GC * P), 512 * m:512 * m + 512].rearrange("(c p) n -> p c n", p=P)

    def unit_dst(u, down):
        if down:
            return raw[:, u, :].rearrange("p (c n) -> p c n", c=GC)
        return raw[:, u, :].rearrange("p (c n) -> p c n", c=KC)

    block = ctx.enter_context(nc.Block())

    cA, cX = r_act.again(), r_x.again()
    st_rows = cA.take("st_rows", [20, F2])
    st_cols = cA.take("st_cols", [P, 2 * FC, 20])
    rel33 = cX.take("rel33", [33, 16])
    hot = cX.take("hot", [33, 384])
    brow = cX.take("brow", [16, 384])
    cA, cX = r_act.again(), r_x.again()
    gi = cA.take("gi", [4, 8, N])
    gf = cX.take("gf", [36, 4, N])
    vtok = cA.take("vtok", [P, NB, 4, P + 1])
    kw = cA.take("kw", [P, NB, 4, 64])
    dmat = cA.take("dmat", [P, 1280])
    pmat = cA.take("pmat", [P, 1280])
    tmpm = cA.take("tmpm", [P, T])
    qab = cA.take("qab", [P, T])
    den = cA.take("den", [P, T])
    cst = cX.take("cst", [P, 2 * S, P])
    vm = cX.take("vm", [8, 4, S * P])
    cout = cA.take("cout", [P, 2, P + 1])
    ct = cA.take("ct", [P, 8, 4])
    cs = cA.take("cs", [P, 2, 16])
    emts = cA.take("emts", [P, 32])
    kws = cA.take("kws", [P, 2, S])
    ns = cA.take("ns", [P, 2 * S])
    nq = cA.take("nq", [P, 2, S])
    hs = cA.take("hs", [P, 3, 32])
    k8 = cA.take("k8", [8, 256])
    v8 = cA.take("v8", [8, 512])
    m0 = cA.take("m0", [4, S])
    gs = cA.take("gs", [4, 2, S])
    nA = Region(cA.at, r_act.end - cA.at)
    nsq = nA.take("nsq", [P, 2, N])
    nvar = nA.take("nvar", [P, 2, N])
    bA, bX = r_act.again(), r_x.again()
    kd = bA.take("kd", [P, 2, N])
    qst = bA.take("qst", [P, 2, N])
    vtb = bA.take("vtb", [P, NB, P])
    ktb = bA.take("ktb", [P, P])
    sx = bA.take("sx", [P, 4, 2, 257])
    pt = bA.take("pt", [P, 2, 512])
    bst = bA.take("bst", [P, 2, 2, 256])
    sinkbc = bA.take("sinkbc", [P, 16])
    mxn = bA.take("mxn", [P, 4, 2, 4])
    bsink = bA.take("bsink", [P, 1])
    kv8 = bA.take("kv8", [8, 2, P])
    assert bA.at <= nA.start
    kc_ = bX.take("kc_", [P, S, P])
    vc_ = bX.take("vc_", [P, S, P])
    kct = bX.take("kct", [P, S, P])
    qb_ = bX.take("qb_", [P, S, 16])
    s_t = bX.take("s_t", [P, P])
    s_s = bX.take("s_s", [P, 129])
    bias_s = bX.take("bias_s", [P, P])
    p_t = bX.take("p_t", [P, P])
    aA = r_act.again()
    vnt = aA.take("vnt", [P, NB, 4, P])
    ws = aA.take("ws", [P, 4, P])
    wst = aA.take("wst", [P, 4, P])
    bbc = aA.take("bbc", [P, 4, P])
    w00 = aA.take("w00", [P, 4])
    vn8 = aA.take("vn8", [8, 512])
    amix = aA.take("amix", [P, T])
    asmp = aA.take("asmp", [P, 4, S])
    assert aA.at <= nA.start
    fA = r_act.again()
    g_hi = fA.take("g_hi", [P, GC, N], F32R)
    g_lo = fA.take("g_lo", [P, GC, N], F32R)
    zg = fA.take("zg", [P, N + 2])
    za = fA.take("za", [P, N + 2])
    cg = fA.take("cg", [P, N])
    ca = fA.take("ca", [P, N])
    gm = fA.take("gm", [P, N])
    ztail = fA.take("ztail", [P, 2 * FC, S + 2])
    cpar = fA.take("cpar", [P, 2, GC, 20])
    ytok = fA.take("ytok", [P, NB, D])
    fZ = r_z.again()
    trow = fZ.take("trow", [S + 2, F2])
    ytok8 = fZ.take("ytok8", [S, D])

    ssq = keep.take("ssq", [P, 2, N])
    ssum = rs1

    sems = {}

    def s(name):
        if name not in sems:
            sems[name] = sem(name)
        return sems[name]

    bias_in = [sem("bias_in0"), sem("bias_in1")]
    begins = sem("begins")
    mix_hi, mix_lo, cpar_in = sem("mix_hi"), sem("mix_lo"), sem("cpar_in")
    DIAG = [0, 512, 896, 1152]
    USED_IN = 4 + 4 * Z_N
    USED_OUT = 4 + 4 * U_FFN
    BANKS = [4, 6]

    class Chain:

        def __init__(self, eng, semaphore):
            self.eng, self.sem, self.n = eng, semaphore, 0

        def __call__(self, ins):
            self.n += 1
            ins.then_inc(self.sem, 1)
            self.eng.wait_ge(self.sem, self.n)

    out_count = [0]

    def store(eng, dst, src):
        out_count[0] += 16
        eng.dma_start(dst, src).then_inc(out_done, 16)

    def barrier(eng, k):
        eng.drain().then_inc(stage, 1)
        eng.wait_ge(stage, 4 * k)

    def begun(eng):
        eng.sem_inc(begins)

    def heads_of(ap, q):
        return ap.rearrange("p (k q b) -> p q k b", q=2, b=S)[:, q]

    def norm_tiles(which):
        if which == "b":
            return [(Z_BQ + i, GBQ) for i in range(8)] + [(Z_BK, GBK)], pairones, 64, 4
        if which == "c":
            return [(Z_CV + i, GCH + i) for i in range(4)], ones, P, 0
        return [(Z_AV + i, GAV + i) for i in range(4)], ones, P, 13

    def norm_act(act, which):
        tiles, _, _, k0 = norm_tiles(which)
        for i in range(len(tiles) + 1):
            if i < len(tiles):
                k = k0 + i
                if k >= 2:
                    act.wait_ge(s("norm_mm"), k - 1)
                nc.scalar.activation(nsq[:, k % 2, :], zT[:, tiles[i][0], :], ACT.Square).then_inc(s("norm_sq"), 1)
            if i >= 1:
                k = k0 + i - 1
                act.wait_ge(s("norm_var"), k + 1)
                nc.scalar.activation(nvar[:, k % 2, :], nvar[:, k % 2, :], ACT.Sqrt).then_inc(s("norm_root"), 1)

    def norm_pe(pe, which):
        tiles, summer, _, k0 = norm_tiles(which)
        for i in range(len(tiles)):
            k = k0 + i
            b = BANKS[k % 2]
            pe.wait_ge(s("norm_sq"), k + 1)
            if k >= 2:
                pe.wait_ge(s("norm_var"), k - 1)
            for h in range(2):
                mm = nc.tensor.matmul(ps[:, b + h, 0:NH], summer[:], nsq[:, k % 2, h * NH:(h + 1) * NH],
                                      start=True, stop=True)
            mm.then_inc(s("norm_mm"), 1)

    def norm_dve(dve, which, link):
        tiles, _, width, k0 = norm_tiles(which)
        for i in range(len(tiles) + 1):
            if i < len(tiles):
                k = k0 + i
                dve.wait_ge(s("norm_mm"), k + 1)
                if k >= 2:
                    dve.wait_ge(s("norm_out"), k - 1)
                nc.vector.tensor_scalar(halves(nvar[:, k % 2, :]), pair(BANKS[k % 2]), 1.0 / width, EPS,
                                        ALU.mult, ALU.add).then_inc(s("norm_var"), 1)
            if i >= 1:
                k = k0 + i - 1
                tile, gain = tiles[i - 1]
                dve.wait_ge(s("norm_root"), k + 1)
                link(nc.vector.reciprocal(nvar[:, k % 2, :], nvar[:, k % 2, :]))
                nc.vector.scalar_tensor_tensor(out=zT[:, tile, :], in0=zT[:, tile, :], scalar=vecs[:, gain:gain + 1],
                                               in1=nvar[:, k % 2, :], op0=ALU.mult, op1=ALU.mult)\
                    .then_inc(s("norm_out"), 1)

    @block.tensor
    def _(pe):
        def unit_mm(q0, bank, before=None):
            for k in range(4):
                pe.wait_ge(w_lo, q0 + (k + 1))
                if before is not None:
                    before(k)
                tile_mm(k, bank, whi, wlo)

        def tile_mm(k, bank, w_h, w_l, x_h=None, x_l=None):
            x_h, x_l = x_h or act_hi, x_l or act_lo
            for kind, (w, x) in enumerate(((w_h, x_h), (w_h, x_l), (w_l, x_h))):
                for c in range(4):
                    for h in range(2):
                        mm = nc.tensor.matmul(ps[:, bank + h, 0:NH], w[:, k, c, :],
                                              x[:, 4 * c + k, h * NH:(h + 1) * NH],
                                              start=(k == 0 and kind == 0 and c == 0),
                                              stop=(k == 3 and kind == 2 and c == 3))
            mm.then_inc(w_used, 1)

        pe.wait_ge(const_made, 1)
        pe.wait_ge(vec_in, 16 * 8)
        nc.tensor.transpose(ps[:, 7, 0:42], vrow[0:42, :], ident[0:42, 0:42]).then_inc(vec_tr, 1)
        for idx in range(16):
            i, cg_ = idx // 4, idx % 4
            if cg_ == 0:
                pe.wait_ge(x_in[i], 16)
            if idx >= 6:
                pe.wait_ge(x_ev_v if idx % 2 else x_ev_a, (idx - 6) // 2 + 1)
            for c in range(4):
                t = nc.tensor.transpose(ps[:, idx % 6, c * P:(c + 1) * P], xtok[:, i, (4 * cg_ + c) * P:(4 * cg_ + c + 1) * P],
                                        ident[:])
            t.then_inc(x_tr, 1)
        pe.wait_ge(x_in[4], 16)
        for c in range(KC):
            t = nc.tensor.transpose(ps[:, 6, c * S:(c + 1) * S], xtok[0:S, 4, c * P:(c + 1) * P], ident[0:S, 0:S])
        t.then_inc(x_tr, 1)
        pe.wait_ge(wg_lo, 1)
        for k in range(4):
            pe.wait_ge(h_lo, 4 * (k + 1))
            tile_mm(k, 4, whi, wlo)
        pe.wait_ge(rs_diag, 1)
        for i in range(NB):
            nc.tensor.matmul(ps[:, 7, i * P:(i + 1) * P], ones[:], xjunk[:, i * P:(i + 1) * P], start=True, stop=True)
        nc.tensor.matmul(ps[:, 6, 256:256 + S], ones[0:S, :], xjunk[0:S, 512:512 + S], start=True, stop=True)\
            .then_inc(rs_mm, 1)

        with pe.Fori(0, Z_N // 2) as i:
            for u in range(2):
                pe.wait_ge(z_free, i * 2 + (u + 1))
                unit_mm(i * 8 + 4 * u, 2 * u)

        pe.wait_ge(z_free, Z_N + 2)
        pe.wait_ge(s("p_in"), 48)
        for r in range(4):
            for c in range(22):
                k = 22 * r + c
                t = nc.tensor.transpose(ps[:, r, 20 * c:20 * c + 20], st_rows[:, k * P:(k + 1) * P], ident[0:20, 0:20])
            t.then_inc(s("p_tr"), 1)
        pe.wait_ge(s("rel_in"), 32)
        pe.wait_ge(s("rel_set"), 1)
        nc.tensor.matmul(ps[0:16, 6, 0:384], rel33[:], hot[:], start=True, stop=True).then_inc(s("p_tr"), 1)
        pe.wait_ge(s("p_tr"), 5)
        barrier(pe, 1)

        for h in range(4):
            b = (6, 7, 4, 5)[h]
            if h == 2:
                pe.wait_ge(s("c_gates_read"), 1)
            for j in range(NB):
                t = nc.tensor.transpose(ps[:, b, j * P:(j + 1) * P], zT[:, Z_CV + h, j * P:(j + 1) * P], ident[:])
            t.then_inc(s("c_vt"), 1)
        pe.wait_ge(s("c_vt_read"), 1)
        for h in range(4):
            t = nc.tensor.transpose(ps[0:S, 6, h * P:(h + 1) * P], zT[:, Z_CV + h, T:N], ident[:])
        t.then_inc(s("c_v8"), 1)
        pe.wait_ge(s("c_vt_read"), 4)
        pe.wait_ge(s("c_rows"), 1)
        for j in range(NB):
            nc.tensor.transpose(ps[:, 7, 4 * j:4 * j + 4], gi[:, 2, j * P:(j + 1) * P], ident[0:4, 0:4])
            nc.tensor.transpose(ps[:, 7, 16 + 4 * j:20 + 4 * j], gi[:, 7, j * P:(j + 1) * P], ident[0:4, 0:4])
        for hp in range(2):
            for q in range(2):
                nc.tensor.matmul(ps[64 * q:64 * q + 64, 7, 64 + 16 * hp:80 + 16 * hp], sel[:, 2 * hp + q, 0:64],
                                 gs[:].rearrange("p a b -> p (a b)"), start=True, stop=True)
        for h in range(4):
            mm = nc.tensor.matmul(ps[:, 7, 128 + S * h:128 + S * (h + 1)], sel[:, h, :], gi[:, 6, T:N], start=True, stop=True)
        mm.then_inc(s("c_small"), 1)
        for t2 in range(2):
            for j in range(NB):
                t = nc.tensor.transpose(ps[:, 4 + t2, j * P:(j + 1) * P], zT[:, Z_CK + t2, j * P:(j + 1) * P], ident[:])
            t.then_inc(s("c_kt"), 1)
        pe.wait_ge(s("c_v8_read"), 1)
        pe.wait_ge(s("c_kws"), 1)
        for hp in range(2):
            t = nc.tensor.transpose(ps[0:S, 6, hp * P:(hp + 1) * P], kws[:, hp, :], ident[:])
        t.then_inc(s("c_k8"), 1)
        pe.wait_ge(s("c_kw"), 2)
        for h in range(4):
            r = 64 * (h % 2)
            for j in range(NB):
                mm = nc.tensor.matmul(ps[r:r + 64, 7, 129 * (h // 2):129 * (h // 2) + 129], kw[:, j, h, :],
                                      vtok[:, j, h, :], start=(j == 0), stop=(j == NB - 1))
        mm.then_inc(s("c_mem"), 1)
        pe.wait_ge(s("c_vm"), 4)
        pe.wait_ge(s("c_k8_read"), 1)
        for hp in range(2):
            if hp:
                pe.wait_ge(s("c_outer_read"), 1)
            for q in range(2):
                for half in range(2):
                    mm = nc.tensor.matmul(ps[64 * q:64 * q + 64, 4 + half, :], k8[:, hp * P + 64 * q:hp * P + 64 * q + 64],
                                          vm[:, 2 * hp + q, half * 512:half * 512 + 512], start=True, stop=True)
            mm.then_inc(s("c_outer"), 1)
        pe.wait_ge(s("c_outer_read"), 2)
        pe.wait_ge(s("c_nq"), 1)
        for h in range(4):
            r = 64 * (h % 2)
            for b in range(S):
                nc.tensor.matmul(ps[:, 6 - h % 2, S * h + b:S * h + b + 1], cst[r:r + 64, 2 * b + h // 2, :],
                                 zT[r:r + 64, Z_CQ + h // 2, T + b:T + b + 1], start=True, stop=True)
            nc.tensor.matmul(ps[:, 6 - h % 2, 64 + S * h:64 + S * (h + 1)], ones[r:r + 64, :], nq[r:r + 64, h // 2, :],
                             start=True, stop=True).then_inc(s("c_num8"), 1)
        pe.wait_ge(s("c_num8_read"), 1)
        for h in range(4):
            r, t2 = 64 * (h % 2), h // 2
            if h:
                pe.wait_ge(s("c_head"), h)
            nc.tensor.matmul(ps[:, 4, :], sel[:, h, :], gi[:, 5, 0:T], start=True, stop=True).then_inc(s("c_bc"), 1)
            for j in range(NB):
                b = 5 - j % 2
                if j == 1:
                    pe.wait_ge(s("c_decay"), h + 1)
                if j >= 2:
                    pe.wait_ge(s("c_p"), 4 * h + j - 1)
                nc.tensor.matmul(ps[:, b, 0:T - j * P], zT[r:r + 64, Z_CK + t2, j * P:(j + 1) * P],
                                 zT[r:r + 64, Z_CQ + t2, j * P:T], start=True, stop=True).then_inc(s("c_s"), 1)
            for j in range(NB):
                pe.wait_ge(s("c_p"), 4 * h + j + 1)
                p_j = pmat[:, DIAG[j]:DIAG[j] + T - j * P]
                nc.tensor.matmul(ps[:, 6, j * P:T], vtok[:, j, h, 0:P], p_j, start=(j == 0), stop=(j == NB - 1))
                mm = nc.tensor.matmul(ps[:, 7, j * P:T], ones[:], p_j, start=(j == 0), stop=(j == NB - 1))
            nc.tensor.matmul(ps[:, 4, :], sel[:, h, :], gi[:, 6, 0:T], start=True, stop=True).then_inc(s("c_num"), 1)
        pe.wait_ge(s("c_head"), 4)
        norm_pe(pe, "c")
        pe.wait_ge(s("norm_mm"), 4)
        barrier(pe, 2)

        norm_pe(pe, "b")
        pe.wait_ge(s("norm_out"), 13)
        for j in range(NB):
            t = nc.tensor.transpose(ps[:, 0, j * P:(j + 1) * P], zT[:, Z_BV, j * P:(j + 1) * P], ident[:])
        t.then_inc(s("b_t"), 1)
        nc.tensor.transpose(ps[:, 1, 0:P], zT[:, Z_BK, T - P:T], ident[:])
        nc.tensor.transpose(ps[0:S, 1, 128:256], zT[:, Z_BK, T:N], ident[:])
        nc.tensor.transpose(ps[0:S, 1, 256:384], zT[:, Z_BV, T:N], ident[:]).then_inc(s("b_t"), 1)
        pe.wait_ge(s("kc_in"), 16 * 4)
        for b in range(S):
            t = nc.tensor.transpose(ps[:, 2 + b // 4, (b % 4) * P:(b % 4 + 1) * P], kc_[:, b, :], ident[:])
        t.then_inc(s("b_kct"), 1)
        pe.wait_ge(s("b_kct_read"), 2)
        pe.wait_ge(s("b_q8"), 1)
        for b in range(S):
            mm = nc.tensor.matmul(ps[:, 2, b * 16:b * 16 + 16], kct[:, b, :], qb_[:, b, :], start=True, stop=True)
        mm.then_inc(s("b_s8"), 1)
        pe.wait_ge(s("b_s8_read"), 1)
        nc.tensor.transpose(ps[:, 3, 0:P], s_t[:], ident[:]).then_inc(s("b_s8t"), 1)
        pe.wait_ge(s("b_p8"), 1)
        nc.tensor.transpose(ps[:, 2, 0:P], s_s[:, 0:P], ident[:]).then_inc(s("b_p8t"), 1)
        pe.wait_ge(s("b_p8t_read"), 1)
        for b in range(S):
            mm = nc.tensor.matmul(ps[:, 3, b * 16:b * 16 + 16], vc_[:, b, :], p_t[:, b * 16:b * 16 + 16],
                                  start=True, stop=True)
        mm.then_inc(s("b_o8"), 1)
        pe.wait_ge(s("b_vk"), 1)
        for kv in range(2):
            with pe.Fori(0, 2) as it:
                first = it * 8 + 16 * kv

                def qk(n):
                    sl, i = n // 4, n % 4
                    pe.wait_ge(s("b_pair"), it * 2 + (4 * kv + sl + 1))
                    pe.wait_ge(s("b_sc_free"), first + (n + 1))
                    for r in range(2):
                        lo = 0 if i else P
                        mm = nc.tensor.matmul(ps[:, 4 - 2 * r + n % 2, lo:256],
                                              qst[64 * r:64 * r + 64, sl, i * P:(i + 1) * P],
                                              kd[64 * r:64 * r + 64, kv, (i - 1) * P + lo:(i + 1) * P],
                                              start=True, stop=True)
                    mm.then_inc(s("b_qk"), 1)

                def turn(n):
                    i = n % 4
                    pe.wait_ge(s("b_prob"), first + (n + 1))
                    pe.wait_ge(s("b_pt"), first + (n + 1))
                    for r in range(2):
                        for kb in range(0 if i else 1, 2):
                            t = nc.tensor.transpose(ps[:, 6, (2 * r + kb) * P:(2 * r + kb + 1) * P],
                                                    sx[:, n % 4, r, kb * P:(kb + 1) * P], ident[:])
                    t.then_inc(s("b_turn"), 1)

                def pv(n):
                    i = n % 4
                    pe.wait_ge(s("b_pt"), first + (n + 2))
                    pe.wait_ge(s("b_o_free"), first + (n + 1))
                    for r in range(2):
                        for kb in range(0 if i else 1, 2):
                            mm = nc.tensor.matmul(ps[64 * r:64 * r + 64, 7 * (n % 2), 0:P],
                                                  vtb[:, i - 1 + kb, 64 * kv:64 * kv + 64],
                                                  pt[:, n % 2, (2 * r + kb) * P:(2 * r + kb + 1) * P],
                                                  start=(kb == 0 or i == 0), stop=(kb == 1))
                    mm.then_inc(s("b_o"), 1)

                for n in range(8 + 3):
                    if n < 8:
                        qk(n)
                    if 2 <= n < 10:
                        turn(n - 2)
                    if n >= 3:
                        pv(n - 3)
        pe.wait_ge(s("b_ended"), 2)
        barrier(pe, 3)

        pe.wait_ge(s("a_in"), 48)
        for g in range(4):
            t = nc.tensor.transpose(ps[:, 0, g * P:(g + 1) * P], ws[:, g, :], ident[:])
        t.then_inc(s("a_wt"), 1)
        norm_pe(pe, "a")
        for g in range(4):
            pe.wait_ge(s("norm_out"), 13 + g + 1)
            if g == 3:
                pe.wait_ge(s("a_vt_read"), 1)
            for j in range(NB):
                t = nc.tensor.transpose(ps[:, (1, 2, 3, 1)[g], j * P:(j + 1) * P],
                                        zT[:, Z_AV + g, j * P:(j + 1) * P], ident[:])
            t.then_inc(s("a_vt"), 1)
        pe.wait_ge(s("a_wt_read"), 1)
        for g in range(4):
            t = nc.tensor.transpose(ps[0:S, 0, g * P:(g + 1) * P], zT[:, Z_AV + g, T:N], ident[:])
        t.then_inc(s("a_v8"), 1)
        pe.wait_ge(s("a_wst"), 1)
        for g in range(4):
            pe.wait_ge(s("a_vt_read"), g + 1)
            b = 4 + g
            if g == 0:
                pe.wait_ge(s("norm_var"), 17)
            for j in range(NB):
                mm = nc.tensor.matmul(ps[:, b, j * P:(j + 1) * P], vnt[:, j, g, :], wst[:, g, :], start=True, stop=True)
            mm.then_inc(s("a_mix"), 1)
        pe.wait_ge(s("a_mix"), 4)
        barrier(pe, 4)

        for u in range(2):
            pe.wait_ge(z_free, U_OUT + u + 1)
            unit_mm(4 * (U_OUT + u), 2 * u,
                    before=(lambda k: pe.wait_ge(mix_lo, 4 * (k + 1))) if u == 0 else None)
        with pe.Fori(U_OUT // 2 + 1, U_FFN // 2) as i:
            for u in range(2):
                pe.wait_ge(z_free, i * 2 + (u + 1))
                unit_mm(i * 8 + 4 * u, 2 * u)

        def up_mm(q0, bank, before=None):
            for k in range(4):
                pe.wait_ge(w_lo, q0 + (k + 1))
                if before is not None:
                    before(k)
                tile_mm(k, bank, whi, wlo, h2_hi, h2_lo)

        def down_mm(q0, d0):
            for k in range(4):
                pe.wait_ge(w_lo, q0 + (k + 1))
                pe.wait_ge(s("d_add"), d0 + (k + 1))
                b = 4 + 2 * (k % 2)
                for kind, (w, x) in enumerate(((whi, g_hi), (whi, g_lo), (wlo, g_hi))):
                    for c in range(4):
                        for h in range(2):
                            mm = nc.tensor.matmul(ps[:, b + h, 0:NH], w[:, k, c, :], x[:, c, h * NH:(h + 1) * NH],
                                                  start=(kind == 0 and c == 0), stop=(kind == 2 and c == 3))
                mm.then_inc(w_used, 1)
                yield k

        def first_up(k):
            pe.wait_ge(s("h2_lo"), 13 + k)

        def sum_squares():
            pe.wait_ge(s("o_sum"), KC)
            for h in range(2):
                mm = nc.tensor.matmul(ps[:, 4 + h, 0:NH], ones[:], ssum[:, h * NH:(h + 1) * NH], start=True, stop=True)
            mm.then_inc(s("o_sum_mm"), 1)

        def up_units(q0, use0, j, before=None):
            for u in range(2):
                pe.wait_ge(z_free, use0 + (2 * j + u + 1))
                up_mm(q0 + 4 * u, 2 * u, before if u == 0 else None)
                if before is not None and u == 0:
                    sum_squares()

        up_units(4 * U_FFN, U_FFN, 0, first_up)
        for j in range(1, GC):
            up_units(4 * U_FFN + 8 * j, U_FFN, j)
        with pe.Fori(1, NG) as i:
            q0, use0 = i * 48 + 4 * (U_FFN + U_GRP - 12), i * 8 + U_FFN
            up_units(q0, use0, 0)
            pe.wait_ge(s("g_lo"), i * GC)
            for m in range(GC):
                for _ in down_mm(q0 + (8 + 4 * m), i * 16 + (4 * m - 16)):
                    pass
            for j in range(1, GC):
                up_units(q0 + (16 + 8 * j), use0, j)

        def turn_tail(r):
            b = 2 + r % 2
            if r >= 2:
                pe.wait_ge(s("t_read"), r - 1)
            for c in range(4):
                t = nc.tensor.transpose(ps[0:S + 2, b, c * P:(c + 1) * P], ztail[:, 4 * r + c, :], ident[:])
            t.then_inc(s("t_turn"), 1)

        def turn_y(dt):
            pe.wait_ge(s("d_add"), (NG - 1) * 16 + dt + 3)
            if dt >= 2:
                pe.wait_ge(s("y_read"), dt - 1)
            for j in range(NB):
                t = nc.tensor.transpose(ps[:, dt % 2, j * P:(j + 1) * P], xT[:, dt, j * P:(j + 1) * P], ident[:])
            t.then_inc(s("y_turn"), 1)

        pe.wait_ge(z_free, U_FFN + 8 * NG + 2)
        tails = iter(range(FC // 2))
        for _ in range(6):
            turn_tail(next(tails))
        pe.wait_ge(s("g_lo"), NG * GC)
        for m in range(GC):
            for k in down_mm(4 * (U_ALL - GC + m), (NG - 1) * 16 + 4 * m):
                if 4 * m + k >= 1:
                    turn_y(4 * m + k - 1)
                    turn_tail(next(tails))
        turn_y(15)
        turn_tail(next(tails))
        assert next(tails, None) is None
        pe.wait_ge(s("t_read"), FC // 2)
        for q in range(4):
            if q == 0:
                pe.wait_ge(s("d_add"), NG * 16 + 2)
            for c in range(4):
                t = nc.tensor.transpose(ps[0:S, 4 + q, c * P:(c + 1) * P], xT[:, 4 * q + c, T:N], ident[:])
        t.then_inc(s("y8_turn"), 1)

    @block.scalar
    def _(act):
        link = Chain(act, chain_a)

        def q_hi(q, k, slot, landed):
            if k == 0:
                act.wait_ge(raw_in[slot], landed)
            act.wait_ge(w_used, q + 1)
            nc.scalar.activation(whi[:, k, :, :], rawq(k, slot), ACT.Copy)\
                .then_inc(w_hi, 1)

        def unit_hi(q0, slot, landed):
            for k in range(4):
                q_hi(q0 + k, k, slot, landed)

        for rows, name, a, b in (((0, 16), "norm1", 0, D), ((16, 32), "norm2", 0, D),
                                 ((32, 36), "a_v_gain", 0, 512), ((36, 40), "c_h_gain", 0, 512)):
            act.dma_start(vrow[rows[0]:rows[1], :], io[name].rearrange("l (c p) -> (l c) p", p=P)).then_inc(vec_in, 16)
        act.dma_start(wg_raw[:], w_in[:, COL_G:COL_G + 8].rearrange("(c p) n -> p c n", p=P)).then_inc(wg_in, 16)
        for row, name in ((40, "b_q_gain"), (41, "b_k_gain")):
            for h in range(2):
                act.dma_start(vrow[row:row + 1, 64 * h:64 * h + 64], io[name]).then_inc(vec_in, 16)
        cgb = io["c_gate_bias"].rearrange("l g -> g l")
        act.dma_start(gbi[:], cgb[0:4]).then_inc(misc_in, 16)
        act.dma_start(gbf[32:36, :], cgb[4:8]).then_inc(misc_in, 16)
        store(act, io["ffn_conv_sample"][0, :, 0, :], io["state_ffn_conv"][0, :, 1, :])

        for idx in range(0, 16, 2):
            i, c4 = idx // 4, idx % 4
            act.wait_ge(x_tr, idx + 1)
            nc.scalar.activation(xT[:, 4 * c4:4 * c4 + 4, i * P:(i + 1) * P],
                                 ps[:, idx % 6, :].rearrange("p (c n) -> p c n", c=4), ACT.Copy).then_inc(x_ev_a, 1)
        act.wait_ge(x_ev_a, 8)
        act.wait_ge(x_ev_v, 9)
        act.wait_ge(vec_ev, 1)
        act.wait_ge(wg_in, 16)
        act.wait_ge(ring_zero, 2)
        gates = wg_raw[:].rearrange("p (c k) n -> p k c n", k=4)
        nc.scalar.activation(whi[:, :, :, 0:4], gates[:, :, :, 0:4], ACT.Copy)
        nc.scalar.activation(whi[:, :, :, 32:36], gates[:, :, :, 4:8], ACT.Copy).then_inc(wg_hi, 1)
        for c in K_ORDER:
            nc.scalar.activation(act_hi[:, c, :], xT[:, c, :], ACT.Copy, scale=vecs[:, G1 + c:G1 + c + 1]).then_inc(h_hi, 1)
        act.wait_ge(var_v, 1)
        nc.scalar.activation(small[:, 16:21], small[:, 8:13], ACT.Sqrt).then_inc(var_a, 1)

        unit_hi(0, 0, 16)
        with act.Fori(0, Z_N // 2) as i:
            unit_hi(i * 8 + 4, 1, i * 16 + 16)
            unit_hi(i * 8 + 8, 0, i * 16 + 32)

        act.wait_ge(w_used, USED_IN)
        act.dma_start(st_rows[0:16, :], io["state_ffn_conv"].rearrange("l b j f -> (l b j) f")).then_inc(s("p_in"), 16)
        act.dma_start(st_rows[16:19, :], io["ffn_conv_w"][0]).then_inc(s("p_in"), 16)
        act.dma_start(st_rows[19:20, :], io["ffn_conv_b"]).then_inc(s("p_in"), 16)
        act.wait_ge(spilled, 16)
        act.dma_start(rel33[0:32, :], io["rel_bias"]).then_inc(s("rel_in"), 16)
        act.dma_start(hot[:], io["bucket_table"]).then_inc(s("rel_in"), 16)
        for r in range(0, 4, 2):
            act.wait_ge(s("p_tr"), r + 1)
            link(nc.scalar.activation(st_cols[:, 22 * r:22 * r + 22, :],
                                      ps[:, r, 0:440].rearrange("p (c n) -> p c n", n=20), ACT.Copy))
        act.wait_ge(s("p_cols"), 2)
        act.dma_start(conv_rows, st_cols[:]).then_inc(s("p_out"), 16)
        act.wait_ge(s("p_tr"), 5)
        link(nc.scalar.activation(brow[:], ps[0:16, 6, 0:384], ACT.Copy, scale=8.0))
        act.dma_start(bias_rows, brow[:].rearrange("h (a w) -> h a w", a=1).broadcast_to([16, P + 1, 384])).then_inc(s("p_out"), 16)
        act.wait_ge(s("p_out"), 32)
        barrier(act, 1)

        act.dma_start(m0[:], io["state_mlstm_m"].rearrange("l b h -> h (l b)")).then_inc(misc_in, 16)
        for q in range(2):
            act.dma_start(cst[64 * q:64 * q + 64, :, :],
                          io["state_mlstm_C"].rearrange("l b (k two) d e -> two d (l b k) e", two=2)[q]).then_inc(s("c_st"), 16)
            act.dma_start(ns[64 * q:64 * q + 64, :],
                          io["state_mlstm_n"].rearrange("l b (k two) d -> two d (l b k)", two=2)[q]).then_inc(s("c_st"), 16)
        act.wait_ge(s("c_fabs"), 1)
        link(nc.scalar.activation(gf[32:36, 2, :], gf[32:36, 1, :], ACT.Exp, scale=-1.0))
        nc.scalar.activation(gf[32:36, 2, :], gf[32:36, 2, :], ACT.Ln, bias=1.0).then_inc(s("c_ln"), 1)
        for h in range(4):
            act.wait_ge(s("c_vt"), h + 1)
            nc.scalar.activation(vtok[:, :, h, 0:P], ps[:, (6, 7, 4, 5)[h], :].rearrange("p (j n) -> p j n", j=NB),
                                 ACT.Copy).then_inc(s("c_vt_read"), 1)
        act.wait_ge(s("c_lines"), 1)
        nc.scalar.activation(gi[:, 6, :], gi[:, 4, :], ACT.Exp, scale=-1.0)
        nc.scalar.activation(gi[:, 7, 0:T], gi[:, 2, 0:T], ACT.Exp, bias=gi[:, 5, T - 1:T])
        nc.scalar.activation(gs[:].rearrange("p a b -> p (a b)"), gs[:].rearrange("p a b -> p (a b)"), ACT.Exp)\
            .then_inc(s("c_exp"), 1)
        act.wait_ge(s("c_v8"), 1)
        nc.scalar.activation(v8[:], ps[0:S, 6, :], ACT.Copy).then_inc(s("c_v8_read"), 1)
        act.wait_ge(s("c_lines"), 1)
        store(act, io["m_prompt"].rearrange("l b h -> h (l b)"), gi[:, 4, T - 1:T])
        store(act, io["m_sample"].rearrange("l b h -> h (l b)"), gi[:, 4, T:N])
        act.wait_ge(s("c_mem_read"), 1)
        for q in range(2):
            store(act, io["C_prompt"].rearrange("l b (k two) d e -> two d (l b k) e", two=2)[q], cout[64 * q:64 * q + 64, :, 0:P])
            store(act, io["n_prompt"].rearrange("l b (k two) d -> two d (l b k)", two=2)[q], cout[64 * q:64 * q + 64, :, P])
        act.wait_ge(s("c_nq"), 1)
        act.wait_ge(s("c_outer_read"), 2)
        for q in range(2):
            store(act, io["n_sample"].rearrange("l b (k two) d -> two d (l b k)", two=2)[q], ns[64 * q:64 * q + 64, :])
            store(act, io["C_sample"].rearrange("l b (k two) d e -> two d (l b k) e", two=2)[q], cst[64 * q:64 * q + 64, :, :])
        act.wait_ge(s("c_num8"), 4)
        for q in range(2):
            abs8 = nc.scalar.activation(heads_of(hs[:, 0, :], q), heads_of(ps[:, 6 - q, 64:96], q), ACT.Abs)
        abs8.then_inc(s("c_abs8"), 1)
        for h in range(4):
            act.wait_ge(s("c_masked"), h + 1)
            if h:
                act.wait_ge(s("c_p"), 4 * h)
            for j in range(NB):
                b_j = ct[:, j, h:h + 1]
                last = nc.scalar.activation(dmat[:, DIAG[j]:DIAG[j] + P], tmpm[:, j * P:(j + 1) * P], ACT.Exp, bias=b_j)
                if j < NB - 1:
                    last = nc.scalar.activation(dmat[:, DIAG[j] + P:DIAG[j] + T - j * P], ps[:, 4, (j + 1) * P:T],
                                                ACT.Exp, bias=b_j)
            last.then_inc(s("c_decay"), 1)
            act.wait_ge(s("c_num"), h + 1)
            if h:
                act.wait_ge(s("c_head"), h)
            nc.scalar.activation(qab[:], ps[:, 7, :], ACT.Abs).then_inc(s("c_abs"), 1)
        act.wait_ge(s("c_head"), 4)
        nc.scalar.activation(zT[:, Z_CO:Z_CO + 4, :], zT[:, Z_CO:Z_CO + 4, :], ACT.Sigmoid).then_inc(s("c_sig"), 1)
        norm_act(act, "c")
        act.wait_ge(out_done, out_count[0])
        barrier(act, 2)

        if True:
            act.dma_start(kc_[1:P, :, :], io["cache_swa_k"][0, :, 1:P].rearrange("b w h d -> w b (h d)")).then_inc(s("kc_in"), 16)
            act.dma_start(vc_[1:P, :, :], io["cache_swa_v"][0, :, 1:P].rearrange("b w h d -> w b (h d)")).then_inc(s("kc_in"), 16)
        sinks = io["b_sinks"]
        act.dma_start(sinkbc[:], bass.AP(tensor=sinks.tensor, offset=sinks.offset, ap=[[0, P], [1, 16]])).then_inc(s("b_in"), 16)
        act.dma_start(bsink[:], bass.AP(tensor=sinks.tensor, offset=sinks.offset, ap=[[0, S], [1, 16], [1, 1]])).then_inc(s("b_in"), 16)
        act.dma_start(bias_s[:, 1:P], bass.AP(tensor=bias_rows.tensor, offset=128, ap=[[0, S], [BIAS_PITCH, 16], [1, P - 1]])).then_inc(s("b_in"), 16)
        act.dma_start(bias_s[:, 0:1], bass.AP(tensor=bias_rows.tensor, offset=255, ap=[[0, S], [BIAS_PITCH, 16], [1, 1]])).then_inc(s("b_in"), 16)
        norm_act(act, "b")
        act.wait_ge(s("b_t"), 1)
        link(nc.scalar.activation(vtb[:], ps[:, 0, :].rearrange("p (j n) -> p j n", j=NB), ACT.Copy))
        act.wait_ge(s("b_t"), 2)
        link(nc.scalar.activation(ktb[:], ps[:, 1, 0:P], ACT.Copy))
        link(nc.scalar.activation(kv8[:], ps[0:S, 1, 128:384].rearrange("p (a n) -> p a n", a=2), ACT.Copy))
        act.dma_start(kc_[0:1, :, :], kv8[:, 0, :]).then_inc(s("kc_in"), 16)
        act.dma_start(vc_[0:1, :, :], kv8[:, 1, :]).then_inc(s("kc_in"), 16)
        act.drain().then_inc(s("b_vk_a"), 1)
        store(act, io["k_prompt"].rearrange("l b w h d -> (l b w) (h d)"), ktb[:])
        store(act, io["v_prompt"].rearrange("l b w h d -> (l b w) (h d)"), vtb[:, NB - 1, :])
        store(act, io["k_sample"].rearrange("l b w h d -> (l b w) (h d)"), kv8[:, 0, :])
        store(act, io["v_sample"].rearrange("l b w h d -> (l b w) (h d)"), kv8[:, 1, :])
        for i in range(2):
            act.wait_ge(s("b_kct"), 1)
            nc.scalar.activation(kct[:, 4 * i:4 * i + 4, :], ps[:, 2 + i, :].rearrange("p (j n) -> p j n", j=NB),
                                 ACT.Copy).then_inc(s("b_kct_read"), 1)
        act.wait_ge(s("b_s8"), 1)
        nc.scalar.activation(s_t[:], ps[:, 2, 0:P], ACT.Copy).then_inc(s("b_s8_read"), 1)
        act.wait_ge(s("b_max8"), 1)
        nc.scalar.activation(s_s[:], s_s[:], ACT.Exp, bias=mxn[:, 0, 0, 1:2], accum_out=mxn[:, 0, 0, 2:3]).then_inc(s("b_exp8"), 1)
        act.wait_ge(s("b_p8t"), 1)
        nc.scalar.activation(p_t[:], ps[:, 2, 0:P], ACT.Copy).then_inc(s("b_p8t_read"), 1)
        act.wait_ge(s("b_o8_read"), 1)
        for kv in range(2):
            with act.Fori(0, 2) as it:
                first = it * 8 + 16 * kv

                def exps(n):
                    lo = 0 if n % 4 else P
                    act.wait_ge(s("b_max"), first + (n + 1))
                    for r in range(2):
                        e = nc.scalar.activation(sx[:, n % 4, r, lo:257], sx[:, n % 4, r, lo:257], ACT.Exp,
                                                 bias=mxn[:, n % 4, r, 1:2], accum_out=mxn[:, n % 4, r, 2:3])
                    e.then_inc(s("b_exp"), 1)

                def read_turn(n):
                    lo = 0 if n % 4 else P
                    act.wait_ge(s("b_turn"), first + (n + 5))
                    act.wait_ge(s("b_o"), first + (n + 1))
                    nc.scalar.activation(pt[:, n % 2, :].rearrange("p (r k) -> p r k", r=2)[:, :, lo:256],
                                         ps[:, 6, :].rearrange("p (r k) -> p r k", r=2)[:, :, lo:256], ACT.Copy)\
                        .then_inc(s("b_pt"), 1)

                for n in range(8 + 2):
                    if n < 8:
                        exps(n)
                    if n >= 2:
                        read_turn(n - 2)
        act.wait_ge(s("b_pt"), 33)
        act.wait_ge(out_done, out_count[0])
        act.wait_ge(s("b_ended"), 2)
        barrier(act, 3)

        act.dma_start(ws[:], io["a_spatial_w"].rearrange("l g t s -> t (l g) s")).then_inc(s("a_in"), 16)
        asb, asw = io["a_spatial_b"], io["a_spatial_w"]
        act.dma_start(bbc[:], bass.AP(tensor=asb.tensor, offset=asb.offset, ap=[[0, P], [P, 4], [1, P]])).then_inc(s("a_in"), 16)
        act.dma_start(w00[:], bass.AP(tensor=asw.tensor, offset=asw.offset, ap=[[0, P], [P * P, 4], [1, 1]])).then_inc(s("a_in"), 16)
        link(nc.scalar.activation(zT[:, Z_AV:Z_AV + 4, :], zT[:, Z_AV:Z_AV + 4, :], ACT.Gelu))
        nc.scalar.activation(zT[:, Z_AU:Z_AU + 4, :], zT[:, Z_AU:Z_AU + 4, :], ACT.Gelu).then_inc(s("a_gelu"), 1)
        norm_act(act, "a")
        act.wait_ge(s("a_v8"), 1)
        link(nc.scalar.activation(vn8[:], ps[0:S, 0, :], ACT.Copy))
        store(act, io["chunk_v"].rearrange("l b t w -> (l b t) w"), vn8[:])
        act.wait_ge(out_done, out_count[0])
        barrier(act, 4)

        for c in K_ORDER:
            nc.scalar.activation(act_hi[:, c, :], zT[:, MIX_TILES[c], :], ACT.Copy).then_inc(mix_hi, 1)

        def residual(n, u, tile):
            act.wait_ge(z_free, n + (Z_N + 3))
            nc.scalar.activation(ssq[:, u, :], xT[:, tile, :].rearrange("p a n -> p (a n)"), ACT.Square).then_inc(s("o_sq"), 1)
            nc.scalar.activation(h2_hi[:, tile, :].rearrange("p a n -> p (a n)"), xT[:, tile, :].rearrange("p a n -> p (a n)"),
                                 ACT.Copy, scale=gain2[:, u:u + 1]).then_inc(s("h2_hi"), 1)

        with act.Fori(U_OUT // 2, U_FFN // 2) as i:
            unit_hi(i * 8 + 4, 1, i * 16 + 16)
            residual(i * 2 - U_OUT, 0, bass.ds(i * 2 - U_OUT, 1))
            unit_hi(i * 8 + 8, 0, i * 16 + 32)
            residual(i * 2 + (1 - U_OUT), 1, bass.ds(i * 2 + (1 - U_OUT), 1))
        act.wait_ge(s("o_mean"), 1)
        nc.scalar.activation(rs2[:], rs2[:], ACT.Sqrt).then_inc(s("o_root"), 1)

        def start_g(n, j):
            act.wait_ge(s("f_zg"), n + 1)
            act.wait_ge(cpar_in, n_cpar)
            nc.scalar.activation(cg[:], zg[:, 2:], ACT.Identity, scale=cpar[:, 0, j, 18:19], bias=cpar[:, 0, j, 19:20])\
                .then_inc(s("f_tg"), 1)

        def start_a(n, j):
            act.wait_ge(s("f_za"), n + 1)
            nc.scalar.activation(ca[:], za[:, 2:], ACT.Identity, scale=cpar[:, 1, j, 18:19], bias=cpar[:, 1, j, 19:20])\
                .then_inc(s("f_ta"), 1)

        def silu(n, j):
            act.wait_ge(s("f_cg"), n + 1)
            nc.scalar.activation(cg[:], cg[:], ACT.Silu).then_inc(s("f_silu"), 1)

        def gated_hi(n, j):
            act.wait_ge(s("f_m"), n + 1)
            nc.scalar.activation(g_hi[:, j, :], gm[:], ACT.Copy).then_inc(s("g_hi"), 1)

        def ffn_group_act(q1, pair0, n0, grp, with_down):
            nonlocal n_cpar
            n_cpar = grp * 32 + 32
            units = GC * 3 if with_down else U_GRP
            due = {}
            for j in range(GC):
                g = 2 * j + (GC if with_down and j else 0)
                due.setdefault((g + 2, 1), []).append((start_g, j))
                late = g + 3 <= units
                due.setdefault((g + 3, 0) if late else (units, 3), []).append((start_a, j))
                due.setdefault((g + 3, 1) if late else (units, 3), []).append((silu, j))
                hi_at = ((GC + 2, 3) if with_down and j == 0 else (g + 3, 2)) if late else (units, 3)
                due.setdefault(hi_at, []).append((gated_hi, j))
            for u in range(1, units + 1):
                for k in range(4):
                    q_hi(q1 + (4 * (u - 1) + k), k, u % 2, pair0 + 16 * (u // 2))
                    for step, j in due.get((u, k), []):
                        if step is gated_hi and j == 0 and with_down:
                            act.wait_ge(w_used, q1 + (4 * (GC + 1) + 4))
                        step(n0 + j, j)

        n_cpar = 0
        ffn_group_act(4 * U_FFN + 4, 8 * U_FFN + 16, 0, 0, False)
        with act.Fori(1, NG) as i:
            ffn_group_act(i * 48 + 4 * (U_FFN + U_GRP - 12 + 1), i * 96 + 8 * (U_FFN + U_GRP - 12 + 2), i * GC, i, True)

        def read_tail(r):
            act.wait_ge(s("t_turn"), r + 1)
            nc.scalar.activation(trow[:, 512 * r:512 * r + 512], ps[0:S + 2, 2 + r % 2, :], ACT.Copy).then_inc(s("t_read"), 1)

        r = 0
        for u in range(U_ALL - GC, U_ALL):
            for k in range(4):
                if u > U_ALL - GC:
                    q_hi(4 * u + k, k, u % 2, 16 * (u // 2 + 1))
                    reads = 1
                else:
                    reads = 2
                for _ in range(reads):
                    if r < 6 or u > U_ALL - GC:
                        if r < FC // 2:
                            read_tail(r)
                            r += 1
        while r < FC // 2:
            read_tail(r)
            r += 1
        act.wait_ge(s("y8_turn"), 1)
        nc.scalar.activation(ytok8[:], ps[0:S, 4:8, :].rearrange("p a n -> p (a n)"), ACT.Copy).then_inc(s("y8_read"), 1)

    def read_y(dve, dt):
        dve.wait_ge(s("y_turn"), dt + 1)
        nc.vector.tensor_copy(ytok[:, :, dt * P:(dt + 1) * P], ps[:, dt % 2, :].rearrange("p (j n) -> p j n", j=NB))\
            .then_inc(s("y_read"), 1)

    @block.vector
    def _(dve):
        link = Chain(dve, chain_v)
        mult, add, sub, mx = ALU.mult, ALU.add, ALU.subtract, ALU.max
        tt, stt, ts = nc.vector.tensor_tensor, nc.vector.scalar_tensor_tensor, nc.vector.tensor_scalar

        dve.nop().then_inc(z_free, 2)
        link(nc.vector.memset(small[:], 1.0))
        dve.wait_ge(vec_tr, 1)
        nc.vector.tensor_copy(vecs[:, 0:42], ps[:, 7, 0:42]).then_inc(vec_ev, 1)
        for idx in range(1, 16, 2):
            i, c4 = idx // 4, idx % 4
            dve.wait_ge(x_tr, idx + 1)
            nc.vector.tensor_copy(xT[:, 4 * c4:4 * c4 + 4, i * P:(i + 1) * P],
                                  ps[:, idx % 6, :].rearrange("p (c n) -> p c n", c=4)).then_inc(x_ev_v, 1)
            if c4 == 3:
                link(nc.vector.tensor_tensor_reduce(out=xjunk[:], in0=xtok[:, i, :], in1=xtok[:, i, :], scale=1.0,
                                                    scalar=0.0, op0=mult, op1=add, accum_out=small[:, i:i + 1]))
        dve.wait_ge(x_tr, 17)
        nc.vector.tensor_copy(xT[:, :, T:N], ps[:, 6, 0:P].rearrange("p (c n) -> p c n", c=KC)).then_inc(x_ev_v, 1)
        link(nc.vector.tensor_tensor_reduce(out=xjunk[0:S, :], in0=xtok[0:S, 4, :], in1=xtok[0:S, 4, :], scale=1.0,
                                            scalar=0.0, op0=mult, op1=add, accum_out=small[0:S, 4:5]))
        dve.wait_ge(x_ev_v, 9)
        dve.wait_ge(x_ev_a, 8)
        dve.wait_ge(vec_ev, 1)
        nc.vector.tensor_scalar(small[:, 8:13], small[:, 0:5], 1.0 / D, EPS, mult, add).then_inc(var_v, 1)
        for i, c in enumerate(K_ORDER):
            dve.wait_ge(h_hi, i + 1)
            stt(out=act_lo[:, c, :], in0=xT[:, c, :], scalar=vecs[:, G1 + c:G1 + c + 1], in1=act_hi[:, c, :].bitcast(F32),
                op0=mult, op1=sub).then_inc(h_lo, 1)
        dve.wait_ge(var_a, 1)
        link(nc.vector.reciprocal(small[:, 24:29], small[:, 16:21]))
        dve.wait_ge(const_made, 1)
        for i in range(NB):
            ts(xjunk[:, i * P:(i + 1) * P], ident[:], small[:, 24 + i:25 + i], None, mult)
        ts(xjunk[0:S, 512:512 + S], ident[0:S, 0:S], small[0:S, 28:29], None, mult).then_inc(rs_diag, 1)
        dve.wait_ge(rs_mm, 1)
        nc.vector.tensor_copy(rs1[:, 0:T], ps[:, 7, :])
        nc.vector.tensor_copy(rs1[:, T:N], ps[:, 6, 256:256 + S]).then_inc(rs_ready, 1)
        dve.wait_ge(rs_ready, 1)
        with dve.Fori(0, Z_N // 2) as i:
            for u in range(2):
                dve.wait_ge(w_used, i * 8 + (4 * u + 8))
                tt(zT[:, bass.ds(i * 2 + u, 1), :].rearrange("p a (h n) -> p (a h) n", h=2), pair(2 * u), halves(rs1[:]),
                   mult).then_inc(z_free, 1)
        for r in range(1, 4, 2):
            dve.wait_ge(s("p_tr"), r + 1)
            nc.vector.tensor_copy(st_cols[:, 22 * r:22 * r + 22, :], ps[:, r, 0:440].rearrange("p (c n) -> p c n", n=20))\
                .then_inc(s("p_cols"), 1)
        dve.wait_ge(s("p_cols"), 2)
        dve.wait_ge(s("rel_in"), 32)
        nc.vector.memset(rel33[32:33, :], NEG).then_inc(s("rel_set"), 1)
        dve.wait_ge(s("rel_set"), 1)
        barrier(dve, 1)

        dve.wait_ge(misc_in, 48)
        r4, rf = slice(0, 4), slice(32, 36)
        tt(halves(gf[rf, 0, :]), ps[rf, 4:6, 0:NH], halves(rs1[rf, :]), mult)
        tt(halves(gi[:, 0, :]), ps[r4, 4:6, 0:NH], halves(rs1[r4, :]), mult).then_inc(s("c_gates_read"), 1)
        dve.wait_ge(s("c_gates_read"), 1)
        link(ts(gf[rf, 0, :], gf[rf, 0, :], gbf[rf, :], None, add))
        stt(out=gf[rf, 1, :], in0=gf[rf, 0, :], scalar=-1.0, in1=gf[rf, 0, :], op0=mult, op1=mx).then_inc(s("c_fabs"), 1)
        link(ts(gi[:, 0, :], gi[:, 0, :], gbi[:], None, add))
        link(ts(gf[rf, 3, :], gf[rf, 0, :], 0.0, None, ALU.min))
        dve.wait_ge(s("c_ln"), 1)
        link(tt(gf[rf, 3, :], gf[rf, 3, :], gf[rf, 2, :], sub))
        link(nc.vector.memset(gf[rf, 0, :], 1.0))
        link(nc.vector.tensor_tensor_scan(gf[rf, 1, 0:T], gf[rf, 0, 0:T], gf[rf, 3, 0:T], 0.0, mult, add))
        link(nc.vector.tensor_copy(gf[rf, 1, T:N], gf[rf, 3, T:N]))
        link(nc.vector.tensor_copy(gi[:, 1, :], gf[rf, 1, :]))
        link(tt(gi[:, 2, :], gi[:, 0, :], gi[:, 1, :], sub))
        link(nc.vector.tensor_tensor_scan(gi[:, 3, 0:T], gi[:, 2, 0:T], gi[:, 2, 0:T], 0.0, mx, mx))
        link(tt(gi[:, 3, T:N], gi[:, 2, T:N], m0[:], mx))
        link(tt(gi[:, 4, :], gi[:, 1, :], gi[:, 3, :], add))
        link(tt(gs[:, 0, :], gi[:, 2, T:N], gi[:, 3, T:N], sub))
        link(tt(gs[:, 1, :], m0[:], gi[:, 3, T:N], sub))
        ts(gi[:, 5, :], gi[:, 3, :], -1.0, None, mult).then_inc(s("c_lines"), 1)
        dve.wait_ge(s("c_exp"), 1)
        ts(gi[:, 7, 0:T], gi[:, 7, 0:T], 0.125, None, mult)
        ts(gs[:, 0, :], gs[:, 0, :], 0.125, None, mult).then_inc(s("c_rows"), 1)
        link(nc.vector.memset(vtok[:, :, :, P:P + 1], 1.0))
        dve.wait_ge(s("c_small"), 1)
        link(nc.vector.tensor_copy(ct[:].rearrange("p a b -> p (a b)"), ps[:, 7, 0:32]))
        link(nc.vector.tensor_copy(cs[:].rearrange("p a b -> p (a b)"), ps[:, 7, 64:96]))
        link(nc.vector.tensor_copy(emts[:], ps[:, 7, 128:160]))
        dve.wait_ge(s("c_st"), 64)
        link(tt(kws[:], zT[:, Z_CK:Z_CK + 2, T:N], cs[:, :, 0:S], mult))
        dve.drain().then_inc(s("c_kws"), 1)
        n_kb = ns[:].rearrange("p (b k) -> p k b", k=2)
        link(tt(n_kb, n_kb, cs[:, :, S:2 * S], mult))
        link(tt(n_kb, n_kb, kws[:], add))
        tt(nq[:], zT[:, Z_CQ:Z_CQ + 2, T:N], n_kb, mult).then_inc(s("c_nq"), 1)
        for t2 in range(2):
            dve.wait_ge(s("c_kt"), t2 + 1)
            for q in range(2):
                h = 2 * t2 + q
                k = tt(kw[:, :, h, :], ps[:, 4 + t2, :].rearrange("p (j d) -> p j d", j=NB)[:, :, 64 * q:64 * q + 64],
                       ct[:, 4:8, h:h + 1].broadcast_to([P, NB, 64]), mult)
            k.then_inc(s("c_kw"), 1)
        dve.wait_ge(s("c_k8"), 1)
        nc.vector.tensor_copy(k8[:], ps[0:S, 6, 0:256]).then_inc(s("c_k8_read"), 1)
        dve.wait_ge(s("c_mem"), 1)
        nc.vector.tensor_copy(cout[:].rearrange("p a b -> p (a b)"), ps[:, 7, 0:258]).then_inc(s("c_mem_read"), 1)
        dve.wait_ge(s("c_scaled"), 2)
        for hp in range(2):
            dve.wait_ge(s("c_outer"), hp + 1)
            for half in range(2):
                c_v = cst[:].rearrange("p (b k) e -> p k b e", k=2)[:, hp, 4 * half:4 * half + 4, :]
                o = tt(c_v, c_v, ps[:, 4 + half, :].rearrange("p (b e) -> p b e", b=4), add)
            o.then_inc(s("c_outer_read"), 1)
        dve.wait_ge(s("c_abs8"), 1)
        link(tt(hs[:, 1, :], hs[:, 0, :], emts[:], mx))
        link(nc.vector.reciprocal(hs[:, 2, :], hs[:, 1, :]))
        for q in range(2):
            o = tt(zT[:, Z_CV:Z_CV + 4, T:N].rearrange("p (k q) b -> p q k b", q=2)[:, q], heads_of(ps[:, 6 - q, 0:32], q),
                   heads_of(hs[:, 2, :], q), mult)
        o.then_inc(s("c_num8_read"), 1)
        for h in range(4):
            dve.wait_ge(s("c_bc"), h + 1)
            tt(tmpm[:].rearrange("p (j n) -> p j n", j=NB), ps[:, 4, :].rearrange("p (j n) -> p j n", j=NB),
               causal[:].rearrange("p (j n) -> p j n", j=1).broadcast_to([P, NB, P]), add).then_inc(s("c_masked"), 1)
            dve.wait_ge(s("c_decay"), h + 1)
            for j in range(NB):
                dve.wait_ge(s("c_s"), 4 * h + j + 1)
                n = T - j * P
                stt(out=pmat[:, DIAG[j]:DIAG[j] + n], in0=ps[:, 5 - j % 2, 0:n], scalar=0.125,
                    in1=dmat[:, DIAG[j]:DIAG[j] + n], op0=mult, op1=mult).then_inc(s("c_p"), 1)
            dve.wait_ge(s("c_abs"), h + 1)
            link(tt(den[:], qab[:], ps[:, 4, :], mx))
            link(nc.vector.reciprocal(den[:], den[:]))
            tt(zT[:, Z_CV + h, 0:T], ps[:, 6, :], den[:], mult).then_inc(s("c_head"), 1)
            dve.wait_ge(s("c_head"), h + 1)
        norm_dve(dve, "c", link)
        dve.wait_ge(s("norm_out"), 4)
        dve.wait_ge(s("c_sig"), 1)
        for h in range(4):
            o = tt(zT[:, Z_CO + h, :], zT[:, Z_CV + h, :], zT[:, Z_CO + h, :], mult)
        link(o)
        barrier(dve, 2)

        for name, credit in (("b_o", 2), ("b_pt", 1), ("b_turn", 4), ("b_sc_free", 2), ("b_o_free", 2)):
            dve.nop().then_inc(s(name), credit)
        norm_dve(dve, "b", link)
        dve.wait_ge(s("norm_out"), 13)
        for kv in range(2):
            for q in range(2):
                nc.vector.tensor_copy(kd[64 * q:64 * q + 64, kv, :], zT[64 * kv:64 * kv + 64, Z_BK, :])
        link(nc.vector.memset(qb_[:], 0.0))
        for kv in range(2):
            for q in range(2):
                o = nc.vector.tensor_copy(
                    qb_[64 * kv:64 * kv + 64, :, :].rearrange("p b (u q) -> p q u b", q=2)[:, q, 4 * kv:4 * kv + 4, :],
                    zT[64 * q:64 * q + 64, Z_BQ + 4 * kv:Z_BQ + 4 * kv + 4, T:N])
        o.then_inc(s("b_q8"), 1)
        dve.wait_ge(s("b_vk_a"), 1)
        dve.wait_ge(s("b_q8"), 1)
        dve.drain().then_inc(s("b_vk"), 1)
        dve.wait_ge(s("b_in"), 64)
        dve.wait_ge(s("b_s8t"), 1)
        link(nc.vector.tensor_copy(s_s[:, P:P + 1], bsink[:]))
        link(nc.vector.tensor_tensor_reduce(out=s_s[:, 0:P], in0=ps[:, 3, 0:P], in1=bias_s[:], scale=0.125,
                                            scalar=s_s[:, P:P + 1], op0=add, op1=mx, accum_out=mxn[:, 0, 0, 0:1]))
        ts(mxn[:, 0, 0, 1:2], mxn[:, 0, 0, 0:1], -1.0, None, mult).then_inc(s("b_max8"), 1)
        dve.wait_ge(s("b_exp8"), 1)
        link(nc.vector.reciprocal(mxn[:, 0, 0, 3:4], mxn[:, 0, 0, 2:3]))
        ts(s_s[:, 0:P], s_s[:, 0:P], mxn[:, 0, 0, 3:4], None, mult).then_inc(s("b_p8"), 1)
        dve.wait_ge(s("b_o8"), 1)
        for kv in range(2):
            for q in range(2):
                o = nc.vector.tensor_copy(
                    zT[64 * q:64 * q + 64, Z_BQ + 4 * kv:Z_BQ + 4 * kv + 4, T:N],
                    ps[64 * kv:64 * kv + 64, 3, 0:P].rearrange("p (b u q) -> p q u b", q=2, u=8)[:, q, 4 * kv:4 * kv + 4, :])
        o.then_inc(s("b_o8_read"), 1)
        dve.wait_ge(s("b_o8_read"), 1)
        STEPS = 8 * 2
        for kv in range(2):
            with dve.Fori(0, 2) as it:
                first = it * 8 + 16 * kv
                mine = it * STEPS + 2 * STEPS * kv
                told = [0]

                def then(ins):
                    told[0] += 1
                    ins.then_inc(s("b_steps"), 1)
                    dve.wait_ge(s("b_steps"), mine + told[0])

                def score(n):
                    sl, lo = n // 4, 0 if n % 4 else P
                    u = it * 2 + (4 * kv + sl)
                    if n % 4 == 0:
                        nc.vector.tensor_copy(qst[:, sl, 0:T], zT[:, bass.ds(u + Z_BQ, 1), 0:T].rearrange("p a n -> p (a n)"))\
                            .then_inc(s("b_pair"), 1)
                        dve.wait_ge(bias_in[sl], it * 16 + (32 * kv + 16))
                    dve.wait_ge(s("b_turn"), first + (n + 1))
                    begun(dve)
                    then(nc.vector.tensor_copy(sx[:, n % 4, :, 256], sinkbc[:, bass.ds(u * 2, 2)]))
                    dve.wait_ge(s("b_qk"), first + (n + 1))
                    begun(dve)
                    for r in range(2):
                        ins = nc.vector.tensor_tensor_reduce(
                            out=sx[:, n % 4, r, lo:256], in0=ps[:, 4 - 2 * r + n % 2, lo:256],
                            in1=bst[:, sl, r, lo:256], scale=0.125, scalar=sx[:, n % 4, r, 256:257], op0=add, op1=mx,
                            accum_out=mxn[:, n % 4, r, 0:1])
                    ins.then_inc(s("b_sc_free"), 1)
                    dve.wait_ge(s("b_sc_free"), first + (n + 3))
                    ts(mxn[:, n % 4, :, 1], mxn[:, n % 4, :, 0], -1.0, None, mult).then_inc(s("b_max"), 1)

                def scale(n):
                    lo = 0 if n % 4 else P
                    dve.wait_ge(s("b_exp"), first + (n + 1))
                    then(nc.vector.reciprocal(mxn[:, n % 4, :, 3], mxn[:, n % 4, :, 2]))
                    for r in range(2):
                        ins = ts(sx[:, n % 4, r, lo:256], sx[:, n % 4, r, lo:256], mxn[:, n % 4, r, 3:4], None, mult)
                    ins.then_inc(s("b_prob"), 1)

                def read_o(n):
                    u = it * 2 + (4 * kv + n // 4)
                    dve.wait_ge(s("b_o"), first + (n + 3))
                    begun(dve)
                    nc.vector.tensor_copy(zT[:, bass.ds(u + Z_BQ, 1), (n % 4) * P:(n % 4 + 1) * P].rearrange("p a n -> p (a n)"),
                                          ps[:, 7 * (n % 2), 0:P]).then_inc(s("b_o_free"), 1)

                for n in range(8 + 4):
                    if n < 8:
                        score(n)
                    if 1 <= n < 9:
                        scale(n - 1)
                    if n >= 4:
                        read_o(n - 4)
                assert told[0] == STEPS
        dve.wait_ge(s("b_o_free"), 34)
        dve.drain().then_inc(s("b_ended"), 2)
        barrier(dve, 3)

        dve.wait_ge(s("a_wt"), 1)
        nc.vector.tensor_copy(wst[:].rearrange("p g n -> p (g n)"), ps[:, 0, :]).then_inc(s("a_wt_read"), 1)
        dve.wait_ge(s("a_gelu"), 1)
        norm_dve(dve, "a", link)
        for g in range(4):
            dve.wait_ge(s("a_vt"), g + 1)
            nc.vector.tensor_copy(vnt[:, :, g, :], ps[:, (1, 2, 3, 1)[g], :].rearrange("p (j n) -> p j n", j=NB))\
                .then_inc(s("a_vt_read"), 1)
        dve.wait_ge(s("norm_out"), 17)
        dve.wait_ge(s("a_in"), 48)
        dve.wait_ge(s("a_v8"), 1)
        for g in range(4):
            link(ts(asmp[:, g, :], zT[:, Z_AV + g, T:N], w00[:, g:g + 1], bbc[:, g, 0:1], mult, add))
        link(tt(zT[:, Z_AU:Z_AU + 4, T:N], zT[:, Z_AU:Z_AU + 4, T:N], asmp[:], mult))
        for g in range(4):
            dve.wait_ge(s("a_mix"), g + 1)
            link(tt(amix[:].rearrange("p (j n) -> p j n", j=NB), ps[:, 4 + g, :].rearrange("p (j n) -> p j n", j=NB),
                    bbc[:, g:g + 1, :].broadcast_to([P, NB, P]), add))
            link(tt(zT[:, Z_AU + g, 0:T], zT[:, Z_AU + g, 0:T], amix[:], mult))
        barrier(dve, 4)

        for i, c in enumerate(K_ORDER):
            dve.wait_ge(mix_hi, i + 1)
            tt(act_lo[:, c, :], zT[:, MIX_TILES[c], :], act_hi[:, c, :].bitcast(F32), sub).then_inc(mix_lo, 1)

        dve.wait_ge(spilled, 32)
        dve.wait_ge(mix_lo, KC)
        link(nc.vector.memset(ssum[:], 0.0))

        def one(ap):
            return ap.rearrange("p a n -> p (a n)")

        def residual(i, u):
            n = i * 2 + (u - U_OUT)
            tile = bass.ds(n, 1)
            begun(dve)
            nc.vector.tensor_copy(gain2[:, u:u + 1], vecs[:, bass.ds(n + G2, 1)])
            dve.wait_ge(w_used, i * 8 + (4 * u + 8))
            x2 = xT[:, tile, :].rearrange("p a (h n) -> p (a h) n", h=2)
            tt(x2, pair(2 * u), x2, add).then_inc(z_free, 1)
            dve.wait_ge(z_free, n + (Z_N + 3))
            dve.wait_ge(s("o_sq"), n + 1)
            tt(ssum[:], ssum[:], ssq[:, u, :], add).then_inc(s("o_sum"), 1)
            dve.wait_ge(s("h2_hi"), n + 1)
            stt(out=one(h2_lo[:, tile, :]), in0=one(xT[:, tile, :]), scalar=gain2[:, u:u + 1],
                in1=one(h2_hi[:, tile, :]).bitcast(F32), op0=mult, op1=sub).then_inc(s("h2_lo"), 1)
            dve.wait_ge(s("h2_lo"), n + 1)

        with dve.Fori(U_OUT // 2, U_FFN // 2) as i:
            for u in range(2):
                residual(i, u)
        dve.wait_ge(w_used, USED_OUT)
        link(nc.vector.memset(zg[:, 0:2], 0.0))
        link(nc.vector.memset(za[:, 0:2], 0.0))
        dve.wait_ge(s("o_sum_mm"), 1)
        ts(halves(rs2[:]), pair(4), 1.0 / D, EPS, mult, add).then_inc(s("o_mean"), 1)
        dve.nop().then_inc(s("d_add"), 2)
        dve.wait_ge(s("o_root"), 1)
        link(nc.vector.reciprocal(rs2[:], rs2[:]))

        def ffn_group_dve(u0, n0, d0, base, tail, with_down):
            told = [0]

            def then(ins):
                told[0] += 1
                ins.then_inc(s("f_steps"), 1)
                dve.wait_ge(s("f_steps"), base + told[0])

            def read(n, half, unit, j):
                z, name, bank = ((zg, "f_zg", 0), (za, "f_za", 2))[half]
                dve.wait_ge(w_used, u0 * 4 + (4 * unit + 8))
                tt(halves(z[:, 2:]), pair(bank), halves(rs2[:]), mult).then_inc(s(name), 1)
                dve.wait_ge(s(name), n + 1)
                begun(dve)
                nc.vector.tensor_copy(ztail[:, bass.ds(tail(half, j), 1), :].rearrange("p a n -> p (a n)"), z[:, T:])\
                    .then_inc(z_free, 1)

            def conv(n, half, j):
                z, c_, name = ((zg, cg, "f_tg"), (za, ca, "f_ta"))[half]
                par = cpar[:, half, j, :]
                dve.wait_ge(s(name), n + 1)
                old = par[:, 0:16].rearrange("p (b t) -> p t b", t=2)
                for tap, from_col in ((1, 1), (0, 0)):
                    stt(out=c_[:, T:N], in0=old[:, tap, :], scalar=par[:, 16 + tap:17 + tap], in1=c_[:, T:N],
                        op0=mult, op1=add)
                    ins = stt(out=c_[:, 0:T], in0=z[:, from_col:from_col + T], scalar=par[:, 16 + tap:17 + tap],
                              in1=c_[:, 0:T], op0=mult, op1=add)
                    if tap:
                        then(ins)
                if half:
                    then(ins)
                else:
                    ins.then_inc(s("f_cg"), 1)

            def gate(n, j):
                dve.wait_ge(s("f_silu"), n + 1)
                if isinstance(n, int) and n == 0:
                    pass
                tt(gm[:], cg[:], ca[:], mult).then_inc(s("f_m"), 1)
                dve.wait_ge(s("f_m"), n + 1)

            def lo(n, j):
                dve.wait_ge(s("g_hi"), n + 1)
                tt(g_lo[:, j, :], gm[:], g_hi[:, j, :].bitcast(F32), sub).then_inc(s("g_lo"), 1)

            def down(m, k):
                e = 4 * m + k
                dve.wait_ge(w_used, u0 * 4 + (4 * (2 + m) + k + 5))
                x2 = halves(xT[:, e, :])
                tt(x2, pair(4 + 2 * (k % 2)), x2, add).then_inc(s("d_add"), 1)

            for j in range(GC):
                g = 2 * j + (GC if with_down and j else 0)
                n = n0 + j
                read(n, 0, g, j)
                read(n, 1, g + 1, j)
                conv(n, 0, j)
                if with_down and j == 0:
                    down(0, 0)
                conv(n, 1, j)
                if with_down and j == 0:
                    down(0, 1)
                gate(n, j)
                if with_down and j == 0:
                    for e in range(2, 16):
                        down(e // 4, e % 4)
                lo(n, j)
            return told[0]

        steps = ffn_group_dve(U_FFN, 0, None, 0, lambda half, j: FC * half + j, False)
        with dve.Fori(1, NG) as i:
            assert ffn_group_dve(i * 12 + (U_FFN + U_GRP - 12), i * GC, i * 16 - 16, i * steps,
                                 lambda half, j: i * GC + (FC * half + j), True) == steps
        for e in range(16):
            dve.wait_ge(w_used, 4 * (U_ALL - GC) + e + 5)
            x2 = halves(xT[:, e, :])
            tt(x2, pair(4 + 2 * (e % 2)), x2, add).then_inc(s("d_add"), 1)
            if e:
                read_y(dve, e - 1)
        read_y(dve, 15)

    @block.gpsimd
    def _(pool):
        link = Chain(pool, chain_p)
        link(nc.gpsimd.memset(ident[:], 0.0))
        link(nc.gpsimd.affine_select(out=ident[:], in_=ident[:], compare_op=ALU.not_equal, fill=1.0, base=0,
                                     pattern=[[-1, P]], channel_multiplier=1))
        nc.gpsimd.memset(ones[:], 1.0).then_inc(const_made, 1)
        pool.wait_ge(const_made, 1)
        nc.gpsimd.memset(whi[:].rearrange("p q c n -> p (q c n)").bitcast(F32), 0.0).then_inc(ring_zero, 1)
        nc.gpsimd.memset(wlo[:].rearrange("p q c n -> p (q c n)").bitcast(F32), 0.0).then_inc(ring_zero, 1)
        link(nc.gpsimd.memset(pairones[:], 0.0))
        for q in range(2):
            link(nc.gpsimd.memset(pairones[64 * q:64 * q + 64, 64 * q:64 * q + 64], 1.0))
        link(nc.gpsimd.memset(causal[:], 0.0))
        link(nc.gpsimd.affine_select(out=causal[:], in_=causal[:], compare_op=ALU.is_ge, fill=NEG, base=0,
                                     pattern=[[1, P]], channel_multiplier=-1))
        for h in range(4):
            link(nc.gpsimd.tensor_copy(sel[:, h, :], ident[0:4, h:h + 1].broadcast_to([4, P])))
        pool.wait_ge(wg_hi, 1)
        pool.wait_ge(ring_zero, 2)
        gates = wg_raw[:].rearrange("p (c k) n -> p k c n", k=4)
        for rows in (0, 32):
            from_col = rows // 8
            g = nc.gpsimd.tensor_tensor(wlo[:, :, :, rows:rows + 4], gates[:, :, :, from_col:from_col + 4],
                                        whi[:, :, :, rows:rows + 4].bitcast(F32), ALU.subtract)
        g.then_inc(wg_lo, 1)

        def split_pairs(first, last):
            with pool.Fori(first, last) as i:
                for u in range(2):
                    for k in range(4):
                        pool.wait_ge(w_hi, i * 8 + (4 * u + k + 1))
                        nc.gpsimd.tensor_tensor(wlo[:, k, :, :], rawq(k, u), whi[:, k, :, :].bitcast(F32),
                                                ALU.subtract).then_inc(w_lo, 1)

        split_pairs(0, Z_N // 2)
        pool.wait_ge(s("rel_in"), 32)
        barrier(pool, 1)

        pool.wait_ge(s("c_v8_read"), 1)
        for h in range(4):
            nc.gpsimd.tensor_tensor(vm[:, h, :].rearrange("p (b e) -> p b e", b=S),
                                    v8[:, h * P:(h + 1) * P].rearrange("p (a e) -> p a e", a=1).broadcast_to([S, S, P]),
                                    ident[0:S, 0:S].rearrange("p (b a) -> p b a", a=1).broadcast_to([S, S, P]),
                                    ALU.mult).then_inc(s("c_vm"), 1)
        pool.wait_ge(s("c_st"), 64)
        pool.wait_ge(s("c_kws"), 1)
        for hp in range(2):
            c_v = cst[:].rearrange("p (b k) e -> p k b e", k=2)[:, hp, :, :]
            nc.gpsimd.tensor_tensor(c_v, c_v, cs[:, hp, S:2 * S].rearrange("p (b a) -> p b a", a=1).broadcast_to([P, S, P]),
                                    ALU.mult).then_inc(s("c_scaled"), 1)
        pool.wait_ge(s("c_scaled"), 2)
        barrier(pool, 2)
        barrier(pool, 3)
        pool.wait_ge(s("a_wt_read"), 1)
        nc.gpsimd.affine_select(out=wst[:], in_=wst[:], compare_op=ALU.is_ge, fill=0.0, base=0,
                                pattern=[[0, 4], [1, P]], channel_multiplier=-1).then_inc(s("a_wst"), 1)
        pool.wait_ge(s("a_wst"), 1)
        barrier(pool, 4)
        split_pairs(Z_N // 2, U_ALL // 2)

    @block.sync
    def _(sp):
        for i in range(NB):
            sp.dma_start(xtok[:, i, :], io["x_prompt"][0, i * P:(i + 1) * P, :]).then_inc(x_in[i], 16)
        sp.dma_start(xtok[0:S, 4, :], io["x_sample"].rearrange("b t d -> (b t) d")).then_inc(x_in[4], 16)

        def load_pair(sources, split, down=False):
            for u in range(2):
                if split is not None:
                    sp.wait_ge(w_lo, split + 4 * u)
                sp.dma_start(unit_dst(u, down), sources[u]).then_inc(raw_in[u], 16)

        load_pair([cols_of(w_in, COL_C), cols_of(w_in, COL_C + P)], None)
        for a, b, col, unit in ((1, 6, COL_C, Z_CQ), (6, 11, COL_B, Z_BQ), (11, 15, COL_A, Z_AU)):
            with sp.Fori(a, b) as i:
                load_pair([cols_of(w_in, i * (2 * P) + (col + (u - unit) * P)) for u in range(2)], i * 8 - 4)
        sp.wait_ge(x_ev_a, 8)
        sp.wait_ge(x_ev_v, 9)
        sp.dma_start(spill, xT[:].rearrange("p c n -> p (c n)")).then_inc(spilled, 16)
        load_pair([cols_of(w_out, 0), cols_of(w_out, P)], 4 * Z_N - 4)
        sp.wait_ge(stage, 8)
        for u in range(8):
            if u >= 2:
                sp.wait_ge(s("b_sc_free"), 4 * u - 2)
            sp.dma_start(bst[:, u % 2, :, :], bass.AP(tensor=bias_rows.tensor, offset=P - 1 + 2 * u * BIAS_PITCH,
                                                       ap=[[383, P], [BIAS_PITCH, 2], [1, 256]])).then_inc(bias_in[u % 2], 16)
        sp.wait_ge(stage, 12)
        sp.dma_start(xT[:].rearrange("p c n -> p (c n)"), spill).then_inc(spilled, 16)
        with sp.Fori(U_OUT // 2 + 1, U_FFN // 2) as i:
            load_pair([cols_of(w_out, i * (2 * P) + (u - U_OUT) * P) for u in range(2)], i * 8 - 4)

        def load_group(col, split, with_down, n_before):
            def up(j):
                return [cols_of(w_up, col + j * P), cols_of(w_up, col + (FF + j * P))]

            def conv_params():
                if n_before is not None:
                    sp.wait_ge(s("f_m"), n_before)
                for half, row in ((0, col_chunk), (1, col_chunk + FC)):
                    sp.dma_start(cpar[:, half, :, :], conv_rows[:, bass.ds(row, GC), :]).then_inc(cpar_in, 16)

            load_pair(up(0), split)
            if with_down:
                load_pair([down_of(col - GC * P, m) for m in (0, 1)], split + 8, True)
                conv_params()
                load_pair([down_of(col - GC * P, m) for m in (2, 3)], split + 16, True)
            else:
                sp.wait_ge(w_used, USED_OUT)
                conv_params()
            for j in range(1, GC):
                load_pair(up(j), split + 8 * (j + (2 if with_down else 0)))

        col_chunk = 0
        load_group(0, 4 * U_FFN - 4, False, None)
        with sp.Fori(1, NG) as i:
            col_chunk = i * GC
            load_group(i * (GC * P), i * 48 + 4 * (U_FFN + U_GRP - 12) - 4, True, i * GC)
        for m in (0, 2):
            load_pair([down_of((NG - 1) * GC * P, mm) for mm in (m, m + 1)],
                      4 * (U_ALL - GC + m) - 4, True)
        sp.wait_ge(s("t_read"), FC // 2)
        store(sp, io["ffn_conv_prompt"][0, 0], trow[0:2, :])
        store(sp, io["ffn_conv_sample"][0, :, 1, :], trow[2:2 + S, :])
        for half in range(2):
            sp.wait_ge(s("y_read"), 8 * half + 8)
            store(sp, io["y_prompt"][0, :, half * 1024:(half + 1) * 1024].rearrange("(j p) d -> p j d", p=P),
                  ytok[:, :, half * 1024:(half + 1) * 1024])
        sp.wait_ge(s("y8_read"), 1)
        store(sp, io["y_sample"].rearrange("b t d -> (b t) d"), ytok8[:])
        sp.wait_ge(out_done, out_count[0])

    ctx.close()


_INS = ["x_prompt", "x_sample", "cache_swa_k", "cache_swa_v", "state_mlstm_C", "state_mlstm_n", "state_mlstm_m",
        "state_ffn_conv", "rel_bias", "norm1", "w_in", "a_v_gain", "a_spatial_w", "a_spatial_b", "b_q_gain",
        "b_k_gain", "b_sinks", "c_gate_bias", "c_h_gain", "w_out", "norm2", "w_up", "ffn_conv_w", "ffn_conv_b",
        "w_down"]
_OUTS = [("y_prompt", (1, T, D)), ("y_sample", (S, 1, D)),
         ("k_prompt", (1, 1, WINDOW, 2, 64)), ("v_prompt", (1, 1, WINDOW, 2, 64)),
         ("k_sample", (1, S, 1, 2, 64)), ("v_sample", (1, S, 1, 2, 64)),
         ("C_prompt", (1, 1, 4, 64, 128)), ("n_prompt", (1, 1, 4, 64)), ("m_prompt", (1, 1, 4)),
         ("C_sample", (1, S, 4, 64, 128)), ("n_sample", (1, S, 4, 64)), ("m_sample", (1, S, 4)),
         ("ffn_conv_prompt", (1, 1, 2, F2)), ("ffn_conv_sample", (1, S, 2, F2)), ("chunk_v", (1, S, 1, 512))]


def kernel(**inputs):
    import concourse.bacc as bacc
    from concourse.bass_utils import run_bass_kernel_spmd

    nc = bacc.Bacc("TRN2", target_bir_lowering=False, num_devices=1)
    arrays = {f"in_{n}": np.ascontiguousarray(inputs[n]) for n in _INS}
    arrays["in_bucket_table"] = bucket_table()
    io = {n[3:]: nc.dram_tensor(n, a.shape, F32, kind="ExternalInput").ap() for n, a in arrays.items()}
    for n in ("w_in", "w_out", "w_up", "w_down"):
        io[n] = io[n][0]
    for n, shape in _OUTS:
        io[n] = nc.dram_tensor(f"out_{n}", shape, F32, kind="ExternalOutput").ap()
    hybrid_layer(nc, io)
    r = run_bass_kernel_spmd(nc, [arrays], core_ids=[0])
    return tuple(r.results[0][f"out_{n}"] for n, _ in _OUTS)
```

```python
from contextlib import ExitStack

import numpy as np

import concourse.bass as bass
from concourse import mybir

F32 = mybir.dt.float32
F32R = mybir.dt.float32r
ACT = mybir.ActivationFunctionType
ALU = mybir.AluOpType
AX_X = mybir.AxisListType.X

P = 128
D = 2048
KC = D // P
T = 512
S = 8
N = T + S
NH = N // 2
NB = T // P
EPS = 1e-6
NEG = -1e30
IN_W = 3848
FF = 5632
F2 = 2 * FF
FC = FF // P
GC = 4
NG = FC // GC
WINDOW = 128
NBUCKET = 32

Z_CQ, Z_CK, Z_CV, Z_CO, Z_AU, Z_AV, Z_BK, Z_BV, Z_BQ, Z_N = 0, 2, 4, 8, 12, 16, 20, 21, 22, 30
COL_C, COL_A, COL_BQ, COL_BK, COL_G = 2304, 0, 1024, 2048, 3840
SLICE0 = 11
K_ORDER = [4 * c + k for k in range(4) for c in range(4)]
MIX_TILES = [Z_AU + i for i in range(4)] + [Z_BQ + i for i in range(8)] + [Z_CO + i for i in range(4)]

U_OUT = Z_N
U_FFN = U_OUT + KC
U_GRP = 2 * GC
U_ALL = U_FFN + NG * (U_GRP + GC)


def bucket_of(dist):
    n = max(dist, 0)
    if n < NBUCKET // 2:
        return n
    large = NBUCKET // 2 + int(np.float32(np.log(np.float32(n) / np.float32(16))) / np.log(8.0) * 16)
    return min(large, NBUCKET - 1)


def bucket_table():
    e = np.zeros((NBUCKET + 1, 384), np.float32)
    for w in range(384):
        dist = 255 - w
        e[bucket_of(dist) if 0 <= dist < WINDOW else NBUCKET, w] = 1.0
    return e


def hybrid_layer(nc, io):
    ctx = ExitStack()
    base = (nc.sbuf_base + 31) // 32 * 32
    limit = nc.sbuf_usable_end // 32 * 32

    class Region:

        def __init__(self, start, size):
            self.start, self.end, self.at = start, start + size, start

        def again(self):
            return Region(self.start, self.end - self.start)

        def take(self, name, shape, dt=F32):
            size = int(np.prod(shape[1:])) * 4
            size = (size + 31) // 32 * 32
            assert self.at + size <= self.end, (name, self.at + size - self.end)
            t = nc.alloc_sbuf_tensor_at(name, shape, dt, offset=self.at)
            self.at += size
            return t

    ACTB = 2 * KC * N * 4
    XB = KC * N * 4
    keep = Region(base, limit - base - 2 * ACTB - XB)
    r_act = Region(keep.end, ACTB)
    r_z = Region(r_act.end, ACTB)
    r_x = Region(r_z.end, XB)

    ident = keep.take("ident", [P, P])
    ones = keep.take("ones", [P, P])
    pairones = keep.take("pairones", [P, P])
    causal = keep.take("causal", [P, P])
    vrow = keep.take("vrow", [48, P])
    vecs = keep.take("vecs", [P, 48])
    G1, G2, GAV, GCH, GBQ, GBK = 0, 16, 32, 36, 40, 41
    sel = keep.take("sel", [4, 4, P])
    rs1 = keep.take("rs1", [P, N])
    rs2 = keep.take("rs2", [P, N])
    small = keep.take("small", [P, 64])
    gbi = keep.take("gbi", [4, 1])
    gbf = keep.take("gbf", [36, 1])
    gain2 = keep.take("gain2", [P, 2])
    raw = keep.take("raw", [P, 2, KC * P])
    whi = keep.take("whi", [P, 4, 4, P], F32R)
    wlo = keep.take("wlo", [P, 4, 4, P], F32R)

    act_hi = r_act.take("act_hi", [P, KC, N], F32R)
    act_lo = r_act.take("act_lo", [P, KC, N], F32R)

    z0 = r_z.again()
    xtok = z0.take("xtok", [P, 5, D])
    xjunk = z0.take("xjunk", [P, D])
    wg_raw = z0.take("wg_raw", [P, KC, S])
    rel33 = z0.take("rel33", [33, 16])
    hot = z0.take("hot", [33, 384])
    brow = z0.take("brow", [16, 384])
    z1 = r_z.again()
    zT = z1.take("zT", [P, Z_N, N])
    z2 = r_z.again()
    h2_hi = z2.take("h2_hi", [P, KC, N], F32R)
    h2_lo = z2.take("h2_lo", [P, KC, N], F32R)
    xT = r_x.take("xT", [P, KC, N])

    ctx.enter_context(nc.allow_non_contiguous_dma(reason="small states, a few hundred elements"))
    ps = ctx.enter_context(nc.psum_tensor("ps", [P, 8, 512], F32))

    spill = nc.dram_tensor("x_spill", [P, KC * N], F32, kind="Internal").ap()
    BIAS_PITCH = (P + 1) * 384
    bias_rows = nc.dram_tensor("bias_rows", [16, P + 1, 384], F32, kind="Internal").ap()

    def sem(name):
        return ctx.enter_context(nc.semaphore(name))

    out_done = sem("out_done")
    stores = [0]

    def stored():
        stores[0] += 16
        return 16

    raw_in = [sem("raw_in0"), sem("raw_in1")]
    w_hi = sem("w_hi")
    w_lo = sem("w_lo")
    w_used = sem("w_used")
    z_free = sem("z_free")
    stage = sem("stage")
    chain_v, chain_a, chain_p = sem("chain_v"), sem("chain_a"), sem("chain_p")

    x_in = [sem(f"x_in{i}") for i in range(5)]
    vec_in, misc_in, wg_in = sem("vec_in"), sem("misc_in"), sem("wg_in")
    const_made = sem("const_made")
    ring_zero = sem("ring_zero")
    x_tr, x_ev_a, x_ev_v = sem("x_tr"), sem("x_ev_a"), sem("x_ev_v")
    vec_tr, vec_ev, rs_diag, rs_mm, rs_ready = (sem(n) for n in ("vec_tr", "vec_ev", "rs_diag", "rs_mm", "rs_ready"))
    var_v, var_a = sem("var_v"), sem("var_a")
    h_hi, h_lo = sem("h_hi"), sem("h_lo")
    wg_hi, wg_lo = sem("wg_hi"), sem("wg_lo")
    spilled = sem("spilled")

    def qslot(t, k):
        return t[:, k, :, :]

    def rawq(k, s):
        return raw[:, s, :].rearrange("p (c k n) -> p c k n", c=4, k=4)[:, :, k, :]

    def pair(b):
        return ps[:, b:b + 2, 0:NH]

    def halves(ap):
        return ap.rearrange("p (h n) -> p h n", h=2)

    w_in, w_out, w_up, w_down = io["w_in"], io["w_out"], io["w_up"], io["w_down"]

    def cols_of(w, col):
        return w[:, bass.ds(col, P)].rearrange("(c p) n -> p c n", p=P)

    def down_of(row, m):
        return w_down[bass.ds(row, GC * P), 512 * m:512 * m + 512].rearrange("(c p) n -> p c n", p=P)

    def unit_dst(u, down):
        if down:
            return raw[:, u, :].rearrange("p (c n) -> p c n", c=GC)
        return raw[:, u, :].rearrange("p (c n) -> p c n", c=KC)

    block = ctx.enter_context(nc.Block())

    r_ssq = Region(keep.at, 2 * N * 4)
    ssq = keep.take("ssq", [P, 2, N])
    v8 = r_ssq.take("v8", [8, 512])
    k8 = r_ssq.take("k8", [8, 256])
    ssum = rs1

    cX = r_x.again()
    gi = cX.take("gi", [4, 8, N])
    cH = Region(gi_start := r_x.start, 6 * N * 4)
    gf = nc.alloc_sbuf_tensor_at("gf", [36, 4, N], F32, offset=gi_start)
    dmat = cH.take("dmat", [P, 1280])
    pmat = cH.take("pmat", [P, 1280])
    tmpm = cH.take("tmpm", [P, T])
    vtok = cX.take("vtok", [P, NB, 4, P + 1])
    kw = cX.take("kw", [P, NB, 4, 64])
    qab = cX.take("qab", [P, T])
    den = cX.take("den", [P, T])
    cout = z1.take("cout", [P, 2, P + 1])
    ct = z1.take("ct", [P, 8, 4])
    cs = z1.take("cs", [P, 2, 16])
    emts = z1.take("emts", [P, 32])
    kws = z1.take("kws", [P, 2, S])
    ns = z1.take("ns", [P, 2 * S])
    nq = z1.take("nq", [P, 2, S])
    hs = z1.take("hs", [P, 3, 32])
    m0 = z1.take("m0", [4, S])
    gs = z1.take("gs", [4, 2, S])
    nX = r_x.again()
    nsq = nX.take("nsq", [P, 2, N])
    nvar = nX.take("nvar", [P, 2, N])
    cst = nX.take("cst", [P, 2 * S, P])
    bX = Region(nX.at, r_x.end - nX.at)
    vm = nX.take("vm", [8, 4, S * P])
    bA = r_act.again()
    kd = bA.take("kd", [P, 2, N])
    qst = bA.take("qst", [P, 2, N])
    vtb = bA.take("vtb", [P, NB, P])
    ktb = bA.take("ktb", [P, P])
    sx = bA.take("sx", [P, 4, 2, 257])
    pt = bA.take("pt", [P, 2, 512])
    bst = bA.take("bst", [P, 2, 2, 256])
    sinkbc = bA.take("sinkbc", [P, 16])
    mxn = bA.take("mxn", [P, 4, 2, 4])
    bsink = bA.take("bsink", [P, 1])
    kv8 = bA.take("kv8", [8, 2, P])
    kc_ = bX.take("kc_", [P, S, P])
    vc_ = bX.take("vc_", [P, S, P])
    kct = bX.take("kct", [P, S, P])
    qb_ = bX.take("qb_", [P, S, 16])
    s_t = bX.take("s_t", [P, P])
    s_s = bX.take("s_s", [P, 129])
    bias_s = bX.take("bias_s", [P, P])
    p_t = bX.take("p_t", [P, P])
    aA = Region(bA.at, r_act.end - bA.at)
    vnt = aA.take("vnt", [P, NB, 4, P])
    ws = aA.take("ws", [P, 4, P])
    wst = aA.take("wst", [P, 4, P])
    bbc = aA.take("bbc", [P, 4, P])
    w00 = aA.take("w00", [P, 4])
    vn8 = aA.take("vn8", [8, 512])
    amix = aA.take("amix", [P, T])
    asmp = aA.take("asmp", [P, 4, S])
    fA = r_act.again()
    g_hi = fA.take("g_hi", [P, GC, N], F32R)
    g_lo = fA.take("g_lo", [P, GC, N], F32R)
    zg = fA.take("zg", [P, N + 2])
    za = fA.take("za", [P, N + 2])
    cg = fA.take("cg", [P, N])
    ca = fA.take("ca", [P, N])
    gm = fA.take("gm", [P, N])
    ztail = fA.take("ztail", [P, 2 * FC, S + 2])
    cpar = fA.take("cpar", [P, 2, GC, 20])
    par_rows = Region(fA.at, 2 * GC * P * 4).take("par_rows", [20, 2, GC * P])
    ytok = fA.take("ytok", [P, NB, D])
    fZ = r_z.again()
    trow = fZ.take("trow", [S + 2, F2])
    ytok8 = fZ.take("ytok8", [S, D])

    sems = {}

    def s(name):
        if name not in sems:
            sems[name] = sem(name)
        return sems[name]

    bias_in = [sem("bias_in0"), sem("bias_in1")]
    begins = sem("begins")
    mix_hi, mix_lo = sem("mix_hi"), sem("mix_lo")
    slice_mm = sem("slice_mm")
    slice_read = sem("slice_read")
    DIAG = [0, 512, 896, 1152]
    SCORE_AT = [(5, 0), (6, 0), (7, 0), (6, 384)]
    USED_IN = 4 + 4 * Z_N
    USED_OUT = 4 + 4 * U_FFN

    class Chain:

        def __init__(self, eng, semaphore):
            self.eng, self.sem, self.n = eng, semaphore, 0

        def __call__(self, ins):
            self.n += 1
            ins.then_inc(self.sem, 1)
            self.eng.wait_ge(self.sem, self.n)

    out_count = [0]

    def store(eng, dst, src):
        out_count[0] += 16
        eng.dma_start(dst, src).then_inc(out_done, 16)

    def barrier(eng, k):
        eng.drain().then_inc(stage, 1)
        eng.wait_ge(stage, 4 * k)

    def begun(eng):
        eng.sem_inc(begins)

    def heads_of(ap, q):
        return ap.rearrange("p (k q b) -> p q k b", q=2, b=S)[:, q]

    NORMS = [(Z_AV + i, GAV + i, ones, P) for i in range(4)] + [(Z_BK, GBK, pairones, 64)]
    NORMS += [(Z_BQ + i, GBQ, pairones, 64) for i in range(2)] + [(Z_CV + i, GCH + i, ones, P) for i in range(4)]
    NORMS += [(Z_BQ + i, GBQ, pairones, 64) for i in range(2, 8)]
    NORM_SLICES = {21: (0, 1), 22: (2, 3), 23: (4,), 24: (5,), 25: (6,), 26: (7, 8), 27: (9, 10), 28: (11, 12),
                   29: (13, 14), 30: (15, 16)}
    LAST_SLICE = 30

    def norm_banks(g):
        ks = NORM_SLICES.get(g, ())
        return list(zip(ks, (4, 6) if len(ks) == 2 else (6,)))

    def squares_act(act, g):
        for k in NORM_SLICES.get(g, ()):
            act.wait_ge(z_free, NORMS[k][0] + 3)
            if k >= 2:
                act.wait_ge(s("norm_var"), k - 1)
            nc.scalar.activation(nsq[:, k % 2, :], zT[:, NORMS[k][0], :], ACT.Square).then_inc(s("norm_sq"), 1)

    def roots_act(act, g):
        for k in NORM_SLICES.get(g, ()):
            act.wait_ge(s("norm_var"), k + 1)
            nc.scalar.activation(nvar[:, k % 2, :], nvar[:, k % 2, :], ACT.Sqrt).then_inc(s("norm_root"), 1)

    def norms_pe(pe, g):
        for k, b in norm_banks(g):
            pe.wait_ge(s("norm_sq"), k + 1)
            for h in range(2):
                mm = nc.tensor.matmul(ps[:, b + h, 0:NH], NORMS[k][2][:], nsq[:, k % 2, h * NH:(h + 1) * NH],
                                      start=True, stop=True)
        return mm

    def norms_dve(dve, g, link):
        for k, b in norm_banks(g):
            if k >= 2:
                dve.wait_ge(s("norm_out"), k - 1)
            nc.vector.tensor_scalar(halves(nvar[:, k % 2, :]), pair(b), 1.0 / NORMS[k][3], EPS,
                                    ALU.mult, ALU.add).then_inc(s("norm_var"), 1)
        for k, _ in norm_banks(g):
            tile, gain = NORMS[k][:2]
            dve.wait_ge(s("norm_root"), k + 1)
            link(nc.vector.reciprocal(nvar[:, k % 2, :], nvar[:, k % 2, :]))
            nc.vector.scalar_tensor_tensor(out=zT[:, tile, :], in0=zT[:, tile, :], scalar=vecs[:, gain:gain + 1],
                                           in1=nvar[:, k % 2, :], op0=ALU.mult, op1=ALU.mult)\
                .then_inc(s("norm_out"), 1)
            dve.wait_ge(s("norm_out"), k + 1)

    @block.tensor
    def _(pe):
        def unit_mm(q0, bank, before=None):
            for k in range(4):
                pe.wait_ge(w_lo, q0 + (k + 1))
                if before is not None:
                    before(k)
                tile_mm(k, bank, whi, wlo)

        def tile_mm(k, bank, w_h, w_l, x_h=None, x_l=None):
            x_h, x_l = x_h or act_hi, x_l or act_lo
            for kind, (w, x) in enumerate(((w_h, x_h), (w_h, x_l), (w_l, x_h))):
                for c in range(4):
                    for h in range(2):
                        mm = nc.tensor.matmul(ps[:, bank + h, 0:NH], w[:, k, c, :],
                                              x[:, 4 * c + k, h * NH:(h + 1) * NH],
                                              start=(k == 0 and kind == 0 and c == 0),
                                              stop=(k == 3 and kind == 2 and c == 3))
            mm.then_inc(w_used, 1)

        pe.wait_ge(const_made, 1)
        pe.wait_ge(vec_in, 16 * 8)
        nc.tensor.transpose(ps[:, 7, 0:42], vrow[0:42, :], ident[0:42, 0:42]).then_inc(vec_tr, 1)
        pe.wait_ge(s("rel_in"), 32)
        pe.wait_ge(s("rel_set"), 1)
        nc.tensor.matmul(ps[0:16, 6, 0:384], rel33[:], hot[:], start=True, stop=True).then_inc(s("rel_mm"), 1)
        for idx in range(16):
            i, cg_ = idx // 4, idx % 4
            if cg_ == 0:
                pe.wait_ge(x_in[i], 16)
            if idx >= 6:
                pe.wait_ge(x_ev_v if idx % 2 else x_ev_a, (idx - 6) // 2 + 1)
            for c in range(4):
                t = nc.tensor.transpose(ps[:, idx % 6, c * P:(c + 1) * P], xtok[:, i, (4 * cg_ + c) * P:(4 * cg_ + c + 1) * P],
                                        ident[:])
            t.then_inc(x_tr, 1)
        pe.wait_ge(x_in[4], 16)
        pe.wait_ge(s("rel_read"), 1)
        for c in range(KC):
            t = nc.tensor.transpose(ps[:, 6, c * S:(c + 1) * S], xtok[0:S, 4, c * P:(c + 1) * P], ident[0:S, 0:S])
        t.then_inc(x_tr, 1)
        pe.wait_ge(wg_lo, 1)
        for k in range(4):
            pe.wait_ge(h_lo, 4 * (k + 1))
            tile_mm(k, 4, whi, wlo)
        pe.wait_ge(rs_diag, 1)
        for i in range(NB):
            nc.tensor.matmul(ps[:, 7, i * P:(i + 1) * P], ones[:], xjunk[:, i * P:(i + 1) * P], start=True, stop=True)
        nc.tensor.matmul(ps[:, 6, 256:256 + S], ones[0:S, :], xjunk[0:S, 512:512 + S], start=True, stop=True)\
            .then_inc(rs_mm, 1)

        with pe.Fori(0, (SLICE0 + 1) // 2) as i:
            for u in range(2):
                pe.wait_ge(z_free, i * 2 + (u + 1))
                unit_mm(i * 8 + 4 * u, 2 * u)

        def keys_and_values(g):
            for i in range(2):
                h = 2 * (g - SLICE0) + i
                for j in range(NB):
                    nc.tensor.transpose(ps[:, 4 + i, j * P:(j + 1) * P], zT[:, Z_CV + h, j * P:(j + 1) * P], ident[:])
            for j in range(NB):
                t = nc.tensor.transpose(ps[:, 6, j * P:(j + 1) * P], zT[:, Z_CK + g - SLICE0, j * P:(j + 1) * P], ident[:])
            if g > SLICE0:
                for h in range(4):
                    t = nc.tensor.transpose(ps[0:S, 7, h * P:(h + 1) * P], zT[:, Z_CV + h, T:N], ident[:])
                return t
            pe.wait_ge(s("c_rows"), 1)
            for j in range(NB):
                nc.tensor.transpose(ps[:, 7, 4 * j:4 * j + 4], gi[:, 2, j * P:(j + 1) * P], ident[0:4, 0:4])
                nc.tensor.transpose(ps[:, 7, 16 + 4 * j:20 + 4 * j], gi[:, 5, j * P:(j + 1) * P], ident[0:4, 0:4])
            for hp in range(2):
                for q in range(2):
                    nc.tensor.matmul(ps[64 * q:64 * q + 64, 7, 64 + 16 * hp:80 + 16 * hp], sel[:, 2 * hp + q, 0:64],
                                     gs[:].rearrange("p a b -> p (a b)"), start=True, stop=True)
            for h in range(4):
                t = nc.tensor.matmul(ps[:, 7, 128 + S * h:128 + S * (h + 1)], sel[:, h, :], gi[:, 7, T:N],
                                     start=True, stop=True)
            return t

        def scores(h):
            r, t2 = 64 * (h % 2), h // 2
            nc.tensor.matmul(ps[:, 4, :], sel[:, h, :], gi[:, 6, 0:T], start=True, stop=True)
            for j in range(NB):
                b, at = SCORE_AT[j]
                mm = nc.tensor.matmul(ps[:, b, at:at + T - j * P], zT[r:r + 64, Z_CK + t2, j * P:(j + 1) * P],
                                      zT[r:r + 64, Z_CQ + t2, j * P:T], start=True, stop=True)
            return mm

        def outputs(h):
            for j in range(NB):
                p_j = pmat[:, DIAG[j]:DIAG[j] + T - j * P]
                nc.tensor.matmul(ps[:, 5, j * P:T], vtok[:, j, h, 0:P], p_j, start=(j == 0), stop=(j == NB - 1))
                nc.tensor.matmul(ps[:, 6, j * P:T], ones[:], p_j, start=(j == 0), stop=(j == NB - 1))
            mm = nc.tensor.matmul(ps[:, 4, :], sel[:, h, :], gi[:, 7, 0:T], start=True, stop=True)
            if h == 0:
                for hp in range(2):
                    mm = nc.tensor.transpose(ps[0:S, 7, hp * P:(hp + 1) * P], kws[:, hp, :], ident[:])
            if h == 1:
                for hh in range(4):
                    r = 64 * (hh % 2)
                    for j in range(NB):
                        mm = nc.tensor.matmul(ps[r:r + 64, 7, 129 * (hh // 2):129 * (hh // 2) + 129], kw[:, j, hh, :],
                                              vtok[:, j, hh, :], start=(j == 0), stop=(j == NB - 1))
            return mm

        def outer(hp):
            pe.wait_ge(s("c_vm"), 4)
            for q in range(2):
                for half in range(2):
                    mm = nc.tensor.matmul(ps[64 * q:64 * q + 64, 4 + half, :], k8[:, hp * P + 64 * q:hp * P + 64 * q + 64],
                                          vm[:, 2 * hp + q, half * 512:half * 512 + 512], start=True, stop=True)
            return mm

        def memory_out():
            for h in range(4):
                r = 64 * (h % 2)
                for b in range(S):
                    nc.tensor.matmul(ps[:, 4 + h % 2, S * h + b:S * h + b + 1], cst[r:r + 64, 2 * b + h // 2, :],
                                     zT[r:r + 64, Z_CQ + h // 2, T + b:T + b + 1], start=True, stop=True)
                mm = nc.tensor.matmul(ps[:, 4 + h % 2, 64 + S * h:64 + S * (h + 1)], ones[r:r + 64, :],
                                      nq[r:r + 64, h // 2, :], start=True, stop=True)
            return mm

        def slice_pe(g):
            if g > SLICE0:
                pe.wait_ge(slice_read, g - SLICE0)
            if g < SLICE0 + 2:
                mm = keys_and_values(g)
            elif g < SLICE0 + 10:
                h = (g - SLICE0 - 2) // 2
                mm = outputs(h) if (g - SLICE0) % 2 else scores(h)
            else:
                if g in (23, 24):
                    outer(g - 23)
                if g == 25:
                    memory_out()
                mm = norms_pe(pe, g)
            mm.then_inc(slice_mm, 1)

        slice_pe(SLICE0)
        for u in range(SLICE0 + 1, Z_N):
            pe.wait_ge(z_free, u + 1)
            unit_mm(4 * u, 2 * (u % 2))
            slice_pe(u)
        slice_pe(LAST_SLICE)
        pe.wait_ge(slice_read, LAST_SLICE - SLICE0 + 1)
        barrier(pe, 1)

        for j in range(NB):
            t = nc.tensor.transpose(ps[:, 0, j * P:(j + 1) * P], zT[:, Z_BV, j * P:(j + 1) * P], ident[:])
        t.then_inc(s("b_t"), 1)
        nc.tensor.transpose(ps[:, 1, 0:P], zT[:, Z_BK, T - P:T], ident[:])
        nc.tensor.transpose(ps[0:S, 1, 128:256], zT[:, Z_BK, T:N], ident[:])
        nc.tensor.transpose(ps[0:S, 1, 256:384], zT[:, Z_BV, T:N], ident[:]).then_inc(s("b_t"), 1)
        pe.wait_ge(s("kc_in"), 16 * 4)
        for b in range(S):
            t = nc.tensor.transpose(ps[:, 2 + b // 4, (b % 4) * P:(b % 4 + 1) * P], kc_[:, b, :], ident[:])
        t.then_inc(s("b_kct"), 1)
        pe.wait_ge(s("b_kct_read"), 2)
        pe.wait_ge(s("b_q8"), 1)
        for b in range(S):
            mm = nc.tensor.matmul(ps[:, 2, b * 16:b * 16 + 16], kct[:, b, :], qb_[:, b, :], start=True, stop=True)
        mm.then_inc(s("b_s8"), 1)
        pe.wait_ge(s("b_s8_read"), 1)
        nc.tensor.transpose(ps[:, 3, 0:P], s_t[:], ident[:]).then_inc(s("b_s8t"), 1)
        pe.wait_ge(s("b_p8"), 1)
        nc.tensor.transpose(ps[:, 2, 0:P], s_s[:, 0:P], ident[:]).then_inc(s("b_p8t"), 1)
        pe.wait_ge(s("b_p8t_read"), 1)
        for b in range(S):
            mm = nc.tensor.matmul(ps[:, 3, b * 16:b * 16 + 16], vc_[:, b, :], p_t[:, b * 16:b * 16 + 16],
                                  start=True, stop=True)
        mm.then_inc(s("b_o8"), 1)
        pe.wait_ge(s("b_vk"), 1)
        for kv in range(2):
            with pe.Fori(0, 2) as it:
                first = it * 8 + 16 * kv

                def qk(n):
                    sl, i = n // 4, n % 4
                    pe.wait_ge(s("b_pair"), it * 2 + (4 * kv + sl + 1))
                    pe.wait_ge(s("b_sc_free"), first + (n + 1))
                    for r in range(2):
                        lo = 0 if i else P
                        mm = nc.tensor.matmul(ps[:, 4 - 2 * r + n % 2, lo:256],
                                              qst[64 * r:64 * r + 64, sl, i * P:(i + 1) * P],
                                              kd[64 * r:64 * r + 64, kv, (i - 1) * P + lo:(i + 1) * P],
                                              start=True, stop=True)
                    mm.then_inc(s("b_qk"), 1)

                def turn(n):
                    i = n % 4
                    pe.wait_ge(s("b_prob"), first + (n + 1))
                    pe.wait_ge(s("b_pt"), first + (n + 1))
                    for r in range(2):
                        for kb in range(0 if i else 1, 2):
                            t = nc.tensor.transpose(ps[:, 6, (2 * r + kb) * P:(2 * r + kb + 1) * P],
                                                    sx[:, n % 4, r, kb * P:(kb + 1) * P], ident[:])
                    t.then_inc(s("b_turn"), 1)

                def pv(n):
                    i = n % 4
                    pe.wait_ge(s("b_pt"), first + (n + 2))
                    pe.wait_ge(s("b_o_free"), first + (n + 1))
                    for r in range(2):
                        for kb in range(0 if i else 1, 2):
                            mm = nc.tensor.matmul(ps[64 * r:64 * r + 64, 7 * (n % 2), 0:P],
                                                  vtb[:, i - 1 + kb, 64 * kv:64 * kv + 64],
                                                  pt[:, n % 2, (2 * r + kb) * P:(2 * r + kb + 1) * P],
                                                  start=(kb == 0 or i == 0), stop=(kb == 1))
                    mm.then_inc(s("b_o"), 1)

                for n in range(8 + 3):
                    if n < 8:
                        qk(n)
                    if 2 <= n < 10:
                        turn(n - 2)
                    if n >= 3:
                        pv(n - 3)
        pe.wait_ge(s("b_ended"), 2)
        barrier(pe, 2)

        pe.wait_ge(s("a_in"), 48)
        for g in range(4):
            t = nc.tensor.transpose(ps[:, 0, g * P:(g + 1) * P], ws[:, g, :], ident[:])
        t.then_inc(s("a_wt"), 1)
        for g in range(4):
            if g == 3:
                pe.wait_ge(s("a_vt_read"), 1)
            for j in range(NB):
                t = nc.tensor.transpose(ps[:, (1, 2, 3, 1)[g], j * P:(j + 1) * P],
                                        zT[:, Z_AV + g, j * P:(j + 1) * P], ident[:])
            t.then_inc(s("a_vt"), 1)
        pe.wait_ge(s("a_wt_read"), 1)
        for g in range(4):
            t = nc.tensor.transpose(ps[0:S, 0, g * P:(g + 1) * P], zT[:, Z_AV + g, T:N], ident[:])
        t.then_inc(s("a_v8"), 1)
        pe.wait_ge(s("a_wst"), 1)
        for g in range(4):
            pe.wait_ge(s("a_vt_read"), g + 1)
            b = 4 + g
            for j in range(NB):
                mm = nc.tensor.matmul(ps[:, b, j * P:(j + 1) * P], vnt[:, j, g, :], wst[:, g, :], start=True, stop=True)
            mm.then_inc(s("a_mix"), 1)
        pe.wait_ge(s("a_mix"), 4)
        barrier(pe, 3)

        for u in range(2):
            pe.wait_ge(z_free, U_OUT + u + 1)
            unit_mm(4 * (U_OUT + u), 2 * u,
                    before=(lambda k: pe.wait_ge(mix_lo, 4 * (k + 1))) if u == 0 else None)
        with pe.Fori(U_OUT // 2 + 1, U_FFN // 2) as i:
            for u in range(2):
                pe.wait_ge(z_free, i * 2 + (u + 1))
                unit_mm(i * 8 + 4 * u, 2 * u)

        def up_mm(q0, bank, before=None):
            for k in range(4):
                pe.wait_ge(w_lo, q0 + (k + 1))
                if before is not None:
                    before(k)
                tile_mm(k, bank, whi, wlo, h2_hi, h2_lo)

        def down_mm(q0, d0):
            for k in range(4):
                pe.wait_ge(w_lo, q0 + (k + 1))
                pe.wait_ge(s("d_add"), d0 + (k + 1))
                b = 4 + 2 * (k % 2)
                for kind, (w, x) in enumerate(((whi, g_hi), (whi, g_lo), (wlo, g_hi))):
                    for c in range(4):
                        for h in range(2):
                            mm = nc.tensor.matmul(ps[:, b + h, 0:NH], w[:, k, c, :], x[:, c, h * NH:(h + 1) * NH],
                                                  start=(kind == 0 and c == 0), stop=(kind == 2 and c == 3))
                mm.then_inc(w_used, 1)
                yield k

        def first_up(k):
            pe.wait_ge(s("h2_lo"), 13 + k)

        def sum_squares():
            pe.wait_ge(s("o_sum"), KC)
            for h in range(2):
                mm = nc.tensor.matmul(ps[:, 4 + h, 0:NH], ones[:], ssum[:, h * NH:(h + 1) * NH], start=True, stop=True)
            mm.then_inc(s("o_sum_mm"), 1)

        def turn_params(grp, d0):
            pe.wait_ge(s("par_in"), grp * 48 + 48)
            if d0 is not None:
                pe.wait_ge(s("d_add"), d0 + 2)
                begun(pe)
            for c in range(2 * GC):
                t = nc.tensor.transpose(ps[:, 6, 20 * c:20 * c + 20], par_rows[:, c // GC, (c % GC) * P:(c % GC + 1) * P],
                                        ident[0:20, 0:20])
            t.then_inc(s("par_turn"), 1)

        def up_units(q0, use0, j, before=None, params=None):
            for u in range(2):
                pe.wait_ge(z_free, use0 + (2 * j + u + 1))
                up_mm(q0 + 4 * u, 2 * u, before if u == 0 else None)
                if before is not None and u == 0:
                    sum_squares()
                if params is not None and u == 0:
                    turn_params(*params)

        up_units(4 * U_FFN, U_FFN, 0, first_up, (0, None))
        for j in range(1, GC):
            up_units(4 * U_FFN + 8 * j, U_FFN, j)
        with pe.Fori(1, NG) as i:
            q0, use0 = i * 48 + 4 * (U_FFN + U_GRP - 12), i * 8 + U_FFN
            up_units(q0, use0, 0, None, (i, i * 16 - 16))
            pe.wait_ge(s("par_ready"), i + 1)
            pe.wait_ge(s("g_lo"), i * GC)
            for m in range(GC):
                for _ in down_mm(q0 + (8 + 4 * m), i * 16 + (4 * m - 16)):
                    pass
            for j in range(1, GC):
                up_units(q0 + (16 + 8 * j), use0, j)

        def turn_tail(r):
            b = 2 + r % 2
            if r >= 2:
                pe.wait_ge(s("t_read"), r - 1)
            for c in range(4):
                t = nc.tensor.transpose(ps[0:S + 2, b, c * P:(c + 1) * P], ztail[:, 4 * r + c, :], ident[:])
            t.then_inc(s("t_turn"), 1)

        def turn_y(dt):
            pe.wait_ge(s("d_add"), (NG - 1) * 16 + dt + 3)
            if dt >= 2:
                pe.wait_ge(s("y_read"), dt - 1)
            for j in range(NB):
                t = nc.tensor.transpose(ps[:, dt % 2, j * P:(j + 1) * P], xT[:, dt, j * P:(j + 1) * P], ident[:])
            t.then_inc(s("y_turn"), 1)

        pe.wait_ge(z_free, U_FFN + 8 * NG + 2)
        tails = iter(range(FC // 2))
        for _ in range(6):
            turn_tail(next(tails))
        pe.wait_ge(s("g_lo"), NG * GC)
        for m in range(GC):
            for k in down_mm(4 * (U_ALL - GC + m), (NG - 1) * 16 + 4 * m):
                if 4 * m + k >= 1:
                    turn_y(4 * m + k - 1)
                    turn_tail(next(tails))
        turn_y(15)
        turn_tail(next(tails))
        assert next(tails, None) is None
        pe.wait_ge(s("t_read"), FC // 2)
        for q in range(4):
            if q == 0:
                pe.wait_ge(s("d_add"), NG * 16 + 2)
            for c in range(4):
                t = nc.tensor.transpose(ps[0:S, 4 + q, c * P:(c + 1) * P], xT[:, 4 * q + c, T:N], ident[:])
        t.then_inc(s("y8_turn"), 1)

    @block.scalar
    def _(act):
        link = Chain(act, chain_a)

        def q_hi(q, k, slot, landed):
            if k == 0:
                act.wait_ge(raw_in[slot], landed)
            act.wait_ge(w_used, q + 1)
            nc.scalar.activation(whi[:, k, :, :], rawq(k, slot), ACT.Copy)\
                .then_inc(w_hi, 1)

        def unit_hi(q0, slot, landed):
            for k in range(4):
                q_hi(q0 + k, k, slot, landed)

        act.dma_start(rel33[0:32, :], io["rel_bias"]).then_inc(s("rel_in"), 16)
        act.dma_start(hot[:], io["bucket_table"]).then_inc(s("rel_in"), 16)
        for rows, name, a, b in (((0, 16), "norm1", 0, D), ((16, 32), "norm2", 0, D),
                                 ((32, 36), "a_v_gain", 0, 512), ((36, 40), "c_h_gain", 0, 512)):
            act.dma_start(vrow[rows[0]:rows[1], :], io[name].rearrange("l (c p) -> (l c) p", p=P)).then_inc(vec_in, 16)
        act.dma_start(wg_raw[:], w_in[:, COL_G:COL_G + 8].rearrange("(c p) n -> p c n", p=P)).then_inc(wg_in, 16)
        for row, name in ((40, "b_q_gain"), (41, "b_k_gain")):
            for h in range(2):
                act.dma_start(vrow[row:row + 1, 64 * h:64 * h + 64], io[name]).then_inc(vec_in, 16)
        cgb = io["c_gate_bias"].rearrange("l g -> g l")
        act.dma_start(gbi[:], cgb[0:4]).then_inc(misc_in, 16)
        act.dma_start(gbf[32:36, :], cgb[4:8]).then_inc(misc_in, 16)
        act.dma_start(m0[:], io["state_mlstm_m"].rearrange("l b h -> h (l b)")).then_inc(misc_in, 16)
        for q in range(2):
            act.dma_start(ns[64 * q:64 * q + 64, :],
                          io["state_mlstm_n"].rearrange("l b (k two) d -> two d (l b k)", two=2)[q]).then_inc(s("n_in"), 16)
        store(act, io["ffn_conv_sample"][0, :, 0, :], io["state_ffn_conv"][0, :, 1, :])

        act.wait_ge(s("rel_mm"), 1)
        nc.scalar.activation(brow[:], ps[0:16, 6, 0:384], ACT.Copy, scale=8.0).then_inc(s("rel_read"), 1)
        for idx in range(0, 16, 2):
            i, c4 = idx // 4, idx % 4
            act.wait_ge(x_tr, idx + 1)
            nc.scalar.activation(xT[:, 4 * c4:4 * c4 + 4, i * P:(i + 1) * P],
                                 ps[:, idx % 6, :].rearrange("p (c n) -> p c n", c=4), ACT.Copy).then_inc(x_ev_a, 1)
        act.wait_ge(s("rel_read"), 1)
        act.dma_start(bias_rows, brow[:].rearrange("h (a w) -> h a w", a=1).broadcast_to([16, P + 1, 384]))\
            .then_inc(s("rel_out"), 16)
        act.wait_ge(x_ev_a, 8)
        act.wait_ge(x_ev_v, 9)
        act.wait_ge(vec_ev, 1)
        act.wait_ge(wg_in, 16)
        act.wait_ge(ring_zero, 2)
        gates = wg_raw[:].rearrange("p (c k) n -> p k c n", k=4)
        nc.scalar.activation(whi[:, :, :, 0:4], gates[:, :, :, 0:4], ACT.Copy)
        nc.scalar.activation(whi[:, :, :, 32:36], gates[:, :, :, 4:8], ACT.Copy).then_inc(wg_hi, 1)
        for c in K_ORDER:
            nc.scalar.activation(act_hi[:, c, :], xT[:, c, :], ACT.Copy, scale=vecs[:, G1 + c:G1 + c + 1]).then_inc(h_hi, 1)
        act.wait_ge(var_v, 1)
        nc.scalar.activation(small[:, 16:21], small[:, 8:13], ACT.Sqrt).then_inc(var_a, 1)

        def hi_pairs(first, last):
            with act.Fori(first, last) as i:
                unit_hi(i * 8 + 4, 1, i * 16 + 16)
                unit_hi(i * 8 + 8, 0, i * 16 + 32)

        unit_hi(0, 0, 16)
        hi_pairs(0, 2)
        act.wait_ge(s("c_fabs"), 1)
        link(nc.scalar.activation(gf[32:36, 2, :], gf[32:36, 1, :], ACT.Exp, scale=-1.0))
        nc.scalar.activation(gf[32:36, 2, :], gf[32:36, 2, :], ACT.Ln, bias=1.0).then_inc(s("c_ln"), 1)
        hi_pairs(2, 4)
        act.wait_ge(s("c_lines"), 1)
        nc.scalar.activation(gi[:, 7, :], gi[:, 4, :], ACT.Exp, scale=-1.0)
        nc.scalar.activation(gi[:, 5, 0:T], gi[:, 2, 0:T], ACT.Exp, bias=gi[:, 6, T - 1:T])
        nc.scalar.activation(gs[:].rearrange("p a b -> p (a b)"), gs[:].rearrange("p a b -> p (a b)"), ACT.Exp)\
            .then_inc(s("c_exp"), 1)
        store(act, io["m_prompt"].rearrange("l b h -> h (l b)"), gi[:, 4, T - 1:T])
        store(act, io["m_sample"].rearrange("l b h -> h (l b)"), gi[:, 4, T:N])
        hi_pairs(4, (SLICE0 + 1) // 2)

        def values(g):
            for i in range(2):
                nc.scalar.activation(vtok[:, :, 2 * (g - SLICE0) + i, 0:P], ps[:, 4 + i, :].rearrange("p (j n) -> p j n", j=NB),
                                     ACT.Copy).then_inc(s("c_v_read"), 1)
                yield
            if g > SLICE0:
                nc.scalar.activation(v8[:], ps[0:S, 7, :], ACT.Copy).then_inc(s("c_v_read"), 1)

        def decays(h):
            act.wait_ge(s("c_masked"), h + 1)
            for j in range(NB):
                b_j = ct[:, j, h:h + 1]
                last = nc.scalar.activation(dmat[:, DIAG[j]:DIAG[j] + P], tmpm[:, j * P:(j + 1) * P], ACT.Exp, bias=b_j)
                if j < NB - 1:
                    last = nc.scalar.activation(dmat[:, DIAG[j] + P:DIAG[j] + T - j * P], ps[:, 4, (j + 1) * P:T],
                                                ACT.Exp, bias=b_j)
            last.then_inc(s("c_decay"), 1)
            yield

        def outputs(h):
            nc.scalar.activation(qab[:], ps[:, 6, :], ACT.Abs).then_inc(s("c_abs"), 1)
            yield
            if h == 1:
                act.wait_ge(s("c_mem_read"), 1)
                for q in range(2):
                    store(act, io["C_prompt"].rearrange("l b (k two) d e -> two d (l b k) e", two=2)[q],
                          cout[64 * q:64 * q + 64, :, 0:P])
                    store(act, io["n_prompt"].rearrange("l b (k two) d -> two d (l b k)", two=2)[q],
                          cout[64 * q:64 * q + 64, :, P])

        def late(g):
            if g == 20:
                act.wait_ge(z_free, Z_AV + 4 + 2)
                link(nc.scalar.activation(zT[:, Z_AV:Z_AV + 4, :], zT[:, Z_AV:Z_AV + 4, :], ACT.Gelu))
                yield
                act.wait_ge(s("c_head"), 4)
                for q in range(2):
                    act.dma_start(cst[64 * q:64 * q + 64, :, :],
                                  io["state_mlstm_C"].rearrange("l b (k two) d e -> two d (l b k) e", two=2)[q])\
                        .then_inc(s("c_in"), 16)
                squares_act(act, 21)
                yield
                nc.scalar.activation(zT[:, Z_AU:Z_AU + 4, :], zT[:, Z_AU:Z_AU + 4, :], ACT.Gelu)
                return
            if g == 25:
                abs8 = None
                for q in range(2):
                    abs8 = nc.scalar.activation(heads_of(hs[:, 0, :], q), heads_of(ps[:, 4 + q, 64:96], q), ACT.Abs)
                abs8.then_inc(s("c_abs8"), 1)
                for q in range(2):
                    store(act, io["n_sample"].rearrange("l b (k two) d -> two d (l b k)", two=2)[q], ns[64 * q:64 * q + 64, :])
                    store(act, io["C_sample"].rearrange("l b (k two) d e -> two d (l b k) e", two=2)[q],
                          cst[64 * q:64 * q + 64, :, :])
                for t, name in ((kc_, "cache_swa_k"), (vc_, "cache_swa_v")):
                    act.dma_start(t[1:P, :, :], io[name][0, :, 1:P].rearrange("b w h d -> w b (h d)")).then_inc(s("kc_in"), 16)
            roots_act(act, g)
            yield
            if g == 25:
                act.wait_ge(s("c_num8_read"), 1)
            if g == 27:
                nc.scalar.activation(zT[:, Z_CO:Z_CO + 4, :], zT[:, Z_CO:Z_CO + 4, :], ACT.Sigmoid).then_inc(s("c_sig"), 1)
            squares_act(act, g + 1)

        def slice_act(g):
            act.wait_ge(slice_mm, g - SLICE0 + 1)
            if g < SLICE0 + 2:
                yield from values(g)
            elif g < SLICE0 + 10:
                h = (g - SLICE0 - 2) // 2
                yield from (outputs(h) if (g - SLICE0) % 2 else decays(h))
                if g == 20:
                    yield from late(g)
            else:
                yield from late(g)

        for g in range(SLICE0, LAST_SLICE + 1):
            work = slice_act(g)
            next(work, None)
            if g + 2 <= U_OUT:
                for k in range(4):
                    u = g + 2
                    q_hi(4 * u + k, k, u % 2, 16 * (u // 2) + 16)
                    next(work, None)
            for _ in work:
                pass
        act.wait_ge(s("rel_out"), 16)
        act.wait_ge(out_done, out_count[0])
        barrier(act, 1)

        sinks = io["b_sinks"]
        act.dma_start(sinkbc[:], bass.AP(tensor=sinks.tensor, offset=sinks.offset, ap=[[0, P], [1, 16]])).then_inc(s("b_in"), 16)
        act.dma_start(bsink[:], bass.AP(tensor=sinks.tensor, offset=sinks.offset, ap=[[0, S], [1, 16], [1, 1]])).then_inc(s("b_in"), 16)
        act.dma_start(bias_s[:, 1:P], bass.AP(tensor=bias_rows.tensor, offset=128, ap=[[0, S], [BIAS_PITCH, 16], [1, P - 1]])).then_inc(s("b_in"), 16)
        act.dma_start(bias_s[:, 0:1], bass.AP(tensor=bias_rows.tensor, offset=255, ap=[[0, S], [BIAS_PITCH, 16], [1, 1]])).then_inc(s("b_in"), 16)
        act.wait_ge(s("b_t"), 1)
        link(nc.scalar.activation(vtb[:], ps[:, 0, :].rearrange("p (j n) -> p j n", j=NB), ACT.Copy))
        act.wait_ge(s("b_t"), 2)
        link(nc.scalar.activation(ktb[:], ps[:, 1, 0:P], ACT.Copy))
        link(nc.scalar.activation(kv8[:], ps[0:S, 1, 128:384].rearrange("p (a n) -> p a n", a=2), ACT.Copy))
        act.dma_start(kc_[0:1, :, :], kv8[:, 0, :]).then_inc(s("kc_in"), 16)
        act.dma_start(vc_[0:1, :, :], kv8[:, 1, :]).then_inc(s("kc_in"), 16)
        act.drain().then_inc(s("b_vk_a"), 1)
        store(act, io["k_prompt"].rearrange("l b w h d -> (l b w) (h d)"), ktb[:])
        store(act, io["v_prompt"].rearrange("l b w h d -> (l b w) (h d)"), vtb[:, NB - 1, :])
        store(act, io["k_sample"].rearrange("l b w h d -> (l b w) (h d)"), kv8[:, 0, :])
        store(act, io["v_sample"].rearrange("l b w h d -> (l b w) (h d)"), kv8[:, 1, :])
        for i in range(2):
            act.wait_ge(s("b_kct"), 1)
            nc.scalar.activation(kct[:, 4 * i:4 * i + 4, :], ps[:, 2 + i, :].rearrange("p (j n) -> p j n", j=NB),
                                 ACT.Copy).then_inc(s("b_kct_read"), 1)
        act.wait_ge(s("b_s8"), 1)
        nc.scalar.activation(s_t[:], ps[:, 2, 0:P], ACT.Copy).then_inc(s("b_s8_read"), 1)
        act.wait_ge(s("b_max8"), 1)
        nc.scalar.activation(s_s[:], s_s[:], ACT.Exp, bias=mxn[:, 0, 0, 1:2], accum_out=mxn[:, 0, 0, 2:3]).then_inc(s("b_exp8"), 1)
        act.wait_ge(s("b_p8t"), 1)
        nc.scalar.activation(p_t[:], ps[:, 2, 0:P], ACT.Copy).then_inc(s("b_p8t_read"), 1)
        act.wait_ge(s("b_o8_read"), 1)
        for kv in range(2):
            with act.Fori(0, 2) as it:
                first = it * 8 + 16 * kv

                def exps(n):
                    lo = 0 if n % 4 else P
                    act.wait_ge(s("b_max"), first + (n + 1))
                    for r in range(2):
                        e = nc.scalar.activation(sx[:, n % 4, r, lo:257], sx[:, n % 4, r, lo:257], ACT.Exp,
                                                 bias=mxn[:, n % 4, r, 1:2], accum_out=mxn[:, n % 4, r, 2:3])
                    e.then_inc(s("b_exp"), 1)

                def read_turn(n):
                    lo = 0 if n % 4 else P
                    act.wait_ge(s("b_turn"), first + (n + 5))
                    act.wait_ge(s("b_o"), first + (n + 1))
                    nc.scalar.activation(pt[:, n % 2, :].rearrange("p (r k) -> p r k", r=2)[:, :, lo:256],
                                         ps[:, 6, :].rearrange("p (r k) -> p r k", r=2)[:, :, lo:256], ACT.Copy)\
                        .then_inc(s("b_pt"), 1)

                for n in range(8 + 2):
                    if n < 8:
                        exps(n)
                    if n >= 2:
                        read_turn(n - 2)
        act.wait_ge(s("b_pt"), 33)
        act.wait_ge(out_done, out_count[0])
        act.wait_ge(s("b_ended"), 2)
        barrier(act, 2)

        act.dma_start(ws[:], io["a_spatial_w"].rearrange("l g t s -> t (l g) s")).then_inc(s("a_in"), 16)
        asb, asw = io["a_spatial_b"], io["a_spatial_w"]
        act.dma_start(bbc[:], bass.AP(tensor=asb.tensor, offset=asb.offset, ap=[[0, P], [P, 4], [1, P]])).then_inc(s("a_in"), 16)
        act.dma_start(w00[:], bass.AP(tensor=asw.tensor, offset=asw.offset, ap=[[0, P], [P * P, 4], [1, 1]])).then_inc(s("a_in"), 16)
        act.wait_ge(s("a_v8"), 1)
        link(nc.scalar.activation(vn8[:], ps[0:S, 0, :], ACT.Copy))
        store(act, io["chunk_v"].rearrange("l b t w -> (l b t) w"), vn8[:])
        act.wait_ge(out_done, out_count[0])
        barrier(act, 3)

        for c in K_ORDER:
            nc.scalar.activation(act_hi[:, c, :], zT[:, MIX_TILES[c], :], ACT.Copy).then_inc(mix_hi, 1)

        def residual(n, u, tile):
            act.wait_ge(z_free, n + (Z_N + 3))
            nc.scalar.activation(ssq[:, u, :], xT[:, tile, :].rearrange("p a n -> p (a n)"), ACT.Square).then_inc(s("o_sq"), 1)
            nc.scalar.activation(h2_hi[:, tile, :].rearrange("p a n -> p (a n)"), xT[:, tile, :].rearrange("p a n -> p (a n)"),
                                 ACT.Copy, scale=gain2[:, u:u + 1]).then_inc(s("h2_hi"), 1)

        with act.Fori(U_OUT // 2, U_FFN // 2) as i:
            unit_hi(i * 8 + 4, 1, i * 16 + 16)
            residual(i * 2 - U_OUT, 0, bass.ds(i * 2 - U_OUT, 1))
            unit_hi(i * 8 + 8, 0, i * 16 + 32)
            residual(i * 2 + (1 - U_OUT), 1, bass.ds(i * 2 + (1 - U_OUT), 1))
        act.wait_ge(s("o_mean"), 1)
        nc.scalar.activation(rs2[:], rs2[:], ACT.Sqrt).then_inc(s("o_root"), 1)

        def start_g(n, j):
            act.wait_ge(s("f_zg"), n + 1)
            if j == 0:
                act.wait_ge(s("par_turn"), n_group + 1)
                nc.scalar.activation(cpar[:].rearrange("p a c n -> p (a c n)"), ps[:, 6, 0:40 * GC], ACT.Copy)\
                    .then_inc(s("par_ready"), 1)
                act.wait_ge(s("par_ready"), n_group + 1)
            nc.scalar.activation(cg[:], zg[:, 2:], ACT.Identity, scale=cpar[:, 0, j, 18:19], bias=cpar[:, 0, j, 19:20])\
                .then_inc(s("f_tg"), 1)

        def start_a(n, j):
            act.wait_ge(s("f_za"), n + 1)
            nc.scalar.activation(ca[:], za[:, 2:], ACT.Identity, scale=cpar[:, 1, j, 18:19], bias=cpar[:, 1, j, 19:20])\
                .then_inc(s("f_ta"), 1)

        def silu(n, j):
            act.wait_ge(s("f_cg"), n + 1)
            nc.scalar.activation(cg[:], cg[:], ACT.Silu).then_inc(s("f_silu"), 1)

        def gated_hi(n, j):
            act.wait_ge(s("f_m"), n + 1)
            nc.scalar.activation(g_hi[:, j, :], gm[:], ACT.Copy).then_inc(s("g_hi"), 1)

        def ffn_group_act(q1, pair0, n0, grp, with_down):
            nonlocal n_group
            n_group = grp
            units = GC * 3 if with_down else U_GRP
            due = {}
            for j in range(GC):
                g = 2 * j + (GC if with_down and j else 0)
                due.setdefault((g + 2, 1), []).append((start_g, j))
                late = g + 3 <= units
                due.setdefault((g + 3, 0) if late else (units, 3), []).append((start_a, j))
                due.setdefault((g + 3, 1) if late else (units, 3), []).append((silu, j))
                hi_at = ((GC + 2, 3) if with_down and j == 0 else (g + 3, 2)) if late else (units, 3)
                due.setdefault(hi_at, []).append((gated_hi, j))
            for u in range(1, units + 1):
                for k in range(4):
                    q_hi(q1 + (4 * (u - 1) + k), k, u % 2, pair0 + 16 * (u // 2))
                    for step, j in due.get((u, k), []):
                        if step is gated_hi and j == 0 and with_down:
                            act.wait_ge(w_used, q1 + (4 * (GC + 1) + 4))
                        step(n0 + j, j)

        n_group = 0
        ffn_group_act(4 * U_FFN + 4, 8 * U_FFN + 16, 0, 0, False)
        with act.Fori(1, NG) as i:
            ffn_group_act(i * 48 + 4 * (U_FFN + U_GRP - 12 + 1), i * 96 + 8 * (U_FFN + U_GRP - 12 + 2), i * GC, i, True)

        def read_tail(r):
            act.wait_ge(s("t_turn"), r + 1)
            nc.scalar.activation(trow[:, 512 * r:512 * r + 512], ps[0:S + 2, 2 + r % 2, :], ACT.Copy).then_inc(s("t_read"), 1)

        r = 0
        for u in range(U_ALL - GC, U_ALL):
            for k in range(4):
                if u > U_ALL - GC:
                    q_hi(4 * u + k, k, u % 2, 16 * (u // 2 + 1))
                    reads = 1
                else:
                    reads = 2
                for _ in range(reads):
                    if r < 6 or u > U_ALL - GC:
                        if r < FC // 2:
                            read_tail(r)
                            r += 1
        while r < FC // 2:
            read_tail(r)
            r += 1
        act.wait_ge(s("y8_turn"), 1)
        nc.scalar.activation(ytok8[:], ps[0:S, 4:8, :].rearrange("p a n -> p (a n)"), ACT.Copy).then_inc(s("y8_read"), 1)

    def read_y(dve, dt):
        dve.wait_ge(s("y_turn"), dt + 1)
        nc.vector.tensor_copy(ytok[:, :, dt * P:(dt + 1) * P], ps[:, dt % 2, :].rearrange("p (j n) -> p j n", j=NB))\
            .then_inc(s("y_read"), 1)

    @block.vector
    def _(dve):
        link = Chain(dve, chain_v)
        mult, add, sub, mx = ALU.mult, ALU.add, ALU.subtract, ALU.max
        tt, stt, ts = nc.vector.tensor_tensor, nc.vector.scalar_tensor_tensor, nc.vector.tensor_scalar

        dve.nop().then_inc(z_free, 2)
        nc.vector.memset(rel33[32:33, :], NEG).then_inc(s("rel_set"), 1)
        link(nc.vector.memset(small[:], 1.0))
        dve.wait_ge(vec_tr, 1)
        nc.vector.tensor_copy(vecs[:, 0:42], ps[:, 7, 0:42]).then_inc(vec_ev, 1)
        for idx in range(1, 16, 2):
            i, c4 = idx // 4, idx % 4
            dve.wait_ge(x_tr, idx + 1)
            nc.vector.tensor_copy(xT[:, 4 * c4:4 * c4 + 4, i * P:(i + 1) * P],
                                  ps[:, idx % 6, :].rearrange("p (c n) -> p c n", c=4)).then_inc(x_ev_v, 1)
            if c4 == 3:
                link(nc.vector.tensor_tensor_reduce(out=xjunk[:], in0=xtok[:, i, :], in1=xtok[:, i, :], scale=1.0,
                                                    scalar=0.0, op0=mult, op1=add, accum_out=small[:, i:i + 1]))
        dve.wait_ge(x_tr, 17)
        nc.vector.tensor_copy(xT[:, :, T:N], ps[:, 6, 0:P].rearrange("p (c n) -> p c n", c=KC)).then_inc(x_ev_v, 1)
        link(nc.vector.tensor_tensor_reduce(out=xjunk[0:S, :], in0=xtok[0:S, 4, :], in1=xtok[0:S, 4, :], scale=1.0,
                                            scalar=0.0, op0=mult, op1=add, accum_out=small[0:S, 4:5]))
        dve.wait_ge(x_ev_v, 9)
        dve.wait_ge(x_ev_a, 8)
        dve.wait_ge(vec_ev, 1)
        nc.vector.tensor_scalar(small[:, 8:13], small[:, 0:5], 1.0 / D, EPS, mult, add).then_inc(var_v, 1)
        for i, c in enumerate(K_ORDER):
            dve.wait_ge(h_hi, i + 1)
            stt(out=act_lo[:, c, :], in0=xT[:, c, :], scalar=vecs[:, G1 + c:G1 + c + 1], in1=act_hi[:, c, :].bitcast(F32),
                op0=mult, op1=sub).then_inc(h_lo, 1)
        dve.wait_ge(var_a, 1)
        link(nc.vector.reciprocal(small[:, 24:29], small[:, 16:21]))
        dve.wait_ge(const_made, 1)
        for i in range(NB):
            ts(xjunk[:, i * P:(i + 1) * P], ident[:], small[:, 24 + i:25 + i], None, mult)
        ts(xjunk[0:S, 512:512 + S], ident[0:S, 0:S], small[0:S, 28:29], None, mult).then_inc(rs_diag, 1)
        dve.wait_ge(rs_mm, 1)
        nc.vector.tensor_copy(rs1[:, 0:T], ps[:, 7, :])
        nc.vector.tensor_copy(rs1[:, T:N], ps[:, 6, 256:256 + S]).then_inc(rs_ready, 1)
        dve.wait_ge(rs_ready, 1)
        def read_pairs(first, last):
            with dve.Fori(first, last) as i:
                for u in range(2):
                    dve.wait_ge(w_used, i * 8 + (4 * u + 8))
                    tt(zT[:, bass.ds(i * 2 + u, 1), :].rearrange("p a (h n) -> p (a h) n", h=2), pair(2 * u),
                       halves(rs1[:]), mult).then_inc(z_free, 1)

        read_pairs(0, 2)
        dve.wait_ge(spilled, 16)
        dve.wait_ge(h_lo, KC)
        dve.wait_ge(misc_in, 48)
        r4, rf = slice(0, 4), slice(32, 36)
        tt(halves(gf[rf, 0, :]), ps[rf, 4:6, 0:NH], halves(rs1[rf, :]), mult)
        tt(halves(gi[:, 0, :]), ps[r4, 4:6, 0:NH], halves(rs1[r4, :]), mult).then_inc(s("c_gates_read"), 1)
        dve.wait_ge(s("c_gates_read"), 1)
        link(ts(gf[rf, 0, :], gf[rf, 0, :], gbf[rf, :], None, add))
        stt(out=gf[rf, 1, :], in0=gf[rf, 0, :], scalar=-1.0, in1=gf[rf, 0, :], op0=mult, op1=mx).then_inc(s("c_fabs"), 1)
        link(ts(gi[:, 0, :], gi[:, 0, :], gbi[:], None, add))
        link(ts(gf[rf, 3, :], gf[rf, 0, :], 0.0, None, ALU.min))
        read_pairs(2, 4)
        dve.wait_ge(s("c_ln"), 1)
        link(tt(gf[rf, 3, :], gf[rf, 3, :], gf[rf, 2, :], sub))
        link(nc.vector.memset(gf[rf, 0, :], 1.0))
        link(nc.vector.tensor_tensor_scan(gf[rf, 1, 0:T], gf[rf, 0, 0:T], gf[rf, 3, 0:T], 0.0, mult, add))
        link(nc.vector.tensor_copy(gf[rf, 1, T:N], gf[rf, 3, T:N]))
        link(nc.vector.tensor_copy(gi[:, 1, :], gf[rf, 1, :]))
        link(tt(gi[:, 2, :], gi[:, 0, :], gi[:, 1, :], sub))
        link(nc.vector.tensor_tensor_scan(gi[:, 3, 0:T], gi[:, 2, 0:T], gi[:, 2, 0:T], 0.0, mx, mx))
        link(tt(gi[:, 3, T:N], gi[:, 2, T:N], m0[:], mx))
        link(tt(gi[:, 4, :], gi[:, 1, :], gi[:, 3, :], add))
        link(tt(gs[:, 0, :], gi[:, 2, T:N], gi[:, 3, T:N], sub))
        link(tt(gs[:, 1, :], m0[:], gi[:, 3, T:N], sub))
        ts(gi[:, 6, :], gi[:, 3, :], -1.0, None, mult).then_inc(s("c_lines"), 1)
        dve.wait_ge(s("c_exp"), 1)
        ts(gi[:, 5, 0:T], gi[:, 5, 0:T], 0.125, None, mult)
        ts(gs[:, 0, :], gs[:, 0, :], 0.125, None, mult).then_inc(s("c_rows"), 1)
        link(nc.vector.memset(vtok[:, :, :, P:P + 1], 1.0))
        read_pairs(4, (SLICE0 + 1) // 2)

        def keys(t2):
            if t2 == 0:
                link(nc.vector.tensor_copy(ct[:].rearrange("p a b -> p (a b)"), ps[:, 7, 0:32]))
                link(nc.vector.tensor_copy(cs[:].rearrange("p a b -> p (a b)"), ps[:, 7, 64:96]))
                link(nc.vector.tensor_copy(emts[:], ps[:, 7, 128:160]))
            for q in range(2):
                h = 2 * t2 + q
                tt(kw[:, :, h, :], ps[:, 6, :].rearrange("p (j d) -> p j d", j=NB)[:, :, 64 * q:64 * q + 64],
                   ct[:, 4:8, h:h + 1].broadcast_to([P, NB, 64]), mult)
            if t2 == 1:
                dve.wait_ge(s("n_in"), 32)
                link(tt(kws[:], zT[:, Z_CK:Z_CK + 2, T:N], cs[:, :, 0:S], mult))
                n_kb = ns[:].rearrange("p (b k) -> p k b", k=2)
                link(tt(n_kb, n_kb, cs[:, :, S:2 * S], mult))
                link(tt(n_kb, n_kb, kws[:], add))
                link(tt(nq[:], zT[:, Z_CQ:Z_CQ + 2, T:N], n_kb, mult))
            dve.wait_ge(s("c_v_read"), (2, 5)[t2])

        def scores(h):
            if h == 0:
                dve.wait_ge(out_done, 48)
            tt(tmpm[:].rearrange("p (j n) -> p j n", j=NB), ps[:, 4, :].rearrange("p (j n) -> p j n", j=NB),
               causal[:].rearrange("p (j n) -> p j n", j=1).broadcast_to([P, NB, P]), add).then_inc(s("c_masked"), 1)
            dve.wait_ge(s("c_decay"), h + 1)
            for j in range(NB):
                n, (b, at) = T - j * P, SCORE_AT[j]
                stt(out=pmat[:, DIAG[j]:DIAG[j] + n], in0=ps[:, b, at:at + n], scalar=0.125,
                    in1=dmat[:, DIAG[j]:DIAG[j] + n], op0=mult, op1=mult)

        def outputs(h):
            if h == 0:
                nc.vector.tensor_copy(k8[:], ps[0:S, 7, 0:256])
            if h == 1:
                nc.vector.tensor_copy(cout[:].rearrange("p a b -> p (a b)"), ps[:, 7, 0:258]).then_inc(s("c_mem_read"), 1)
            dve.wait_ge(s("c_abs"), h + 1)
            link(tt(den[:], qab[:], ps[:, 4, :], mx))
            link(nc.vector.reciprocal(den[:], den[:]))
            tt(zT[:, Z_CV + h, 0:T], ps[:, 5, :], den[:], mult).then_inc(s("c_head"), 1)

        def late(g):
            if g == 25:
                dve.wait_ge(s("c_abs8"), 1)
                link(tt(hs[:, 1, :], hs[:, 0, :], emts[:], mx))
                link(nc.vector.reciprocal(hs[:, 2, :], hs[:, 1, :]))
                for q in range(2):
                    o = tt(zT[:, Z_CV:Z_CV + 4, T:N].rearrange("p (k q) b -> p q k b", q=2)[:, q],
                           heads_of(ps[:, 4 + q, 0:32], q), heads_of(hs[:, 2, :], q), mult)
                o.then_inc(s("c_num8_read"), 1)
            norms_dve(dve, g, link)
            if g in (21, 22):
                for h in (2 * g - 42, 2 * g - 41):
                    tt(vm[:, h, :].rearrange("p (b e) -> p b e", b=S),
                       v8[:, h * P:(h + 1) * P].rearrange("p (a e) -> p a e", a=1).broadcast_to([S, S, P]),
                       ident[0:S, 0:S].rearrange("p (b a) -> p b a", a=1).broadcast_to([S, S, P]), mult)\
                        .then_inc(s("c_vm"), 1)
            if g == 22:
                dve.wait_ge(s("c_in"), 32)
                for hp in range(2):
                    c_v = cst[:].rearrange("p (b k) e -> p k b e", k=2)[:, hp, :, :]
                    link(tt(c_v, c_v, cs[:, hp, S:2 * S].rearrange("p (b a) -> p b a", a=1).broadcast_to([P, S, P]), mult))
            if g in (23, 24):
                for half in range(2):
                    c_v = cst[:].rearrange("p (b k) e -> p k b e", k=2)[:, g - 23, 4 * half:4 * half + 4, :]
                    link(tt(c_v, c_v, ps[:, 4 + half, :].rearrange("p (b e) -> p b e", b=4), add))
            if g == 28:
                dve.wait_ge(s("c_sig"), 1)
                for h in range(4):
                    tt(zT[:, Z_CO + h, :], zT[:, Z_CV + h, :], zT[:, Z_CO + h, :], mult)

        def slice_dve(g):
            dve.wait_ge(slice_mm, g - SLICE0 + 1)
            if g < SLICE0 + 2:
                keys(g - SLICE0)
            elif g < SLICE0 + 10:
                h = (g - SLICE0 - 2) // 2
                (outputs if (g - SLICE0) % 2 else scores)(h)
            else:
                late(g)
            dve.drain().then_inc(slice_read, 1)
            dve.wait_ge(slice_read, g - SLICE0 + 1)

        slice_dve(SLICE0)
        for u in range(SLICE0 + 1, Z_N):
            dve.wait_ge(w_used, 4 * u + 8)
            tt(halves(zT[:, u, :]), pair(2 * (u % 2)), halves(rs1[:]), mult).then_inc(z_free, 1)
            slice_dve(u)
        dve.wait_ge(z_free, Z_N + 2)
        slice_dve(LAST_SLICE)
        barrier(dve, 1)

        for name, credit in (("b_o", 2), ("b_pt", 1), ("b_turn", 4), ("b_sc_free", 2), ("b_o_free", 2)):
            dve.nop().then_inc(s(name), credit)
        for kv in range(2):
            for q in range(2):
                nc.vector.tensor_copy(kd[64 * q:64 * q + 64, kv, :], zT[64 * kv:64 * kv + 64, Z_BK, :])
        link(nc.vector.memset(qb_[:], 0.0))
        for kv in range(2):
            for q in range(2):
                o = nc.vector.tensor_copy(
                    qb_[64 * kv:64 * kv + 64, :, :].rearrange("p b (u q) -> p q u b", q=2)[:, q, 4 * kv:4 * kv + 4, :],
                    zT[64 * q:64 * q + 64, Z_BQ + 4 * kv:Z_BQ + 4 * kv + 4, T:N])
        o.then_inc(s("b_q8"), 1)
        dve.wait_ge(s("b_vk_a"), 1)
        dve.wait_ge(s("b_q8"), 1)
        dve.drain().then_inc(s("b_vk"), 1)
        dve.wait_ge(s("b_in"), 64)
        dve.wait_ge(s("b_s8t"), 1)
        link(nc.vector.tensor_copy(s_s[:, P:P + 1], bsink[:]))
        link(nc.vector.tensor_tensor_reduce(out=s_s[:, 0:P], in0=ps[:, 3, 0:P], in1=bias_s[:], scale=0.125,
                                            scalar=s_s[:, P:P + 1], op0=add, op1=mx, accum_out=mxn[:, 0, 0, 0:1]))
        ts(mxn[:, 0, 0, 1:2], mxn[:, 0, 0, 0:1], -1.0, None, mult).then_inc(s("b_max8"), 1)
        dve.wait_ge(s("b_exp8"), 1)
        link(nc.vector.reciprocal(mxn[:, 0, 0, 3:4], mxn[:, 0, 0, 2:3]))
        ts(s_s[:, 0:P], s_s[:, 0:P], mxn[:, 0, 0, 3:4], None, mult).then_inc(s("b_p8"), 1)
        dve.wait_ge(s("b_o8"), 1)
        for kv in range(2):
            for q in range(2):
                o = nc.vector.tensor_copy(
                    zT[64 * q:64 * q + 64, Z_BQ + 4 * kv:Z_BQ + 4 * kv + 4, T:N],
                    ps[64 * kv:64 * kv + 64, 3, 0:P].rearrange("p (b u q) -> p q u b", q=2, u=8)[:, q, 4 * kv:4 * kv + 4, :])
        o.then_inc(s("b_o8_read"), 1)
        dve.wait_ge(s("b_o8_read"), 1)
        STEPS = 8 * 2
        for kv in range(2):
            with dve.Fori(0, 2) as it:
                first = it * 8 + 16 * kv
                mine = it * STEPS + 2 * STEPS * kv
                told = [0]

                def then(ins):
                    told[0] += 1
                    ins.then_inc(s("b_steps"), 1)
                    dve.wait_ge(s("b_steps"), mine + told[0])

                def score(n):
                    sl, lo = n // 4, 0 if n % 4 else P
                    u = it * 2 + (4 * kv + sl)
                    if n % 4 == 0:
                        nc.vector.tensor_copy(qst[:, sl, 0:T], zT[:, bass.ds(u + Z_BQ, 1), 0:T].rearrange("p a n -> p (a n)"))\
                            .then_inc(s("b_pair"), 1)
                        dve.wait_ge(bias_in[sl], it * 16 + (32 * kv + 16))
                    dve.wait_ge(s("b_turn"), first + (n + 1))
                    begun(dve)
                    then(nc.vector.tensor_copy(sx[:, n % 4, :, 256], sinkbc[:, bass.ds(u * 2, 2)]))
                    dve.wait_ge(s("b_qk"), first + (n + 1))
                    begun(dve)
                    for r in range(2):
                        ins = nc.vector.tensor_tensor_reduce(
                            out=sx[:, n % 4, r, lo:256], in0=ps[:, 4 - 2 * r + n % 2, lo:256],
                            in1=bst[:, sl, r, lo:256], scale=0.125, scalar=sx[:, n % 4, r, 256:257], op0=add, op1=mx,
                            accum_out=mxn[:, n % 4, r, 0:1])
                    ins.then_inc(s("b_sc_free"), 1)
                    dve.wait_ge(s("b_sc_free"), first + (n + 3))
                    ts(mxn[:, n % 4, :, 1], mxn[:, n % 4, :, 0], -1.0, None, mult).then_inc(s("b_max"), 1)

                def scale(n):
                    lo = 0 if n % 4 else P
                    dve.wait_ge(s("b_exp"), first + (n + 1))
                    then(nc.vector.reciprocal(mxn[:, n % 4, :, 3], mxn[:, n % 4, :, 2]))
                    for r in range(2):
                        ins = ts(sx[:, n % 4, r, lo:256], sx[:, n % 4, r, lo:256], mxn[:, n % 4, r, 3:4], None, mult)
                    ins.then_inc(s("b_prob"), 1)

                def read_o(n):
                    u = it * 2 + (4 * kv + n // 4)
                    dve.wait_ge(s("b_o"), first + (n + 3))
                    begun(dve)
                    nc.vector.tensor_copy(zT[:, bass.ds(u + Z_BQ, 1), (n % 4) * P:(n % 4 + 1) * P].rearrange("p a n -> p (a n)"),
                                          ps[:, 7 * (n % 2), 0:P]).then_inc(s("b_o_free"), 1)

                for n in range(8 + 4):
                    if n < 8:
                        score(n)
                    if 1 <= n < 9:
                        scale(n - 1)
                    if n >= 4:
                        read_o(n - 4)
                assert told[0] == STEPS
        dve.wait_ge(s("b_o_free"), 34)
        dve.drain().then_inc(s("b_ended"), 2)
        barrier(dve, 2)

        dve.wait_ge(s("a_wt"), 1)
        nc.vector.tensor_copy(wst[:].rearrange("p g n -> p (g n)"), ps[:, 0, :]).then_inc(s("a_wt_read"), 1)
        for g in range(4):
            dve.wait_ge(s("a_vt"), g + 1)
            nc.vector.tensor_copy(vnt[:, :, g, :], ps[:, (1, 2, 3, 1)[g], :].rearrange("p (j n) -> p j n", j=NB))\
                .then_inc(s("a_vt_read"), 1)
        dve.wait_ge(s("a_in"), 48)
        dve.wait_ge(s("a_v8"), 1)
        for g in range(4):
            link(ts(asmp[:, g, :], zT[:, Z_AV + g, T:N], w00[:, g:g + 1], bbc[:, g, 0:1], mult, add))
        link(tt(zT[:, Z_AU:Z_AU + 4, T:N], zT[:, Z_AU:Z_AU + 4, T:N], asmp[:], mult))
        for g in range(4):
            dve.wait_ge(s("a_mix"), g + 1)
            link(tt(amix[:].rearrange("p (j n) -> p j n", j=NB), ps[:, 4 + g, :].rearrange("p (j n) -> p j n", j=NB),
                    bbc[:, g:g + 1, :].broadcast_to([P, NB, P]), add))
            link(tt(zT[:, Z_AU + g, 0:T], zT[:, Z_AU + g, 0:T], amix[:], mult))
        barrier(dve, 3)

        for i, c in enumerate(K_ORDER):
            dve.wait_ge(mix_hi, i + 1)
            tt(act_lo[:, c, :], zT[:, MIX_TILES[c], :], act_hi[:, c, :].bitcast(F32), sub).then_inc(mix_lo, 1)

        dve.wait_ge(spilled, 32)
        dve.wait_ge(mix_lo, KC)
        link(nc.vector.memset(ssum[:], 0.0))

        def one(ap):
            return ap.rearrange("p a n -> p (a n)")

        def residual(i, u):
            n = i * 2 + (u - U_OUT)
            tile = bass.ds(n, 1)
            begun(dve)
            nc.vector.tensor_copy(gain2[:, u:u + 1], vecs[:, bass.ds(n + G2, 1)])
            dve.wait_ge(w_used, i * 8 + (4 * u + 8))
            x2 = xT[:, tile, :].rearrange("p a (h n) -> p (a h) n", h=2)
            tt(x2, pair(2 * u), x2, add).then_inc(z_free, 1)
            dve.wait_ge(z_free, n + (Z_N + 3))
            dve.wait_ge(s("o_sq"), n + 1)
            tt(ssum[:], ssum[:], ssq[:, u, :], add).then_inc(s("o_sum"), 1)
            dve.wait_ge(s("h2_hi"), n + 1)
            stt(out=one(h2_lo[:, tile, :]), in0=one(xT[:, tile, :]), scalar=gain2[:, u:u + 1],
                in1=one(h2_hi[:, tile, :]).bitcast(F32), op0=mult, op1=sub).then_inc(s("h2_lo"), 1)
            dve.wait_ge(s("h2_lo"), n + 1)

        with dve.Fori(U_OUT // 2, U_FFN // 2) as i:
            for u in range(2):
                residual(i, u)
        dve.wait_ge(w_used, USED_OUT)
        link(nc.vector.memset(zg[:, 0:2], 0.0))
        link(nc.vector.memset(za[:, 0:2], 0.0))
        dve.wait_ge(s("o_sum_mm"), 1)
        ts(halves(rs2[:]), pair(4), 1.0 / D, EPS, mult, add).then_inc(s("o_mean"), 1)
        dve.nop().then_inc(s("d_add"), 2)
        dve.wait_ge(s("o_root"), 1)
        link(nc.vector.reciprocal(rs2[:], rs2[:]))

        def ffn_group_dve(u0, n0, d0, base, tail, with_down):
            told = [0]

            def then(ins):
                told[0] += 1
                ins.then_inc(s("f_steps"), 1)
                dve.wait_ge(s("f_steps"), base + told[0])

            def read(n, half, unit, j):
                z, name, bank = ((zg, "f_zg", 0), (za, "f_za", 2))[half]
                dve.wait_ge(w_used, u0 * 4 + (4 * unit + 8))
                tt(halves(z[:, 2:]), pair(bank), halves(rs2[:]), mult).then_inc(s(name), 1)
                dve.wait_ge(s(name), n + 1)
                begun(dve)
                nc.vector.tensor_copy(ztail[:, bass.ds(tail(half, j), 1), :].rearrange("p a n -> p (a n)"), z[:, T:])\
                    .then_inc(z_free, 1)

            def conv(n, half, j):
                z, c_, name = ((zg, cg, "f_tg"), (za, ca, "f_ta"))[half]
                par = cpar[:, half, j, :]
                dve.wait_ge(s(name), n + 1)
                old = par[:, 0:16].rearrange("p (b t) -> p t b", t=2)
                for tap, from_col in ((1, 1), (0, 0)):
                    stt(out=c_[:, T:N], in0=old[:, tap, :], scalar=par[:, 16 + tap:17 + tap], in1=c_[:, T:N],
                        op0=mult, op1=add)
                    ins = stt(out=c_[:, 0:T], in0=z[:, from_col:from_col + T], scalar=par[:, 16 + tap:17 + tap],
                              in1=c_[:, 0:T], op0=mult, op1=add)
                    if tap:
                        then(ins)
                if half:
                    then(ins)
                else:
                    ins.then_inc(s("f_cg"), 1)

            def gate(n, j):
                dve.wait_ge(s("f_silu"), n + 1)
                if isinstance(n, int) and n == 0:
                    pass
                tt(gm[:], cg[:], ca[:], mult).then_inc(s("f_m"), 1)
                dve.wait_ge(s("f_m"), n + 1)

            def lo(n, j):
                dve.wait_ge(s("g_hi"), n + 1)
                tt(g_lo[:, j, :], gm[:], g_hi[:, j, :].bitcast(F32), sub).then_inc(s("g_lo"), 1)

            def down(m, k):
                e = 4 * m + k
                dve.wait_ge(w_used, u0 * 4 + (4 * (2 + m) + k + 5))
                x2 = halves(xT[:, e, :])
                tt(x2, pair(4 + 2 * (k % 2)), x2, add).then_inc(s("d_add"), 1)

            for j in range(GC):
                g = 2 * j + (GC if with_down and j else 0)
                n = n0 + j
                read(n, 0, g, j)
                read(n, 1, g + 1, j)
                conv(n, 0, j)
                if with_down and j == 0:
                    down(0, 0)
                conv(n, 1, j)
                if with_down and j == 0:
                    down(0, 1)
                gate(n, j)
                if with_down and j == 0:
                    for e in range(2, 16):
                        down(e // 4, e % 4)
                lo(n, j)
            return told[0]

        steps = ffn_group_dve(U_FFN, 0, None, 0, lambda half, j: FC * half + j, False)
        with dve.Fori(1, NG) as i:
            assert ffn_group_dve(i * 12 + (U_FFN + U_GRP - 12), i * GC, i * 16 - 16, i * steps,
                                 lambda half, j: i * GC + (FC * half + j), True) == steps
        for e in range(16):
            dve.wait_ge(w_used, 4 * (U_ALL - GC) + e + 5)
            x2 = halves(xT[:, e, :])
            tt(x2, pair(4 + 2 * (e % 2)), x2, add).then_inc(s("d_add"), 1)
            if e:
                read_y(dve, e - 1)
        read_y(dve, 15)

    @block.gpsimd
    def _(pool):
        link = Chain(pool, chain_p)
        link(nc.gpsimd.memset(ident[:], 0.0))
        link(nc.gpsimd.affine_select(out=ident[:], in_=ident[:], compare_op=ALU.not_equal, fill=1.0, base=0,
                                     pattern=[[-1, P]], channel_multiplier=1))
        nc.gpsimd.memset(ones[:], 1.0).then_inc(const_made, 1)
        pool.wait_ge(const_made, 1)
        nc.gpsimd.memset(whi[:].rearrange("p q c n -> p (q c n)").bitcast(F32), 0.0).then_inc(ring_zero, 1)
        nc.gpsimd.memset(wlo[:].rearrange("p q c n -> p (q c n)").bitcast(F32), 0.0).then_inc(ring_zero, 1)
        link(nc.gpsimd.memset(pairones[:], 0.0))
        for q in range(2):
            link(nc.gpsimd.memset(pairones[64 * q:64 * q + 64, 64 * q:64 * q + 64], 1.0))
        link(nc.gpsimd.memset(causal[:], 0.0))
        link(nc.gpsimd.affine_select(out=causal[:], in_=causal[:], compare_op=ALU.is_ge, fill=NEG, base=0,
                                     pattern=[[1, P]], channel_multiplier=-1))
        for h in range(4):
            link(nc.gpsimd.tensor_copy(sel[:, h, :], ident[0:4, h:h + 1].broadcast_to([4, P])))
        pool.wait_ge(wg_hi, 1)
        pool.wait_ge(ring_zero, 2)
        gates = wg_raw[:].rearrange("p (c k) n -> p k c n", k=4)
        for rows in (0, 32):
            from_col = rows // 8
            g = nc.gpsimd.tensor_tensor(wlo[:, :, :, rows:rows + 4], gates[:, :, :, from_col:from_col + 4],
                                        whi[:, :, :, rows:rows + 4].bitcast(F32), ALU.subtract)
        g.then_inc(wg_lo, 1)

        def split_pairs(first, last):
            with pool.Fori(first, last) as i:
                for u in range(2):
                    for k in range(4):
                        pool.wait_ge(w_hi, i * 8 + (4 * u + k + 1))
                        nc.gpsimd.tensor_tensor(wlo[:, k, :, :], rawq(k, u), whi[:, k, :, :].bitcast(F32),
                                                ALU.subtract).then_inc(w_lo, 1)

        split_pairs(0, Z_N // 2)
        barrier(pool, 1)
        barrier(pool, 2)
        pool.wait_ge(s("a_wt_read"), 1)
        nc.gpsimd.affine_select(out=wst[:], in_=wst[:], compare_op=ALU.is_ge, fill=0.0, base=0,
                                pattern=[[0, 4], [1, P]], channel_multiplier=-1).then_inc(s("a_wst"), 1)
        pool.wait_ge(s("a_wst"), 1)
        barrier(pool, 3)
        split_pairs(Z_N // 2, U_ALL // 2)

    @block.sync
    def _(sp):
        for i in range(NB):
            sp.dma_start(xtok[:, i, :], io["x_prompt"][0, i * P:(i + 1) * P, :]).then_inc(x_in[i], 16)
        sp.dma_start(xtok[0:S, 4, :], io["x_sample"].rearrange("b t d -> (b t) d")).then_inc(x_in[4], 16)

        def load_pair(sources, split, down=False):
            for u in range(2):
                if split is not None:
                    sp.wait_ge(w_lo, split + 4 * u)
                sp.dma_start(unit_dst(u, down), sources[u]).then_inc(raw_in[u], 16)

        load_pair([cols_of(w_in, COL_C), cols_of(w_in, COL_C + P)], None)
        sp.wait_ge(x_ev_a, 8)
        sp.wait_ge(x_ev_v, 9)
        sp.dma_start(spill, xT[:].rearrange("p c n -> p (c n)")).then_inc(spilled, 16)
        for a, b, col, unit in ((1, 6, COL_C, Z_CQ), (6, 10, COL_A, Z_AU), (10, 11, COL_BK, Z_BK), (11, 15, COL_BQ, Z_BQ)):
            with sp.Fori(a, b) as i:
                load_pair([cols_of(w_in, i * (2 * P) + (col + (u - unit) * P)) for u in range(2)], i * 8 - 4)
        load_pair([cols_of(w_out, 0), cols_of(w_out, P)], 4 * Z_N - 4)
        sp.wait_ge(stage, 4)
        for u in range(8):
            if u >= 2:
                sp.wait_ge(s("b_sc_free"), 4 * u - 2)
            sp.dma_start(bst[:, u % 2, :, :], bass.AP(tensor=bias_rows.tensor, offset=P - 1 + 2 * u * BIAS_PITCH,
                                                       ap=[[383, P], [BIAS_PITCH, 2], [1, 256]])).then_inc(bias_in[u % 2], 16)
        sp.wait_ge(stage, 8)
        sp.dma_start(xT[:].rearrange("p c n -> p (c n)"), spill).then_inc(spilled, 16)
        with sp.Fori(U_OUT // 2 + 1, U_FFN // 2) as i:
            load_pair([cols_of(w_out, i * (2 * P) + (u - U_OUT) * P) for u in range(2)], i * 8 - 4)

        def params_of(name, col):
            flat = {"state_ffn_conv": "l b j f -> (l b j) f", "ffn_conv_w": "l j f -> (l j) f", "ffn_conv_b": "l f -> l f"}
            return io[name].rearrange(flat[name]).rearrange("r (h f) -> r h f", h=2)[:, :, bass.ds(col, GC * P)]

        def load_group(grp, col, split, with_down):
            def up(j):
                return [cols_of(w_up, col + j * P), cols_of(w_up, col + (FF + j * P))]

            if not with_down:
                sp.wait_ge(w_used, USED_OUT)
            else:
                sp.wait_ge(s("par_turn"), grp)
            for rows, name in (((0, 16), "state_ffn_conv"), ((16, 19), "ffn_conv_w"), ((19, 20), "ffn_conv_b")):
                sp.dma_start(par_rows[rows[0]:rows[1], :, :], params_of(name, col)).then_inc(s("par_in"), 16)
            load_pair(up(0), split)
            if with_down:
                load_pair([down_of(col - GC * P, m) for m in (0, 1)], split + 8, True)
                load_pair([down_of(col - GC * P, m) for m in (2, 3)], split + 16, True)
            for j in range(1, GC):
                load_pair(up(j), split + 8 * (j + (2 if with_down else 0)))

        load_group(0, 0, 4 * U_FFN - 4, False)
        with sp.Fori(1, NG) as i:
            load_group(i, i * (GC * P), i * 48 + 4 * (U_FFN + U_GRP - 12) - 4, True)
        for m in (0, 2):
            load_pair([down_of((NG - 1) * GC * P, mm) for mm in (m, m + 1)],
                      4 * (U_ALL - GC + m) - 4, True)
        sp.wait_ge(s("t_read"), FC // 2)
        store(sp, io["ffn_conv_prompt"][0, 0], trow[0:2, :])
        store(sp, io["ffn_conv_sample"][0, :, 1, :], trow[2:2 + S, :])
        for half in range(2):
            sp.wait_ge(s("y_read"), 8 * half + 8)
            store(sp, io["y_prompt"][0, :, half * 1024:(half + 1) * 1024].rearrange("(j p) d -> p j d", p=P),
                  ytok[:, :, half * 1024:(half + 1) * 1024])
        sp.wait_ge(s("y8_read"), 1)
        store(sp, io["y_sample"].rearrange("b t d -> (b t) d"), ytok8[:])
        sp.wait_ge(out_done, out_count[0])

    ctx.close()


_INS = ["x_prompt", "x_sample", "cache_swa_k", "cache_swa_v", "state_mlstm_C", "state_mlstm_n", "state_mlstm_m",
        "state_ffn_conv", "rel_bias", "norm1", "w_in", "a_v_gain", "a_spatial_w", "a_spatial_b", "b_q_gain",
        "b_k_gain", "b_sinks", "c_gate_bias", "c_h_gain", "w_out", "norm2", "w_up", "ffn_conv_w", "ffn_conv_b",
        "w_down"]
_OUTS = [("y_prompt", (1, T, D)), ("y_sample", (S, 1, D)),
         ("k_prompt", (1, 1, WINDOW, 2, 64)), ("v_prompt", (1, 1, WINDOW, 2, 64)),
         ("k_sample", (1, S, 1, 2, 64)), ("v_sample", (1, S, 1, 2, 64)),
         ("C_prompt", (1, 1, 4, 64, 128)), ("n_prompt", (1, 1, 4, 64)), ("m_prompt", (1, 1, 4)),
         ("C_sample", (1, S, 4, 64, 128)), ("n_sample", (1, S, 4, 64)), ("m_sample", (1, S, 4)),
         ("ffn_conv_prompt", (1, 1, 2, F2)), ("ffn_conv_sample", (1, S, 2, F2)), ("chunk_v", (1, S, 1, 512))]


def kernel(**inputs):
    import concourse.bacc as bacc
    from concourse.bass_utils import run_bass_kernel_spmd

    nc = bacc.Bacc("TRN2", target_bir_lowering=False, num_devices=1)
    arrays = {f"in_{n}": np.ascontiguousarray(inputs[n]) for n in _INS}
    arrays["in_bucket_table"] = bucket_table()
    io = {n[3:]: nc.dram_tensor(n, a.shape, F32, kind="ExternalInput").ap() for n, a in arrays.items()}
    for n in ("w_in", "w_out", "w_up", "w_down"):
        io[n] = io[n][0]
    for n, shape in _OUTS:
        io[n] = nc.dram_tensor(f"out_{n}", shape, F32, kind="ExternalOutput").ap()
    hybrid_layer(nc, io)
    r = run_bass_kernel_spmd(nc, [arrays], core_ids=[0])
    return tuple(r.results[0][f"out_{n}"] for n, _ in _OUTS)
```

```python
from contextlib import ExitStack

import numpy as np

import concourse.bass as bass
from concourse import mybir

F32 = mybir.dt.float32
F32R = mybir.dt.float32r
ACT = mybir.ActivationFunctionType
ALU = mybir.AluOpType

P = 128
D = 2048
KC = D // P
T = 512
S = 8
N = T + S
NH = N // 2
NB = T // P
EPS = 1e-6
NEG = -1e30
IN_W = 3848
FF = 5632
F2 = 2 * FF
FC = FF // P
GC = 4
NG = FC // GC
WINDOW = 128
NBUCKET = 32

Z_CQ, Z_CK, Z_CV, Z_CO, Z_AV, Z_BK, Z_BV, Z_BQ, Z_AU, Z_N = 0, 2, 4, 8, 12, 16, 17, 18, 26, 30
COL_C, COL_AV, COL_BK, COL_BQ, COL_AU, COL_G = 2304, 512, 2048, 1024, 0, 3840
SLICE0 = 11
K_ORDER = [4 * c + k for k in range(4) for c in range(4)]
MIX_TILES = [Z_AU + i for i in range(4)] + [Z_BQ + i for i in range(8)] + [Z_CO + i for i in range(4)]

U_OUT = Z_N
U_FFN = U_OUT + KC
U_GRP = 2 * GC
U_ALL = U_FFN + NG * (U_GRP + GC)


def bucket_of(dist):
    n = max(dist, 0)
    if n < NBUCKET // 2:
        return n
    large = NBUCKET // 2 + int(np.float32(np.log(np.float32(n) / np.float32(16))) / np.log(8.0) * 16)
    return min(large, NBUCKET - 1)


def bucket_table():
    e = np.zeros((NBUCKET + 1, 384), np.float32)
    for w in range(384):
        dist = 255 - w
        e[bucket_of(dist) if 0 <= dist < WINDOW else NBUCKET, w] = 1.0
    return e


def hybrid_layer(nc, io):
    ctx = ExitStack()
    base = (nc.sbuf_base + 31) // 32 * 32
    limit = nc.sbuf_usable_end // 32 * 32

    class Region:

        def __init__(self, start, size):
            self.start, self.end, self.at = start, start + size, start

        def again(self):
            return Region(self.start, self.end - self.start)

        def take(self, name, shape, dt=F32):
            size = int(np.prod(shape[1:])) * 4
            size = (size + 31) // 32 * 32
            assert self.at + size <= self.end, (name, self.at + size - self.end)
            t = nc.alloc_sbuf_tensor_at(name, shape, dt, offset=self.at)
            self.at += size
            return t

    ACTB = 2 * KC * N * 4
    XB = KC * N * 4
    keep = Region(base, limit - base - 2 * ACTB - XB)
    r_act = Region(keep.end, ACTB)
    r_z = Region(r_act.end, ACTB)
    r_x = Region(r_z.end, XB)

    ident = keep.take("ident", [P, P])
    ones = keep.take("ones", [P, P])
    pairones = keep.take("pairones", [P, P])
    causal = keep.take("causal", [P, P])
    vrow = keep.take("vrow", [48, P])
    vecs = keep.take("vecs", [P, 48])
    G1, G2, GAV, GCH, GBQ, GBK = 0, 16, 32, 36, 40, 41
    sel = keep.take("sel", [4, 4, P])
    rs1 = keep.take("rs1", [P, N])
    r_rs2 = Region(keep.at, N * 4)
    rs2 = keep.take("rs2", [P, N])
    ws = r_rs2.again().take("ws", [P, 4, P])
    wst = r_rs2.again().take("wst", [P, 4, P])
    small = keep.take("small", [P, 64])
    gbi = keep.take("gbi", [4, 1])
    gbf = keep.take("gbf", [36, 1])
    gain2 = keep.take("gain2", [P, 2])
    band = keep.take("band", [P, 7])
    raw = keep.take("raw", [P, 2, KC * P])
    whi = keep.take("whi", [P, 4, 4, P], F32R)
    wlo = keep.take("wlo", [P, 4, 4, P], F32R)

    act_hi = r_act.take("act_hi", [P, KC, N], F32R)
    act_lo = r_act.take("act_lo", [P, KC, N], F32R)

    z0 = r_z.again()
    xtok = z0.take("xtok", [P, 5, D])
    xjunk = z0.take("xjunk", [P, D])
    wg_raw = z0.take("wg_raw", [P, KC, S])
    rel33 = z0.take("rel33", [33, 16])
    hot = z0.take("hot", [33, 384])
    brow = z0.take("brow", [16, 384])
    z1 = r_z.again()
    zT = z1.take("zT", [P, Z_N, N])
    z2 = r_z.again()
    h2_hi = z2.take("h2_hi", [P, KC, N], F32R)
    h2_lo = z2.take("h2_lo", [P, KC, N], F32R)
    xT = r_x.take("xT", [P, KC, N])

    ctx.enter_context(nc.allow_non_contiguous_dma(reason="small states, a few hundred elements"))
    ps = ctx.enter_context(nc.psum_tensor("ps", [P, 8, 512], F32))

    spill = nc.dram_tensor("x_spill", [P, KC * N], F32, kind="Internal").ap()
    BIAS_PITCH = (P + 1) * 384
    bias_rows = nc.dram_tensor("bias_rows", [16, P + 1, 384], F32, kind="Internal").ap()

    def sem(name):
        return ctx.enter_context(nc.semaphore(name))

    out_done = sem("out_done")

    raw_in = [sem("raw_in0"), sem("raw_in1")]
    w_hi = sem("w_hi")
    w_lo = sem("w_lo")
    w_used = sem("w_used")
    z_free = sem("z_free")
    stage = sem("stage")
    chain_v, chain_a, chain_p = sem("chain_v"), sem("chain_a"), sem("chain_p")

    x_in = [sem(f"x_in{i}") for i in range(5)]
    vec_in, misc_in, wg_in = sem("vec_in"), sem("misc_in"), sem("wg_in")
    const_made = sem("const_made")
    ring_zero = sem("ring_zero")
    x_tr, x_ev_a, x_ev_v = sem("x_tr"), sem("x_ev_a"), sem("x_ev_v")
    vec_tr, vec_ev, rs_diag, rs_mm, rs_ready = (sem(n) for n in ("vec_tr", "vec_ev", "rs_diag", "rs_mm", "rs_ready"))
    var_v, var_a = sem("var_v"), sem("var_a")
    h_hi, h_lo = sem("h_hi"), sem("h_lo")
    wg_hi, wg_lo = sem("wg_hi"), sem("wg_lo")
    spilled = sem("spilled")

    def rawq(k, s):
        return raw[:, s, :].rearrange("p (c k n) -> p c k n", c=4, k=4)[:, :, k, :]

    def pair(b):
        return ps[:, b:b + 2, 0:NH]

    def halves(ap):
        return ap.rearrange("p (h n) -> p h n", h=2)

    w_in, w_out, w_up, w_down = io["w_in"], io["w_out"], io["w_up"], io["w_down"]

    def cols_of(w, col):
        return w[:, bass.ds(col, P)].rearrange("(c p) n -> p c n", p=P)

    def down_of(row, m):
        return w_down[bass.ds(row, GC * P), 512 * m:512 * m + 512].rearrange("(c p) n -> p c n", p=P)

    def unit_dst(u, down):
        if down:
            return raw[:, u, :].rearrange("p (c n) -> p c n", c=GC)
        return raw[:, u, :].rearrange("p (c n) -> p c n", c=KC)

    r_ssq = Region(keep.at, 2 * N * 4)
    ssq = keep.take("ssq", [P, 2, N])
    bbc = r_ssq.again().take("bbc", [P, 4, P])
    v8 = r_ssq.take("v8", [8, 512])
    k8 = r_ssq.take("k8", [8, 256])
    ssum = rs1

    cX = r_x.again()
    gi = cX.take("gi", [4, 8, N])
    gf = r_x.again().take("gf", [36, 4, N])
    cH = Region(r_x.start, 6 * N * 4)
    dmat = cH.take("dmat", [P, 1280])
    pmat = cH.take("pmat", [P, 1280])
    tmpm = cH.take("tmpm", [P, T])
    vtok = cX.take("vtok", [P, NB, 4, P + 1])
    kw = cX.take("kw", [P, NB, 4, 64])
    qab = cX.take("qab", [P, T])
    den = cX.take("den", [P, T])
    cout = z1.take("cout", [P, 2, P + 1])
    ct = z1.take("ct", [P, 8, 4])
    cs = z1.take("cs", [P, 2, 16])
    emts = z1.take("emts", [P, 32])
    kws = z1.take("kws", [P, 2, S])
    ns = z1.take("ns", [P, 2 * S])
    nq = z1.take("nq", [P, 2, S])
    hs = z1.take("hs", [P, 3, 32])
    m0 = z1.take("m0", [4, S])
    gs = z1.take("gs", [4, 2, S])
    dsq = z1.take("dsq", [P, 18, S])
    dvar = z1.take("dvar", [P, 18, S])
    w00 = z1.take("w00", [P, 4])
    asmp = z1.take("asmp", [P, 4, S])
    nX = r_x.again()
    nsq = nX.take("nsq", [P, 4, T])
    nvar = nX.take("nvar", [P, 2, T])
    head_rows = nX.take("head_rows", [4, 2, T])
    cst = nX.take("cst", [P, 2 * S, P])
    nsqa = Region(nX.at, 8192).take("nsqa", [P, 4, T])
    vnt = Region(nX.at, 8192).take("vnt", [P, NB, 4, P])
    vm = nX.take("vm", [8, 2, S * P])
    kc_ = Region(r_x.start + 4096, 4096).take("kc_", [P, S, P])
    vc_ = Region(r_x.start + 12288, 4096).take("vc_", [P, S, P])
    nM = r_x.again()
    amix = nM.take("amix", [P, T])
    vn8 = nM.take("vn8", [8, 512])
    bA = r_act.again()
    kd = bA.take("kd", [P, 2, N])
    qst = bA.take("qst", [P, 2, N])
    vtb = bA.take("vtb", [P, NB, P])
    ktb = bA.take("ktb", [P, P])
    sx = bA.take("sx", [P, 4, 2, 257])
    pt = bA.take("pt", [P, 2, 512])
    bst = bA.take("bst", [P, 2, 2, 256])
    sinkbc = bA.take("sinkbc", [P, 16])
    mxn = bA.take("mxn", [P, 4, 2, 4])
    bsink = bA.take("bsink", [P, 1])
    kv8 = bA.take("kv8", [8, 2, P])
    kct = bA.take("kct", [P, S, P])
    qb_ = bA.take("qb_", [P, S, 16])
    s_t = bA.take("s_t", [P, P])
    s_s = bA.take("s_s", [P, 129])
    bias_s = bA.take("bias_s", [P, P])
    p_t = bA.take("p_t", [P, P])
    fA = r_act.again()
    g_hi = fA.take("g_hi", [P, GC, N], F32R)
    g_lo = fA.take("g_lo", [P, GC, N], F32R)
    zg = fA.take("zg", [P, N + 2])
    za = fA.take("za", [P, N + 2])
    cg = fA.take("cg", [P, N])
    ca = fA.take("ca", [P, N])
    gm = fA.take("gm", [P, N])
    ztail = fA.take("ztail", [P, 2 * FC, S + 2])
    cpar = fA.take("cpar", [P, 2, GC, 20])
    par_rows = Region(fA.at, 2 * GC * P * 4).take("par_rows", [20, 2, GC * P])
    ytok = fA.take("ytok", [P, NB, D])
    fZ = r_z.again()
    trow = fZ.take("trow", [S + 2, F2])
    ytok8 = fZ.take("ytok8", [S, D])

    sems = {}

    def s(name):
        if name not in sems:
            sems[name] = sem(name)
        return sems[name]

    bias_in = [sem("bias_in0"), sem("bias_in1")]
    begins = sem("begins")
    mix_hi, mix_lo = sem("mix_hi"), sem("mix_lo")
    slice_mm = sem("slice_mm")
    slice_read = sem("slice_read")
    TURN_BANK = (6, 1)
    DIAG = [0, 512, 896, 1152]
    SCORE_AT = [(5, 0), (6, 0), (7, 0), (6, 384)]
    USED_IN = 4 + 4 * Z_N
    USED_OUT = 4 + 4 * U_FFN

    class Chain:

        def __init__(self, eng, semaphore):
            self.eng, self.sem, self.n = eng, semaphore, 0

        def __call__(self, ins):
            self.n += 1
            ins.then_inc(self.sem, 1)
            self.eng.wait_ge(self.sem, self.n)

    out_count = [0]

    def store(eng, dst, src):
        out_count[0] += 16
        eng.dma_start(dst, src).then_inc(out_done, 16)

    def barrier(eng, k):
        eng.drain().then_inc(stage, 1)
        eng.wait_ge(stage, 4 * k)

    def begun(eng):
        eng.sem_inc(begins)

    def heads_of(ap, q):
        return ap.rearrange("p (k q b) -> p q k b", q=2, b=S)[:, q]

    LAST_SLICE = 29
    NORM_SLICES = {24: (0, 1), 25: (2, 3), 26: (4, 5), 27: (6,), 28: (7, 8)}

    def b_tile(k):
        return (Z_BQ + k - 1, GBQ) if k else (Z_BK, GBK)

    def squares_act(act, g):
        for k in NORM_SLICES.get(g, ()):
            act.wait_ge(z_free, b_tile(k)[0] + 3)
            if k >= 2:
                act.wait_ge(s("norm_var"), k - 1)
            nc.scalar.activation(nsq[:, k % 2, :], zT[:, b_tile(k)[0], 0:T], ACT.Square).then_inc(s("norm_sq"), 1)

    def roots_act(act, g):
        for k in NORM_SLICES.get(g, ()):
            act.wait_ge(s("norm_var"), k + 1)
            nc.scalar.activation(nvar[:, k % 2, :], nvar[:, k % 2, :], ACT.Sqrt).then_inc(s("norm_root"), 1)

    def norms_pe(pe, g):
        for k in NORM_SLICES[g]:
            pe.wait_ge(s("norm_sq"), k + 1)
            mm = nc.tensor.matmul(ps[:, 6 + k % 2, :], pairones[:], nsq[:, k % 2, :], start=True, stop=True)
        return mm

    def norms_dve(dve, g, link):
        for k in NORM_SLICES.get(g, ()):
            if k >= 2:
                dve.wait_ge(s("norm_out"), k - 1)
            nc.vector.tensor_scalar(nvar[:, k % 2, :], ps[:, 6 + k % 2, :], 1.0 / 64, EPS,
                                    ALU.mult, ALU.add).then_inc(s("norm_var"), 1)
        for k in NORM_SLICES.get(g, ()):
            tile, gain = b_tile(k)
            dve.wait_ge(s("norm_root"), k + 1)
            link(nc.vector.reciprocal(nvar[:, k % 2, :], nvar[:, k % 2, :]))
            nc.vector.scalar_tensor_tensor(out=zT[:, tile, 0:T], in0=zT[:, tile, 0:T], scalar=vecs[:, gain:gain + 1],
                                           in1=nvar[:, k % 2, :], op0=ALU.mult, op1=ALU.mult)\
                .then_inc(s("norm_out"), 1)
            dve.wait_ge(s("norm_out"), k + 1)

    block = ctx.enter_context(nc.Block())

    @block.tensor
    def _(pe):
        def unit_mm(q0, bank, before=None):
            for k in range(4):
                pe.wait_ge(w_lo, q0 + (k + 1))
                if before is not None:
                    before(k)
                tile_mm(k, bank, whi, wlo)

        def tile_mm(k, bank, w_h, w_l, x_h=None, x_l=None):
            x_h, x_l = x_h or act_hi, x_l or act_lo
            for kind, (w, x) in enumerate(((w_h, x_h), (w_h, x_l), (w_l, x_h))):
                for c in range(4):
                    for h in range(2):
                        mm = nc.tensor.matmul(ps[:, bank + h, 0:NH], w[:, k, c, :],
                                              x[:, 4 * c + k, h * NH:(h + 1) * NH],
                                              start=(k == 0 and kind == 0 and c == 0),
                                              stop=(k == 3 and kind == 2 and c == 3))
            mm.then_inc(w_used, 1)

        pe.wait_ge(const_made, 1)
        for idx in range(16):
            i, cg_ = idx // 4, idx % 4
            if cg_ == 0:
                pe.wait_ge(x_in[i], 16)
            if idx >= 6:
                pe.wait_ge(x_ev_v if idx % 2 else x_ev_a, (idx - 6) // 2 + 1)
            for c in range(4):
                t = nc.tensor.transpose(ps[:, idx % 6, c * P:(c + 1) * P], xtok[:, i, (4 * cg_ + c) * P:(4 * cg_ + c + 1) * P],
                                        ident[:])
            t.then_inc(x_tr, 1)
        pe.wait_ge(x_in[4], 16)
        for c in range(KC):
            t = nc.tensor.transpose(ps[:, 6, c * S:(c + 1) * S], xtok[0:S, 4, c * P:(c + 1) * P], ident[0:S, 0:S])
        t.then_inc(x_tr, 1)
        pe.wait_ge(vec_in, 16 * 8)
        nc.tensor.transpose(ps[:, 7, 0:42], vrow[0:42, :], ident[0:42, 0:42]).then_inc(vec_tr, 1)
        pe.wait_ge(wg_lo, 1)
        for k in range(4):
            pe.wait_ge(h_lo, 4 * (k + 1))
            tile_mm(k, 4, whi, wlo)
        pe.wait_ge(s("rel_in"), 32)
        pe.wait_ge(s("rel_set"), 1)
        nc.tensor.matmul(ps[0:16, 6, 0:384], rel33[:], hot[:], start=True, stop=True).then_inc(s("rel_mm"), 1)

        pe.wait_ge(z_free, 1)
        unit_mm(0, 0)
        pe.wait_ge(rs_diag, 1)
        for i in range(NB):
            nc.tensor.matmul(ps[:, 7, i * P:(i + 1) * P], ones[:], xjunk[:, i * P:(i + 1) * P], start=True, stop=True)
        pe.wait_ge(s("rel_read"), 1)
        nc.tensor.matmul(ps[:, 6, 256:256 + S], ones[0:S, :], xjunk[0:S, 512:512 + S], start=True, stop=True)\
            .then_inc(rs_mm, 1)
        pe.wait_ge(z_free, 2)
        unit_mm(4, 2)
        with pe.Fori(1, (SLICE0 + 1) // 2) as i:
            for u in range(2):
                pe.wait_ge(z_free, i * 2 + (u + 1))
                unit_mm(i * 8 + 4 * u, 2 * u)

        def keys_and_values(g):
            for i in range(2):
                h = 2 * (g - SLICE0) + i
                for j in range(NB):
                    nc.tensor.transpose(ps[:, 4 + i, j * P:(j + 1) * P], zT[:, Z_CV + h, j * P:(j + 1) * P], ident[:])
            for j in range(NB):
                t = nc.tensor.transpose(ps[:, 6, j * P:(j + 1) * P], zT[:, Z_CK + g - SLICE0, j * P:(j + 1) * P], ident[:])
            if g > SLICE0:
                for h in range(4):
                    t = nc.tensor.transpose(ps[0:S, 7, h * P:(h + 1) * P], zT[:, Z_CV + h, T:N], ident[:])
                return t
            pe.wait_ge(s("c_rows"), 1)
            for j in range(NB):
                nc.tensor.transpose(ps[:, 7, 4 * j:4 * j + 4], gi[:, 2, j * P:(j + 1) * P], ident[0:4, 0:4])
                nc.tensor.transpose(ps[:, 7, 16 + 4 * j:20 + 4 * j], gi[:, 5, j * P:(j + 1) * P], ident[0:4, 0:4])
            for hp in range(2):
                for q in range(2):
                    nc.tensor.matmul(ps[64 * q:64 * q + 64, 7, 64 + 16 * hp:80 + 16 * hp], sel[:, 2 * hp + q, 0:64],
                                     gs[:].rearrange("p a b -> p (a b)"), start=True, stop=True)
            for h in range(4):
                t = nc.tensor.matmul(ps[:, 7, 128 + S * h:128 + S * (h + 1)], sel[:, h, :], gi[:, 7, T:N],
                                     start=True, stop=True)
            return t

        def scores(h):
            r, t2 = 64 * (h % 2), h // 2
            nc.tensor.matmul(ps[:, 4, :], sel[:, h, :], gi[:, 6, 0:T], start=True, stop=True)
            for j in range(NB):
                b, at = SCORE_AT[j]
                mm = nc.tensor.matmul(ps[:, b, at:at + T - j * P], zT[r:r + 64, Z_CK + t2, j * P:(j + 1) * P],
                                      zT[r:r + 64, Z_CQ + t2, j * P:T], start=True, stop=True)
            return mm

        def outputs(h):
            for j in range(NB):
                p_j = pmat[:, DIAG[j]:DIAG[j] + T - j * P]
                nc.tensor.matmul(ps[:, 5, j * P:T], vtok[:, j, h, 0:P], p_j, start=(j == 0), stop=(j == NB - 1))
                nc.tensor.matmul(ps[:, 6, j * P:T], ones[:], p_j, start=(j == 0), stop=(j == NB - 1))
            mm = nc.tensor.matmul(ps[:, 4, :], sel[:, h, :], gi[:, 7, 0:T], start=True, stop=True)
            if h == 0:
                for hp in range(2):
                    mm = nc.tensor.transpose(ps[0:S, 7, hp * P:(hp + 1) * P], kws[:, hp, :], ident[:])
            if h == 1:
                for hh in range(4):
                    r = 64 * (hh % 2)
                    for j in range(NB):
                        mm = nc.tensor.matmul(ps[r:r + 64, 7, 129 * (hh // 2):129 * (hh // 2) + 129], kw[:, j, hh, :],
                                              vtok[:, j, hh, :], start=(j == 0), stop=(j == NB - 1))
            return mm

        def outer(hp):
            pe.wait_ge(s("c_vm"), 2 * hp + 2)
            for q in range(2):
                for half in range(2):
                    mm = nc.tensor.matmul(ps[64 * q:64 * q + 64, 4 + half, :], k8[:, hp * P + 64 * q:hp * P + 64 * q + 64],
                                          vm[:, q, half * 512:half * 512 + 512], start=True, stop=True)
            return mm

        def memory_out():
            for h in range(4):
                r = 64 * (h % 2)
                for b in range(S):
                    nc.tensor.matmul(ps[:, 4 + h % 2, S * h + b:S * h + b + 1], cst[r:r + 64, 2 * b + h // 2, :],
                                     zT[r:r + 64, Z_CQ + h // 2, T + b:T + b + 1], start=True, stop=True)
                mm = nc.tensor.matmul(ps[:, 4 + h % 2, 64 + S * h:64 + S * (h + 1)], ones[r:r + 64, :],
                                      nq[r:r + 64, h // 2, :], start=True, stop=True)
            return mm

        def late(g):
            if g == 21:
                for b, squares in ((4, nsq), (5, nsqa)):
                    pe.wait_ge(s("row_sq"), b - 3)
                    for c in range(4):
                        mm = nc.tensor.matmul(ps[0:4, b, :], band[:, 3 - c:7 - c], squares[:, c, :],
                                              start=(c == 0), stop=(c == 3))
                pe.wait_ge(s("ws_in"), 16)
                for c in range(4):
                    mm = nc.tensor.transpose(ps[:, 6, c * P:(c + 1) * P], ws[:, c, :], ident[:])
            if g in (22, 23):
                for c in range(4):
                    mm = nc.tensor.matmul(ps[:, 4 + c, :], sel[:, c, :], head_rows[:, g - 22, :], start=True, stop=True)
            if g in (24, 25):
                outer(g - 24)
            if g == 26:
                memory_out()
            if g in (27, 28):
                for i in range(2):
                    for j in range(NB):
                        nc.tensor.transpose(ps[:, 4 + i, j * P:(j + 1) * P],
                                            zT[:, Z_AV + 2 * (g - 27) + i, j * P:(j + 1) * P], ident[:])
            if g in NORM_SLICES:
                mm = norms_pe(pe, g)
            if g == 27:
                pe.wait_ge(s("dec_sq"), 1)
                nc.tensor.matmul(ps[:, 7, 0:8 * S], ones[:], dsq[:, 0:8, :], start=True, stop=True)
                mm = nc.tensor.matmul(ps[:, 7, 8 * S:18 * S], pairones[:], dsq[:, 8:18, :], start=True, stop=True)
            if g == 29:
                pe.wait_ge(s("a_wst"), 1)
                for c in range(4):
                    for j in range(NB):
                        mm = nc.tensor.matmul(ps[:, 4 + c, j * P:(j + 1) * P], vnt[:, j, c, :], wst[:, c, :],
                                              start=True, stop=True)
            return mm

        def slice_pe(g):
            if g > SLICE0:
                pe.wait_ge(slice_read, g - SLICE0)
            if g < SLICE0 + 2:
                mm = keys_and_values(g)
            elif g < SLICE0 + 10:
                h = (g - SLICE0 - 2) // 2
                mm = outputs(h) if (g - SLICE0) % 2 else scores(h)
            else:
                mm = late(g)
            mm.then_inc(slice_mm, 1)

        def new_keys():
            pe.wait_ge(slice_read, Z_N - 1 - SLICE0)
            pe.wait_ge(z_free, Z_N + 1)
            nc.tensor.transpose(ps[:, 0, 0:P], zT[:, Z_BK, T - P:T], ident[:])
            nc.tensor.transpose(ps[0:S, 0, 128:256], zT[:, Z_BK, T:N], ident[:])
            nc.tensor.transpose(ps[0:S, 0, 256:384], zT[:, Z_BV, T:N], ident[:]).then_inc(s("b_t"), 1)
            for j in range(NB):
                t = nc.tensor.transpose(ps[:, 1, j * P:(j + 1) * P], zT[:, Z_BV, j * P:(j + 1) * P], ident[:])
            t.then_inc(s("b_t"), 1)

        slice_pe(SLICE0)
        for u in range(SLICE0 + 1, Z_N):
            pe.wait_ge(z_free, u + 1)
            unit_mm(4 * u, 2 * (u % 2))
            if u == Z_N - 1:
                new_keys()
            slice_pe(u)
        pe.wait_ge(z_free, Z_N + 2)

        pe.wait_ge(s("kc_in"), 16 * 4)
        for b in range(S):
            t = nc.tensor.transpose(ps[:, 2 + b // 4, (b % 4) * P:(b % 4 + 1) * P], kc_[:, b, :], ident[:])
        t.then_inc(s("b_kct"), 1)
        pe.wait_ge(s("b_kct_read"), 2)
        pe.wait_ge(s("b_q8"), 1)
        for b in range(S):
            mm = nc.tensor.matmul(ps[:, 2, b * 16:b * 16 + 16], kct[:, b, :], qb_[:, b, :], start=True, stop=True)
        mm.then_inc(s("b_s8"), 1)
        pe.wait_ge(slice_read, LAST_SLICE - SLICE0 + 1)
        for c in range(4):
            t = nc.tensor.transpose(ps[0:S, 5, c * P:(c + 1) * P], zT[:, Z_AV + c, T:N], ident[:])
        t.then_inc(s("a_v8"), 1)
        pe.wait_ge(s("b_s8_read"), 1)
        nc.tensor.transpose(ps[:, 3, 0:P], s_t[:], ident[:]).then_inc(s("b_s8t"), 1)
        pe.wait_ge(s("b_p8"), 1)
        nc.tensor.transpose(ps[:, 2, 0:P], s_s[:, 0:P], ident[:]).then_inc(s("b_p8t"), 1)
        pe.wait_ge(s("b_p8t_read"), 1)
        for b in range(S):
            mm = nc.tensor.matmul(ps[:, 3, b * 16:b * 16 + 16], vc_[:, b, :], p_t[:, b * 16:b * 16 + 16],
                                  start=True, stop=True)
        mm.then_inc(s("b_o8"), 1)
        pe.wait_ge(s("b_vk"), 1)
        with pe.Fori(0, 2) as it:
            first = it * 16

            def qk(n):
                kv, sl, i = n // 8, n // 4 % 2, n % 4
                if i == 0:
                    pe.wait_ge(s("b_pair"), it * 4 + (n // 4 + 1))
                pe.wait_ge(s("b_sc_free"), first + (n + 1))
                for r in range(2):
                    lo = 0 if i else P
                    mm = nc.tensor.matmul(ps[:, 4 - 2 * r + n % 2, lo:256],
                                          qst[64 * r:64 * r + 64, sl, i * P:(i + 1) * P],
                                          kd[64 * r:64 * r + 64, kv, (i - 1) * P + lo:(i + 1) * P],
                                          start=True, stop=True)
                mm.then_inc(s("b_qk"), 1)

            def turn(n):
                i = n % 4
                pe.wait_ge(s("b_prob"), first + (n + 1))
                pe.wait_ge(s("b_pt"), first + (n + 1))
                for r in range(2):
                    for kb in range(0 if i else 1, 2):
                        t = nc.tensor.transpose(ps[:, TURN_BANK[n % 2], (2 * r + kb) * P:(2 * r + kb + 1) * P],
                                                sx[:, n % 4, r, kb * P:(kb + 1) * P], ident[:])
                t.then_inc(s("b_turn"), 1)

            def pv(n):
                kv, i = n // 8, n % 4
                pe.wait_ge(s("b_pt"), first + (n + 3))
                pe.wait_ge(s("b_o_free"), first + (n + 1))
                for r in range(2):
                    for kb in range(0 if i else 1, 2):
                        mm = nc.tensor.matmul(ps[64 * r:64 * r + 64, 7 * (n % 2), 0:P],
                                              vtb[:, i - 1 + kb, 64 * kv:64 * kv + 64],
                                              pt[:, n % 2, (2 * r + kb) * P:(2 * r + kb + 1) * P],
                                              start=(kb == 0 or i == 0), stop=(kb == 1))
                mm.then_inc(s("b_o"), 1)

            for n in range(0, 16 + 4, 2):
                for part, late in ((qk, 0), (turn, 2), (pv, 4)):
                    if 0 <= n - late < 16:
                        part(n - late)
                        part(n - late + 1)
        pe.wait_ge(s("b_ended"), 2)
        barrier(pe, 1)

        for u in range(2):
            pe.wait_ge(z_free, U_OUT + u + 1)
            unit_mm(4 * (U_OUT + u), 2 * u,
                    before=(lambda k: pe.wait_ge(mix_lo, 4 * (k + 1))) if u == 0 else None)
        with pe.Fori(U_OUT // 2 + 1, U_FFN // 2) as i:
            for u in range(2):
                pe.wait_ge(z_free, i * 2 + (u + 1))
                unit_mm(i * 8 + 4 * u, 2 * u)

        def up_mm(q0, bank, before=None):
            for k in range(4):
                pe.wait_ge(w_lo, q0 + (k + 1))
                if before is not None:
                    before(k)
                tile_mm(k, bank, whi, wlo, h2_hi, h2_lo)

        def down_mm(q0, d0):
            for k in range(4):
                pe.wait_ge(w_lo, q0 + (k + 1))
                pe.wait_ge(s("d_add"), d0 + (k + 1))
                b = 4 + 2 * (k % 2)
                for kind, (w, x) in enumerate(((whi, g_hi), (whi, g_lo), (wlo, g_hi))):
                    for c in range(4):
                        for h in range(2):
                            mm = nc.tensor.matmul(ps[:, b + h, 0:NH], w[:, k, c, :], x[:, c, h * NH:(h + 1) * NH],
                                                  start=(kind == 0 and c == 0), stop=(kind == 2 and c == 3))
                mm.then_inc(w_used, 1)
                yield k

        def first_up(k):
            pe.wait_ge(s("h2_lo"), 13 + k)

        def sum_squares():
            pe.wait_ge(s("o_sum"), KC)
            for h in range(2):
                mm = nc.tensor.matmul(ps[:, 4 + h, 0:NH], ones[:], ssum[:, h * NH:(h + 1) * NH], start=True, stop=True)
            mm.then_inc(s("o_sum_mm"), 1)

        def turn_params(grp, d0):
            pe.wait_ge(s("par_in"), grp * 48 + 48)
            if d0 is not None:
                pe.wait_ge(s("d_add"), d0 + 2)
                begun(pe)
            for c in range(2 * GC):
                t = nc.tensor.transpose(ps[:, 6, 20 * c:20 * c + 20], par_rows[:, c // GC, (c % GC) * P:(c % GC + 1) * P],
                                        ident[0:20, 0:20])
            t.then_inc(s("par_turn"), 1)

        def up_units(q0, use0, j, before=None, params=None):
            for u in range(2):
                pe.wait_ge(z_free, use0 + (2 * j + u + 1))
                up_mm(q0 + 4 * u, 2 * u, before if u == 0 else None)
                if before is not None and u == 0:
                    sum_squares()
                if params is not None and u == (0 if before is None else 1):
                    turn_params(*params)

        up_units(4 * U_FFN, U_FFN, 0, first_up, (0, None))
        for j in range(1, GC):
            up_units(4 * U_FFN + 8 * j, U_FFN, j)
        with pe.Fori(1, NG) as i:
            q0, use0 = i * 48 + 4 * (U_FFN + U_GRP - 12), i * 8 + U_FFN
            up_units(q0, use0, 0, None, (i, i * 16 - 16))
            pe.wait_ge(s("par_ready"), i + 1)
            pe.wait_ge(s("g_lo"), i * GC)
            for m in range(GC):
                for _ in down_mm(q0 + (8 + 4 * m), i * 16 + (4 * m - 16)):
                    pass
            for j in range(1, GC):
                up_units(q0 + (16 + 8 * j), use0, j)

        def turn_tail(r):
            b = 2 + r % 2
            if r >= 2:
                pe.wait_ge(s("t_read"), r - 1)
            for c in range(4):
                t = nc.tensor.transpose(ps[0:S + 2, b, c * P:(c + 1) * P], ztail[:, 4 * r + c, :], ident[:])
            t.then_inc(s("t_turn"), 1)

        def turn_y(dt):
            pe.wait_ge(s("d_add"), (NG - 1) * 16 + dt + 3)
            if dt >= 2:
                pe.wait_ge(s("y_read"), dt - 1)
            for j in range(NB):
                t = nc.tensor.transpose(ps[:, dt % 2, j * P:(j + 1) * P], xT[:, dt, j * P:(j + 1) * P], ident[:])
            t.then_inc(s("y_turn"), 1)

        pe.wait_ge(z_free, U_FFN + 8 * NG + 2)
        tails = iter(range(FC // 2))
        for _ in range(6):
            turn_tail(next(tails))
        pe.wait_ge(s("g_lo"), NG * GC)
        for m in range(GC):
            for k in down_mm(4 * (U_ALL - GC + m), (NG - 1) * 16 + 4 * m):
                if 4 * m + k >= 1:
                    turn_y(4 * m + k - 1)
                    turn_tail(next(tails))
        turn_y(15)
        turn_tail(next(tails))
        assert next(tails, None) is None
        pe.wait_ge(s("t_read"), FC // 2)
        for q in range(4):
            if q == 0:
                pe.wait_ge(s("d_add"), NG * 16 + 2)
            for c in range(4):
                t = nc.tensor.transpose(ps[0:S, 4 + q, c * P:(c + 1) * P], xT[:, 4 * q + c, T:N], ident[:])
        t.then_inc(s("y8_turn"), 1)

    @block.scalar
    def _(act):
        link = Chain(act, chain_a)

        def q_hi(q, k, slot, landed):
            if k == 0:
                act.wait_ge(raw_in[slot], landed)
            act.wait_ge(w_used, q + 1)
            nc.scalar.activation(whi[:, k, :, :], rawq(k, slot), ACT.Copy)\
                .then_inc(w_hi, 1)

        def unit_hi(q0, slot, landed):
            for k in range(4):
                q_hi(q0 + k, k, slot, landed)

        for rows, name, a, b in (((0, 16), "norm1", 0, D), ((16, 32), "norm2", 0, D),
                                 ((32, 36), "a_v_gain", 0, 512), ((36, 40), "c_h_gain", 0, 512)):
            act.dma_start(vrow[rows[0]:rows[1], :], io[name].rearrange("l (c p) -> (l c) p", p=P)).then_inc(vec_in, 16)
        for row, name in ((40, "b_q_gain"), (41, "b_k_gain")):
            for h in range(2):
                act.dma_start(vrow[row:row + 1, 64 * h:64 * h + 64], io[name]).then_inc(vec_in, 16)
        for idx in range(0, 16, 2):
            i, c4 = idx // 4, idx % 4
            act.wait_ge(x_tr, idx + 1)
            nc.scalar.activation(xT[:, 4 * c4:4 * c4 + 4, i * P:(i + 1) * P],
                                 ps[:, idx % 6, :].rearrange("p (c n) -> p c n", c=4), ACT.Copy).then_inc(x_ev_a, 1)
        act.wait_ge(x_ev_a, 8)
        act.wait_ge(x_ev_v, 9)
        act.wait_ge(vec_ev, 1)
        act.wait_ge(wg_in, 16)
        act.wait_ge(ring_zero, 2)
        gates = wg_raw[:].rearrange("p (c k) n -> p k c n", k=4)
        nc.scalar.activation(whi[:, :, :, 0:4], gates[:, :, :, 0:4], ACT.Copy)
        nc.scalar.activation(whi[:, :, :, 32:36], gates[:, :, :, 4:8], ACT.Copy).then_inc(wg_hi, 1)
        for c in K_ORDER:
            nc.scalar.activation(act_hi[:, c, :], xT[:, c, :], ACT.Copy, scale=vecs[:, G1 + c:G1 + c + 1]).then_inc(h_hi, 1)
        def hi_pairs(first, last):
            with act.Fori(first, last) as i:
                unit_hi(i * 8 + 4, 1, i * 16 + 16)
                unit_hi(i * 8 + 8, 0, i * 16 + 32)

        unit_hi(0, 0, 16)
        act.wait_ge(var_v, 1)
        nc.scalar.activation(small[:, 16:21], small[:, 8:13], ACT.Sqrt).then_inc(var_a, 1)
        act.wait_ge(s("rel_mm"), 1)
        nc.scalar.activation(brow[:], ps[0:16, 6, 0:384], ACT.Copy, scale=8.0).then_inc(s("rel_read"), 1)
        act.wait_ge(s("rel_read"), 1)
        act.dma_start(bias_rows, brow[:].rearrange("h (a w) -> h a w", a=1).broadcast_to([16, P + 1, 384]))\
            .then_inc(s("rel_out"), 16)
        act.dma_start(ws[:], io["a_spatial_w"].rearrange("l g t s -> t (l g) s")).then_inc(s("ws_in"), 16)
        asb, asw = io["a_spatial_b"], io["a_spatial_w"]
        act.dma_start(w00[:], bass.AP(tensor=asw.tensor, offset=asw.offset, ap=[[0, P], [P * P, 4], [1, 1]])).then_inc(s("a_in"), 16)
        hi_pairs(0, 2)
        act.wait_ge(s("c_fabs"), 1)
        link(nc.scalar.activation(gf[32:36, 2, :], gf[32:36, 1, :], ACT.Exp, scale=-1.0))
        nc.scalar.activation(gf[32:36, 2, :], gf[32:36, 2, :], ACT.Ln, bias=1.0).then_inc(s("c_ln"), 1)
        hi_pairs(2, 4)
        act.wait_ge(s("c_lines"), 1)
        nc.scalar.activation(gi[:, 7, :], gi[:, 4, :], ACT.Exp, scale=-1.0)
        nc.scalar.activation(gi[:, 5, 0:T], gi[:, 2, 0:T], ACT.Exp, bias=gi[:, 6, T - 1:T])
        nc.scalar.activation(gs[:].rearrange("p a b -> p (a b)"), gs[:].rearrange("p a b -> p (a b)"), ACT.Exp)\
            .then_inc(s("c_exp"), 1)
        store(act, io["m_prompt"].rearrange("l b h -> h (l b)"), gi[:, 4, T - 1:T])
        store(act, io["m_sample"].rearrange("l b h -> h (l b)"), gi[:, 4, T:N])
        hi_pairs(4, (SLICE0 + 1) // 2)

        def values(g):
            for i in range(2):
                nc.scalar.activation(vtok[:, :, 2 * (g - SLICE0) + i, 0:P], ps[:, 4 + i, :].rearrange("p (j n) -> p j n", j=NB),
                                     ACT.Copy).then_inc(s("c_v_read"), 1)
                yield
            if g > SLICE0:
                nc.scalar.activation(v8[:], ps[0:S, 7, :], ACT.Copy).then_inc(s("c_v_read"), 1)

        def decays(h):
            act.wait_ge(s("c_masked"), h + 1)
            for j in range(NB):
                b_j = ct[:, j, h:h + 1]
                last = nc.scalar.activation(dmat[:, DIAG[j]:DIAG[j] + P], tmpm[:, j * P:(j + 1) * P], ACT.Exp, bias=b_j)
                if j < NB - 1:
                    last = nc.scalar.activation(dmat[:, DIAG[j] + P:DIAG[j] + T - j * P], ps[:, 4, (j + 1) * P:T],
                                                ACT.Exp, bias=b_j)
            last.then_inc(s("c_decay"), 1)
            yield

        def outputs(h):
            nc.scalar.activation(qab[:], ps[:, 6, :], ACT.Abs).then_inc(s("c_abs"), 1)
            yield
            if h == 1:
                act.wait_ge(s("c_mem_read"), 1)
                for q in range(2):
                    store(act, io["C_prompt"].rearrange("l b (k two) d e -> two d (l b k) e", two=2)[q],
                          cout[64 * q:64 * q + 64, :, 0:P])
                    store(act, io["n_prompt"].rearrange("l b (k two) d -> two d (l b k)", two=2)[q],
                          cout[64 * q:64 * q + 64, :, P])

        def after_heads():
            act.wait_ge(z_free, Z_AV + 4 + 2)
            link(nc.scalar.activation(zT[:, Z_AV:Z_AV + 4, :], zT[:, Z_AV:Z_AV + 4, :], ACT.Gelu))
            yield
            act.wait_ge(s("c_head"), 4)
            for q in range(2):
                act.dma_start(cst[64 * q:64 * q + 64, :, :],
                              io["state_mlstm_C"].rearrange("l b (k two) d e -> two d (l b k) e", two=2)[q])\
                    .then_inc(s("c_in"), 16)
            nc.scalar.activation(nsq[:], zT[:, Z_CV:Z_CV + 4, 0:T], ACT.Square).then_inc(s("row_sq"), 1)
            yield
            nc.scalar.activation(nsqa[:], zT[:, Z_AV:Z_AV + 4, 0:T], ACT.Square).then_inc(s("row_sq"), 1)

        def late(g):
            if g == 21:
                nc.scalar.activation(wst[:].rearrange("p g n -> p (g n)"), ps[:, 6, :], ACT.Copy).then_inc(s("a_wt_read"), 1)
                act.wait_ge(s("row_var"), 1)
                nc.scalar.activation(head_rows[:], head_rows[:], ACT.Sqrt).then_inc(s("row_root"), 1)
                yield
            if g == 22:
                act.dma_start(kc_[1:P, :, :], io["cache_swa_k"][0, :, 1:P].rearrange("b w h d -> w b (h d)")).then_inc(s("kc_in"), 16)
                nc.scalar.activation(zT[:, Z_CO:Z_CO + 4, :], zT[:, Z_CO:Z_CO + 4, :], ACT.Sigmoid).then_inc(s("c_sig"), 1)
                yield
            if g == 24:
                act.dma_start(vc_[1:P, :, :], io["cache_swa_v"][0, :, 1:P].rearrange("b w h d -> w b (h d)")).then_inc(s("kc_in"), 16)
            if g == 26:
                for q in range(2):
                    abs8 = nc.scalar.activation(heads_of(hs[:, 0, :], q), heads_of(ps[:, 4 + q, 64:96], q), ACT.Abs)
                abs8.then_inc(s("c_abs8"), 1)
                for q in range(2):
                    store(act, io["n_sample"].rearrange("l b (k two) d -> two d (l b k)", two=2)[q], ns[64 * q:64 * q + 64, :])
                    store(act, io["C_sample"].rearrange("l b (k two) d e -> two d (l b k) e", two=2)[q],
                          cst[64 * q:64 * q + 64, :, :])
                act.dma_start(bbc[:], bass.AP(tensor=asb.tensor, offset=asb.offset, ap=[[0, P], [P, 4], [1, P]])).then_inc(s("a_in"), 16)
            if g in (27, 28):
                for i in range(2):
                    v = nc.scalar.activation(vnt[:, :, 2 * (g - 27) + i, :], ps[:, 4 + i, :].rearrange("p (j n) -> p j n", j=NB), ACT.Copy)
                v.then_inc(s("a_vt_read"), 1)
                yield
            roots_act(act, g)
            if g == 27:
                act.wait_ge(s("dec_var"), 1)
                nc.scalar.activation(dvar[:], dvar[:], ACT.Sqrt).then_inc(s("dec_root"), 1)
            yield
            squares_act(act, g + 1)
            if g == 26:
                act.wait_ge(s("c_num8_read"), 1)
                act.wait_ge(z_free, Z_BQ + 8 + 2)
                nc.scalar.activation(dsq[:, 0:4, :], zT[:, Z_CV:Z_CV + 4, T:N], ACT.Square)
                nc.scalar.activation(dsq[:, 4:18, :], zT[:, Z_AV:Z_AV + 14, T:N], ACT.Square).then_inc(s("dec_sq"), 1)
            if g in (28, 29):
                first = Z_AU + 2 * (g - 28)
                act.wait_ge(z_free, first + 2 + 2)
                nc.scalar.activation(zT[:, first:first + 2, :], zT[:, first:first + 2, :], ACT.Gelu).then_inc(s("a_gelu"), 1)

        def slice_act(g):
            act.wait_ge(slice_mm, g - SLICE0 + 1)
            if g < SLICE0 + 2:
                yield from values(g)
            elif g < SLICE0 + 10:
                h = (g - SLICE0 - 2) // 2
                yield from (outputs(h) if (g - SLICE0) % 2 else decays(h))
                if g == 20:
                    yield from after_heads()
            else:
                yield from late(g)

        def new_keys():
            act.wait_ge(w_used, USED_IN)
            act.wait_ge(s("b_t"), 1)
            link(nc.scalar.activation(kv8[:], ps[0:S, 0, 128:384].rearrange("p (a n) -> p a n", a=2), ACT.Copy))
            act.dma_start(kc_[0:1, :, :], kv8[:, 0, :]).then_inc(s("kc_in"), 16)
            act.dma_start(vc_[0:1, :, :], kv8[:, 1, :]).then_inc(s("kc_in"), 16)
            link(nc.scalar.activation(ktb[:], ps[:, 0, 0:P], ACT.Copy))
            act.wait_ge(s("rel_out"), 16)
            sinks = io["b_sinks"]
            act.dma_start(sinkbc[:], bass.AP(tensor=sinks.tensor, offset=sinks.offset, ap=[[0, P], [1, 16]])).then_inc(s("b_in"), 16)
            act.dma_start(bsink[:], bass.AP(tensor=sinks.tensor, offset=sinks.offset, ap=[[0, S], [1, 16], [1, 1]])).then_inc(s("b_in"), 16)
            act.dma_start(bias_s[:, 1:P], bass.AP(tensor=bias_rows.tensor, offset=128, ap=[[0, S], [BIAS_PITCH, 16], [1, P - 1]])).then_inc(s("b_in"), 16)
            act.dma_start(bias_s[:, 0:1], bass.AP(tensor=bias_rows.tensor, offset=255, ap=[[0, S], [BIAS_PITCH, 16], [1, 1]])).then_inc(s("b_in"), 16)

        for g in range(SLICE0, LAST_SLICE + 1):
            if g == LAST_SLICE:
                new_keys()
            work = slice_act(g)
            next(work, None)
            if g + 2 <= U_OUT:
                for k in range(4):
                    u = g + 2
                    q_hi(4 * u + k, k, u % 2, 16 * (u // 2) + 16)
                    next(work, None)
            for _ in work:
                pass
        act.wait_ge(s("b_t"), 2)
        link(nc.scalar.activation(vtb[:], ps[:, 1, :].rearrange("p (j n) -> p j n", j=NB), ACT.Copy))
        act.drain().then_inc(s("b_vk_a"), 1)
        for i in range(2):
            act.wait_ge(s("b_kct"), 1)
            nc.scalar.activation(kct[:, 4 * i:4 * i + 4, :], ps[:, 2 + i, :].rearrange("p (j n) -> p j n", j=NB),
                                 ACT.Copy).then_inc(s("b_kct_read"), 1)
        act.wait_ge(s("b_s8"), 1)
        nc.scalar.activation(s_t[:], ps[:, 2, 0:P], ACT.Copy).then_inc(s("b_s8_read"), 1)
        act.wait_ge(s("b_max8"), 1)
        nc.scalar.activation(s_s[:], s_s[:], ACT.Exp, bias=mxn[:, 0, 0, 1:2], accum_out=mxn[:, 0, 0, 2:3]).then_inc(s("b_exp8"), 1)
        act.wait_ge(s("a_v8"), 1)
        link(nc.scalar.activation(vn8[:], ps[0:S, 5, :], ACT.Copy))
        act.wait_ge(s("b_p8t"), 1)
        nc.scalar.activation(p_t[:], ps[:, 2, 0:P], ACT.Copy).then_inc(s("b_p8t_read"), 1)
        store(act, io["chunk_v"].rearrange("l b t w -> (l b t) w"), vn8[:])
        store(act, io["k_prompt"].rearrange("l b w h d -> (l b w) (h d)"), ktb[:])
        store(act, io["v_prompt"].rearrange("l b w h d -> (l b w) (h d)"), vtb[:, NB - 1, :])
        store(act, io["k_sample"].rearrange("l b w h d -> (l b w) (h d)"), kv8[:, 0, :])
        store(act, io["v_sample"].rearrange("l b w h d -> (l b w) (h d)"), kv8[:, 1, :])
        act.wait_ge(s("b_o8_read"), 1)
        with act.Fori(0, 2) as it:
            first = it * 16

            def exps(n):
                lo = 0 if n % 4 else P
                act.wait_ge(s("b_max"), first + (n + 1))
                for r in range(2):
                    e = nc.scalar.activation(sx[:, n % 4, r, lo:257], sx[:, n % 4, r, lo:257], ACT.Exp,
                                             bias=mxn[:, n % 4, r, 1:2], accum_out=mxn[:, n % 4, r, 2:3])
                e.then_inc(s("b_exp"), 1)

            def read_turn(n):
                lo = 0 if n % 4 else P
                act.wait_ge(s("b_turn"), first + (n + 5))
                act.wait_ge(s("b_o"), first + (n + 1))
                nc.scalar.activation(pt[:, n % 2, :].rearrange("p (r k) -> p r k", r=2)[:, :, lo:256],
                                     ps[:, TURN_BANK[n % 2], :].rearrange("p (r k) -> p r k", r=2)[:, :, lo:256], ACT.Copy)\
                    .then_inc(s("b_pt"), 1)

            for n in range(16 + 2):
                if n < 16:
                    exps(n)
                if n >= 2:
                    read_turn(n - 2)
        act.wait_ge(s("b_pt"), 34)
        act.wait_ge(out_done, out_count[0])
        act.wait_ge(s("b_ended"), 2)
        barrier(act, 1)

        for c in K_ORDER:
            nc.scalar.activation(act_hi[:, c, :], zT[:, MIX_TILES[c], :], ACT.Copy).then_inc(mix_hi, 1)

        def residual(n, u, tile):
            act.wait_ge(z_free, n + (Z_N + 3))
            nc.scalar.activation(ssq[:, u, :], xT[:, tile, :].rearrange("p a n -> p (a n)"), ACT.Square).then_inc(s("o_sq"), 1)
            nc.scalar.activation(h2_hi[:, tile, :].rearrange("p a n -> p (a n)"), xT[:, tile, :].rearrange("p a n -> p (a n)"),
                                 ACT.Copy, scale=gain2[:, u:u + 1]).then_inc(s("h2_hi"), 1)

        with act.Fori(U_OUT // 2, U_FFN // 2) as i:
            unit_hi(i * 8 + 4, 1, i * 16 + 16)
            residual(i * 2 - U_OUT, 0, bass.ds(i * 2 - U_OUT, 1))
            unit_hi(i * 8 + 8, 0, i * 16 + 32)
            residual(i * 2 + (1 - U_OUT), 1, bass.ds(i * 2 + (1 - U_OUT), 1))

        def norm_root(n, j):
            act.wait_ge(s("o_mean"), 1)
            nc.scalar.activation(rs2[:], rs2[:], ACT.Sqrt).then_inc(s("o_root"), 1)

        def start_g(n, j):
            act.wait_ge(s("f_zg"), n + 1)
            if j == 0:
                act.wait_ge(s("par_turn"), n_group + 1)
                nc.scalar.activation(cpar[:].rearrange("p a c n -> p (a c n)"), ps[:, 6, 0:40 * GC], ACT.Copy)\
                    .then_inc(s("par_ready"), 1)
                act.wait_ge(s("par_ready"), n_group + 1)
            nc.scalar.activation(cg[:], zg[:, 2:], ACT.Identity, scale=cpar[:, 0, j, 18:19], bias=cpar[:, 0, j, 19:20])\
                .then_inc(s("f_tg"), 1)

        def start_a(n, j):
            act.wait_ge(s("f_za"), n + 1)
            nc.scalar.activation(ca[:], za[:, 2:], ACT.Identity, scale=cpar[:, 1, j, 18:19], bias=cpar[:, 1, j, 19:20])\
                .then_inc(s("f_ta"), 1)

        def silu(n, j):
            act.wait_ge(s("f_cg"), n + 1)
            nc.scalar.activation(cg[:], cg[:], ACT.Silu).then_inc(s("f_silu"), 1)

        def gated_hi(n, j):
            act.wait_ge(s("f_m"), n + 1)
            nc.scalar.activation(g_hi[:, j, :], gm[:], ACT.Copy).then_inc(s("g_hi"), 1)

        def ffn_group_act(q1, pair0, n0, grp, with_down):
            nonlocal n_group
            n_group = grp
            units = GC * 3 if with_down else U_GRP
            due = {} if with_down else {(1, 3): [(norm_root, 0)]}
            for j in range(GC):
                g = 2 * j + (GC if with_down and j else 0)
                due.setdefault((g + 2, 1), []).append((start_g, j))
                late = g + 3 <= units
                due.setdefault((g + 3, 0) if late else (units, 3), []).append((start_a, j))
                due.setdefault((g + 3, 1) if late else (units, 3), []).append((silu, j))
                hi_at = ((GC + 2, 3) if with_down and j == 0 else (g + 3, 2)) if late else (units, 3)
                due.setdefault(hi_at, []).append((gated_hi, j))
            for u in range(1, units + 1):
                for k in range(4):
                    q_hi(q1 + (4 * (u - 1) + k), k, u % 2, pair0 + 16 * (u // 2))
                    for step, j in due.get((u, k), []):
                        if step is gated_hi and j == 0 and with_down:
                            act.wait_ge(w_used, q1 + (4 * (GC + 1) + 4))
                        step(n0 + j, j)

        n_group = 0
        ffn_group_act(4 * U_FFN + 4, 8 * U_FFN + 16, 0, 0, False)
        with act.Fori(1, NG) as i:
            ffn_group_act(i * 48 + 4 * (U_FFN + U_GRP - 12 + 1), i * 96 + 8 * (U_FFN + U_GRP - 12 + 2), i * GC, i, True)

        def read_tail(r):
            act.wait_ge(s("t_turn"), r + 1)
            nc.scalar.activation(trow[:, 512 * r:512 * r + 512], ps[0:S + 2, 2 + r % 2, :], ACT.Copy).then_inc(s("t_read"), 1)

        r = 0
        for u in range(U_ALL - GC, U_ALL):
            for k in range(4):
                if u > U_ALL - GC:
                    q_hi(4 * u + k, k, u % 2, 16 * (u // 2 + 1))
                    reads = 1
                else:
                    reads = 2
                for _ in range(reads):
                    if r < 6 or u > U_ALL - GC:
                        if r < FC // 2:
                            read_tail(r)
                            r += 1
        while r < FC // 2:
            read_tail(r)
            r += 1
        act.wait_ge(s("y8_turn"), 1)
        nc.scalar.activation(ytok8[:], ps[0:S, 4:8, :].rearrange("p a n -> p (a n)"), ACT.Copy).then_inc(s("y8_read"), 1)

    def read_y(dve, dt):
        dve.wait_ge(s("y_turn"), dt + 1)
        nc.vector.tensor_copy(ytok[:, :, dt * P:(dt + 1) * P], ps[:, dt % 2, :].rearrange("p (j n) -> p j n", j=NB))\
            .then_inc(s("y_read"), 1)

    @block.vector
    def _(dve):
        link = Chain(dve, chain_v)
        mult, add, sub, mx = ALU.mult, ALU.add, ALU.subtract, ALU.max
        tt, stt, ts = nc.vector.tensor_tensor, nc.vector.scalar_tensor_tensor, nc.vector.tensor_scalar

        dve.nop().then_inc(z_free, 2)
        nc.vector.memset(rel33[32:33, :], NEG).then_inc(s("rel_set"), 1)
        link(nc.vector.memset(small[:], 1.0))
        for idx in range(1, 16, 2):
            i, c4 = idx // 4, idx % 4
            dve.wait_ge(x_tr, idx + 1)
            nc.vector.tensor_copy(xT[:, 4 * c4:4 * c4 + 4, i * P:(i + 1) * P],
                                  ps[:, idx % 6, :].rearrange("p (c n) -> p c n", c=4)).then_inc(x_ev_v, 1)
        dve.wait_ge(x_tr, 17)
        nc.vector.tensor_copy(xT[:, :, T:N], ps[:, 6, 0:P].rearrange("p (c n) -> p c n", c=KC)).then_inc(x_ev_v, 1)
        dve.wait_ge(vec_tr, 1)
        nc.vector.tensor_copy(vecs[:, 0:42], ps[:, 7, 0:42]).then_inc(vec_ev, 1)
        dve.wait_ge(x_ev_v, 9)
        dve.wait_ge(x_ev_a, 8)
        dve.wait_ge(vec_ev, 1)
        for i, c in enumerate(K_ORDER):
            dve.wait_ge(h_hi, i + 1)
            stt(out=act_lo[:, c, :], in0=xT[:, c, :], scalar=vecs[:, G1 + c:G1 + c + 1], in1=act_hi[:, c, :].bitcast(F32),
                op0=mult, op1=sub).then_inc(h_lo, 1)
        for i in range(NB + 1):
            n = P if i < NB else S
            link(nc.vector.tensor_tensor_reduce(out=xjunk[0:n, :], in0=xtok[0:n, i, :], in1=xtok[0:n, i, :], scale=1.0,
                                                scalar=0.0, op0=mult, op1=add, accum_out=small[0:n, i:i + 1]))
        nc.vector.tensor_scalar(small[:, 8:13], small[:, 0:5], 1.0 / D, EPS, mult, add).then_inc(var_v, 1)
        dve.wait_ge(var_a, 1)
        link(nc.vector.reciprocal(small[:, 24:29], small[:, 16:21]))
        dve.wait_ge(const_made, 1)
        for i in range(NB):
            ts(xjunk[:, i * P:(i + 1) * P], ident[:], small[:, 24 + i:25 + i], None, mult)
        ts(xjunk[0:S, 512:512 + S], ident[0:S, 0:S], small[0:S, 28:29], None, mult).then_inc(rs_diag, 1)
        dve.wait_ge(rs_mm, 1)
        nc.vector.tensor_copy(rs1[:, 0:T], ps[:, 7, :])
        nc.vector.tensor_copy(rs1[:, T:N], ps[:, 6, 256:256 + S]).then_inc(rs_ready, 1)
        dve.wait_ge(rs_ready, 1)
        def read_pairs(first, last):
            with dve.Fori(first, last) as i:
                for u in range(2):
                    dve.wait_ge(w_used, i * 8 + (4 * u + 8))
                    tt(zT[:, bass.ds(i * 2 + u, 1), :].rearrange("p a (h n) -> p (a h) n", h=2), pair(2 * u),
                       halves(rs1[:]), mult).then_inc(z_free, 1)

        read_pairs(0, 2)
        dve.wait_ge(spilled, 16)
        dve.wait_ge(h_lo, KC)
        dve.wait_ge(misc_in, 48)
        r4, rf = slice(0, 4), slice(32, 36)
        tt(halves(gf[rf, 0, :]), ps[rf, 4:6, 0:NH], halves(rs1[rf, :]), mult)
        tt(halves(gi[:, 0, :]), ps[r4, 4:6, 0:NH], halves(rs1[r4, :]), mult).then_inc(s("c_gates_read"), 1)
        dve.wait_ge(s("c_gates_read"), 1)
        link(ts(gf[rf, 0, :], gf[rf, 0, :], gbf[rf, :], None, add))
        stt(out=gf[rf, 1, :], in0=gf[rf, 0, :], scalar=-1.0, in1=gf[rf, 0, :], op0=mult, op1=mx).then_inc(s("c_fabs"), 1)
        link(ts(gi[:, 0, :], gi[:, 0, :], gbi[:], None, add))
        link(ts(gf[rf, 3, :], gf[rf, 0, :], 0.0, None, ALU.min))
        read_pairs(2, 4)
        dve.wait_ge(s("c_ln"), 1)
        link(tt(gf[rf, 3, :], gf[rf, 3, :], gf[rf, 2, :], sub))
        link(nc.vector.memset(gf[rf, 0, :], 1.0))
        link(nc.vector.tensor_tensor_scan(gf[rf, 1, 0:T], gf[rf, 0, 0:T], gf[rf, 3, 0:T], 0.0, mult, add))
        link(nc.vector.tensor_copy(gf[rf, 1, T:N], gf[rf, 3, T:N]))
        link(nc.vector.tensor_copy(gi[:, 1, :], gf[rf, 1, :]))
        link(tt(gi[:, 2, :], gi[:, 0, :], gi[:, 1, :], sub))
        link(nc.vector.tensor_tensor_scan(gi[:, 3, 0:T], gi[:, 2, 0:T], gi[:, 2, 0:T], 0.0, mx, mx))
        link(tt(gi[:, 3, T:N], gi[:, 2, T:N], m0[:], mx))
        link(tt(gi[:, 4, :], gi[:, 1, :], gi[:, 3, :], add))
        link(tt(gs[:, 0, :], gi[:, 2, T:N], gi[:, 3, T:N], sub))
        link(tt(gs[:, 1, :], m0[:], gi[:, 3, T:N], sub))
        ts(gi[:, 6, :], gi[:, 3, :], -1.0, None, mult).then_inc(s("c_lines"), 1)
        dve.wait_ge(s("c_exp"), 1)
        ts(gi[:, 5, 0:T], gi[:, 5, 0:T], 0.125, None, mult)
        ts(gs[:, 0, :], gs[:, 0, :], 0.125, None, mult).then_inc(s("c_rows"), 1)
        link(nc.vector.memset(vtok[:, :, :, P:P + 1], 1.0))
        read_pairs(4, (SLICE0 + 1) // 2)

        def keys(t2):
            if t2 == 0:
                link(nc.vector.tensor_copy(ct[:].rearrange("p a b -> p (a b)"), ps[:, 7, 0:32]))
                link(nc.vector.tensor_copy(cs[:].rearrange("p a b -> p (a b)"), ps[:, 7, 64:96]))
                link(nc.vector.tensor_copy(emts[:], ps[:, 7, 128:160]))
            for q in range(2):
                h = 2 * t2 + q
                tt(kw[:, :, h, :], ps[:, 6, :].rearrange("p (j d) -> p j d", j=NB)[:, :, 64 * q:64 * q + 64],
                   ct[:, 4:8, h:h + 1].broadcast_to([P, NB, 64]), mult)
            if t2 == 1:
                dve.wait_ge(s("n_in"), 32)
                link(tt(kws[:], zT[:, Z_CK:Z_CK + 2, T:N], cs[:, :, 0:S], mult))
                n_kb = ns[:].rearrange("p (b k) -> p k b", k=2)
                link(tt(n_kb, n_kb, cs[:, :, S:2 * S], mult))
                link(tt(n_kb, n_kb, kws[:], add))
                link(tt(nq[:], zT[:, Z_CQ:Z_CQ + 2, T:N], n_kb, mult))
            dve.wait_ge(s("c_v_read"), (2, 5)[t2])

        def scores(h):
            if h == 0:
                dve.wait_ge(out_done, 32)
            tt(tmpm[:].rearrange("p (j n) -> p j n", j=NB), ps[:, 4, :].rearrange("p (j n) -> p j n", j=NB),
               causal[:].rearrange("p (j n) -> p j n", j=1).broadcast_to([P, NB, P]), add).then_inc(s("c_masked"), 1)
            dve.wait_ge(s("c_decay"), h + 1)
            for j in range(NB):
                n, (b, at) = T - j * P, SCORE_AT[j]
                stt(out=pmat[:, DIAG[j]:DIAG[j] + n], in0=ps[:, b, at:at + n], scalar=0.125,
                    in1=dmat[:, DIAG[j]:DIAG[j] + n], op0=mult, op1=mult)

        def outputs(h):
            if h == 0:
                nc.vector.tensor_copy(k8[:], ps[0:S, 7, 0:256])
            if h == 1:
                nc.vector.tensor_copy(cout[:].rearrange("p a b -> p (a b)"), ps[:, 7, 0:258]).then_inc(s("c_mem_read"), 1)
            dve.wait_ge(s("c_abs"), h + 1)
            link(tt(den[:], qab[:], ps[:, 4, :], mx))
            link(nc.vector.reciprocal(den[:], den[:]))
            tt(zT[:, Z_CV + h, 0:T], ps[:, 5, :], den[:], mult).then_inc(s("c_head"), 1)

        def late(g):
            if g == 21:
                for b in (4, 5):
                    o = ts(head_rows[:, b - 4, :], ps[0:4, b, :], 1.0 / P, EPS, mult, add)
                o.then_inc(s("row_var"), 1)
                dve.wait_ge(s("row_root"), 1)
                link(nc.vector.reciprocal(head_rows[:], head_rows[:]))
                dve.wait_ge(s("a_wt_read"), 1)
            if g in (22, 23):
                tile, gain = ((Z_CV, GCH), (Z_AV, GAV))[g - 22]
                for c in range(4):
                    stt(out=zT[:, tile + c, 0:T], in0=zT[:, tile + c, 0:T], scalar=vecs[:, gain + c:gain + c + 1],
                        in1=ps[:, 4 + c, :], op0=mult, op1=mult)
            if g in (24, 25):
                for half in range(2):
                    c_v = cst[:].rearrange("p (b k) e -> p k b e", k=2)[:, g - 24, 4 * half:4 * half + 4, :]
                    link(tt(c_v, c_v, ps[:, 4 + half, :].rearrange("p (b e) -> p b e", b=4), add))
            if g in (23, 24):
                for q in range(2):
                    h = 2 * (g - 23) + q
                    tt(vm[:, q, :].rearrange("p (b e) -> p b e", b=S),
                       v8[:, h * P:(h + 1) * P].rearrange("p (a e) -> p a e", a=1).broadcast_to([S, S, P]),
                       ident[0:S, 0:S].rearrange("p (b a) -> p b a", a=1).broadcast_to([S, S, P]), mult)\
                        .then_inc(s("c_vm"), 1)
            if g == 22:
                dve.wait_ge(s("c_in"), 32)
                for hp in range(2):
                    c_v = cst[:].rearrange("p (b k) e -> p k b e", k=2)[:, hp, :, :]
                    link(tt(c_v, c_v, cs[:, hp, S:2 * S].rearrange("p (b a) -> p b a", a=1).broadcast_to([P, S, P]), mult))
            if g == 26:
                dve.wait_ge(s("c_abs8"), 1)
                link(tt(hs[:, 1, :], hs[:, 0, :], emts[:], mx))
                link(nc.vector.reciprocal(hs[:, 2, :], hs[:, 1, :]))
                for q in range(2):
                    o = tt(zT[:, Z_CV:Z_CV + 4, T:N].rearrange("p (k q) b -> p q k b", q=2)[:, q],
                           heads_of(ps[:, 4 + q, 0:32], q), heads_of(hs[:, 2, :], q), mult)
                o.then_inc(s("c_num8_read"), 1)
            norms_dve(dve, g, link)
            if g in (27, 28):
                dve.wait_ge(s("a_vt_read"), g - 26)
            if g == 27:
                ts(dvar[:, 0:8, :], ps[:, 7, 0:8 * S].rearrange("p (c b) -> p c b", b=S), 1.0 / P, EPS, mult, add)
                ts(dvar[:, 8:18, :], ps[:, 7, 8 * S:18 * S].rearrange("p (c b) -> p c b", b=S), 1.0 / 64, EPS, mult, add)\
                    .then_inc(s("dec_var"), 1)
                dve.wait_ge(s("dec_root"), 1)
                link(nc.vector.reciprocal(dvar[:], dvar[:]))
                normed = [(Z_CV + c, 1, c, GCH + c) for c in range(4)] + [(Z_AV + c, 1, 4 + c, GAV + c) for c in range(4)]
                normed += [(Z_BK, 1, 8, GBK), (Z_BQ, 8, 10, GBQ)]
                for tile, n, at, gain in normed:
                    o = stt(out=zT[:, tile:tile + n, T:N], in0=zT[:, tile:tile + n, T:N], scalar=vecs[:, gain:gain + 1],
                            in1=dvar[:, at:at + n, :], op0=mult, op1=mult)
                link(o)
            if g == 28:
                dve.wait_ge(s("a_in"), 32)
                for c in range(4):
                    o = ts(asmp[:, c, :], zT[:, Z_AV + c, T:N], w00[:, c:c + 1], bbc[:, c, 0:1], mult, add)
            if g == 29:
                for c in range(4):
                    link(tt(amix[:].rearrange("p (j n) -> p j n", j=NB), ps[:, 4 + c, :].rearrange("p (j n) -> p j n", j=NB),
                            bbc[:, c:c + 1, :].broadcast_to([P, NB, P]), add))
                    dve.wait_ge(s("a_gelu"), c // 2 + 1)
                    link(tt(zT[:, Z_AU + c, 0:T], zT[:, Z_AU + c, 0:T], amix[:], mult))
                tt(zT[:, Z_AU:Z_AU + 4, T:N], zT[:, Z_AU:Z_AU + 4, T:N], asmp[:], mult)

        def slice_dve(g):
            dve.wait_ge(slice_mm, g - SLICE0 + 1)
            if g < SLICE0 + 2:
                keys(g - SLICE0)
            elif g < SLICE0 + 10:
                h = (g - SLICE0 - 2) // 2
                (outputs if (g - SLICE0) % 2 else scores)(h)
            else:
                late(g)
            dve.drain().then_inc(slice_read, 1)
            dve.wait_ge(slice_read, g - SLICE0 + 1)

        def b_operands():
            for kv in range(2):
                for q in range(2):
                    nc.vector.tensor_copy(kd[64 * q:64 * q + 64, kv, :], zT[64 * kv:64 * kv + 64, Z_BK, :])
            link(nc.vector.memset(qb_[:], 0.0))
            for kv in range(2):
                for q in range(2):
                    o = nc.vector.tensor_copy(
                        qb_[64 * kv:64 * kv + 64, :, :].rearrange("p b (u q) -> p q u b", q=2)[:, q, 4 * kv:4 * kv + 4, :],
                        zT[64 * q:64 * q + 64, Z_BQ + 4 * kv:Z_BQ + 4 * kv + 4, T:N])
            o.then_inc(s("b_q8"), 1)

        slice_dve(SLICE0)
        for u in range(SLICE0 + 1, Z_N):
            dve.wait_ge(w_used, 4 * u + 8)
            tt(halves(zT[:, u, :]), pair(2 * (u % 2)), halves(rs1[:]), mult).then_inc(z_free, 1)
            if u == Z_N - 1:
                b_operands()
            slice_dve(u)

        for name, credit in (("b_o", 2), ("b_pt", 2), ("b_turn", 4), ("b_sc_free", 2), ("b_o_free", 2)):
            dve.nop().then_inc(s(name), credit)
        dve.wait_ge(s("b_vk_a"), 1)
        dve.wait_ge(s("b_q8"), 1)
        dve.drain().then_inc(s("b_vk"), 1)
        dve.wait_ge(s("b_in"), 64)
        dve.wait_ge(s("b_s8t"), 1)
        link(nc.vector.tensor_copy(s_s[:, P:P + 1], bsink[:]))
        link(nc.vector.tensor_tensor_reduce(out=s_s[:, 0:P], in0=ps[:, 3, 0:P], in1=bias_s[:], scale=0.125,
                                            scalar=s_s[:, P:P + 1], op0=add, op1=mx, accum_out=mxn[:, 0, 0, 0:1]))
        ts(mxn[:, 0, 0, 1:2], mxn[:, 0, 0, 0:1], -1.0, None, mult).then_inc(s("b_max8"), 1)
        dve.wait_ge(s("b_exp8"), 1)
        link(nc.vector.reciprocal(mxn[:, 0, 0, 3:4], mxn[:, 0, 0, 2:3]))
        ts(s_s[:, 0:P], s_s[:, 0:P], mxn[:, 0, 0, 3:4], None, mult).then_inc(s("b_p8"), 1)
        dve.wait_ge(s("c_sig"), 1)
        for h in range(4):
            tt(zT[:, Z_CO + h, :], zT[:, Z_CV + h, :], zT[:, Z_CO + h, :], mult)
        dve.wait_ge(s("b_o8"), 1)
        for kv in range(2):
            for q in range(2):
                o = nc.vector.tensor_copy(
                    zT[64 * q:64 * q + 64, Z_BQ + 4 * kv:Z_BQ + 4 * kv + 4, T:N],
                    ps[64 * kv:64 * kv + 64, 3, 0:P].rearrange("p (b u q) -> p q u b", q=2, u=8)[:, q, 4 * kv:4 * kv + 4, :])
        o.then_inc(s("b_o8_read"), 1)
        dve.wait_ge(s("b_o8_read"), 1)
        STEPS = 16 * 2
        with dve.Fori(0, 2) as it:
            first = it * 16
            mine = it * STEPS
            told = [0]

            def then(ins):
                told[0] += 1
                ins.then_inc(s("b_steps"), 1)
                dve.wait_ge(s("b_steps"), mine + told[0])

            def stage_queries(n):
                u = it * 2 + (4 * (n // 8) + n // 4 % 2)
                nc.vector.tensor_copy(qst[:, n // 4 % 2, 0:T], zT[:, bass.ds(u + Z_BQ, 1), 0:T].rearrange("p a n -> p (a n)"))\
                    .then_inc(s("b_pair"), 1)

            def score(n):
                sl, lo = n // 4 % 2, 0 if n % 4 else P
                u = it * 2 + (4 * (n // 8) + sl)
                if n % 4 == 0:
                    dve.wait_ge(bias_in[sl], it * 32 + (16 * (n // 8) + 16))
                dve.wait_ge(s("b_turn"), first + (n + 1))
                begun(dve)
                then(nc.vector.tensor_copy(sx[:, n % 4, :, 256], sinkbc[:, bass.ds(u * 2, 2)]))
                dve.wait_ge(s("b_qk"), first + (n + 1))
                begun(dve)
                for r in range(2):
                    ins = nc.vector.tensor_tensor_reduce(
                        out=sx[:, n % 4, r, lo:256], in0=ps[:, 4 - 2 * r + n % 2, lo:256],
                        in1=bst[:, sl, r, lo:256], scale=0.125, scalar=sx[:, n % 4, r, 256:257], op0=add, op1=mx,
                        accum_out=mxn[:, n % 4, r, 0:1])
                ins.then_inc(s("b_sc_free"), 1)
                dve.wait_ge(s("b_sc_free"), first + (n + 3))
                ts(mxn[:, n % 4, :, 1], mxn[:, n % 4, :, 0], -1.0, None, mult).then_inc(s("b_max"), 1)

            def scale(n):
                lo = 0 if n % 4 else P
                dve.wait_ge(s("b_exp"), first + (n + 1))
                then(nc.vector.reciprocal(mxn[:, n % 4, :, 3], mxn[:, n % 4, :, 2]))
                for r in range(2):
                    ins = ts(sx[:, n % 4, r, lo:256], sx[:, n % 4, r, lo:256], mxn[:, n % 4, r, 3:4], None, mult)
                ins.then_inc(s("b_prob"), 1)

            def read_o(n):
                u = it * 2 + (4 * (n // 8) + n // 4 % 2)
                dve.wait_ge(s("b_o"), first + (n + 3))
                begun(dve)
                nc.vector.tensor_copy(zT[:, bass.ds(u + Z_BQ, 1), (n % 4) * P:(n % 4 + 1) * P].rearrange("p a n -> p (a n)"),
                                      ps[:, 7 * (n % 2), 0:P]).then_inc(s("b_o_free"), 1)

            stage_queries(0)
            for n in range(16 + 5):
                if n < 16:
                    score(n)
                if n < 12 and n % 4 == 2:
                    stage_queries(n + 2)
                if 1 <= n < 17:
                    scale(n - 1)
                if n >= 5:
                    read_o(n - 5)
            assert told[0] == STEPS
        dve.wait_ge(s("b_o_free"), 34)
        dve.drain().then_inc(s("b_ended"), 2)
        barrier(dve, 1)

        for i, c in enumerate(K_ORDER):
            dve.wait_ge(mix_hi, i + 1)
            tt(act_lo[:, c, :], zT[:, MIX_TILES[c], :], act_hi[:, c, :].bitcast(F32), sub).then_inc(mix_lo, 1)

        dve.wait_ge(spilled, 32)
        dve.wait_ge(mix_lo, KC)
        link(nc.vector.memset(ssum[:], 0.0))

        def one(ap):
            return ap.rearrange("p a n -> p (a n)")

        def residual(i, u):
            n = i * 2 + (u - U_OUT)
            tile = bass.ds(n, 1)
            begun(dve)
            nc.vector.tensor_copy(gain2[:, u:u + 1], vecs[:, bass.ds(n + G2, 1)])
            dve.wait_ge(w_used, i * 8 + (4 * u + 8))
            x2 = xT[:, tile, :].rearrange("p a (h n) -> p (a h) n", h=2)
            tt(x2, pair(2 * u), x2, add).then_inc(z_free, 1)
            dve.wait_ge(z_free, n + (Z_N + 3))
            dve.wait_ge(s("o_sq"), n + 1)
            tt(ssum[:], ssum[:], ssq[:, u, :], add).then_inc(s("o_sum"), 1)
            dve.wait_ge(s("h2_hi"), n + 1)
            stt(out=one(h2_lo[:, tile, :]), in0=one(xT[:, tile, :]), scalar=gain2[:, u:u + 1],
                in1=one(h2_hi[:, tile, :]).bitcast(F32), op0=mult, op1=sub).then_inc(s("h2_lo"), 1)
            dve.wait_ge(s("h2_lo"), n + 1)

        with dve.Fori(U_OUT // 2, U_FFN // 2) as i:
            for u in range(2):
                residual(i, u)
        dve.wait_ge(w_used, USED_OUT)
        link(nc.vector.memset(zg[:, 0:2], 0.0))
        link(nc.vector.memset(za[:, 0:2], 0.0))
        dve.wait_ge(s("o_sum_mm"), 1)
        ts(halves(rs2[:]), pair(4), 1.0 / D, EPS, mult, add).then_inc(s("o_mean"), 1)
        dve.nop().then_inc(s("d_add"), 2)
        dve.wait_ge(s("o_root"), 1)
        link(nc.vector.reciprocal(rs2[:], rs2[:]))

        def ffn_group_dve(u0, n0, d0, base, tail, with_down):
            told = [0]

            def then(ins):
                told[0] += 1
                ins.then_inc(s("f_steps"), 1)
                dve.wait_ge(s("f_steps"), base + told[0])

            def read(n, half, unit, j):
                z, name, bank = ((zg, "f_zg", 0), (za, "f_za", 2))[half]
                dve.wait_ge(w_used, u0 * 4 + (4 * unit + 8))
                tt(halves(z[:, 2:]), pair(bank), halves(rs2[:]), mult).then_inc(s(name), 1)
                dve.wait_ge(s(name), n + 1)
                begun(dve)
                nc.vector.tensor_copy(ztail[:, bass.ds(tail(half, j), 1), :].rearrange("p a n -> p (a n)"), z[:, T:])\
                    .then_inc(z_free, 1)

            def conv(n, half, j):
                z, c_, name = ((zg, cg, "f_tg"), (za, ca, "f_ta"))[half]
                par = cpar[:, half, j, :]
                dve.wait_ge(s(name), n + 1)
                old = par[:, 0:16].rearrange("p (b t) -> p t b", t=2)
                for tap, from_col in ((1, 1), (0, 0)):
                    stt(out=c_[:, T:N], in0=old[:, tap, :], scalar=par[:, 16 + tap:17 + tap], in1=c_[:, T:N],
                        op0=mult, op1=add)
                    ins = stt(out=c_[:, 0:T], in0=z[:, from_col:from_col + T], scalar=par[:, 16 + tap:17 + tap],
                              in1=c_[:, 0:T], op0=mult, op1=add)
                    if tap:
                        then(ins)
                if half:
                    then(ins)
                else:
                    ins.then_inc(s("f_cg"), 1)

            def gate(n, j):
                dve.wait_ge(s("f_silu"), n + 1)
                tt(gm[:], cg[:], ca[:], mult).then_inc(s("f_m"), 1)
                dve.wait_ge(s("f_m"), n + 1)

            def lo(n, j):
                dve.wait_ge(s("g_hi"), n + 1)
                tt(g_lo[:, j, :], gm[:], g_hi[:, j, :].bitcast(F32), sub).then_inc(s("g_lo"), 1)

            def down(m, k):
                e = 4 * m + k
                dve.wait_ge(w_used, u0 * 4 + (4 * (2 + m) + k + 5))
                x2 = halves(xT[:, e, :])
                tt(x2, pair(4 + 2 * (k % 2)), x2, add).then_inc(s("d_add"), 1)

            for j in range(GC):
                g = 2 * j + (GC if with_down and j else 0)
                n = n0 + j
                read(n, 0, g, j)
                read(n, 1, g + 1, j)
                conv(n, 0, j)
                if with_down and j == 0:
                    down(0, 0)
                conv(n, 1, j)
                if with_down and j == 0:
                    down(0, 1)
                gate(n, j)
                if with_down and j == 0:
                    for e in range(2, 16):
                        down(e // 4, e % 4)
                lo(n, j)
            return told[0]

        steps = ffn_group_dve(U_FFN, 0, None, 0, lambda half, j: FC * half + j, False)
        with dve.Fori(1, NG) as i:
            assert ffn_group_dve(i * 12 + (U_FFN + U_GRP - 12), i * GC, i * 16 - 16, i * steps,
                                 lambda half, j: i * GC + (FC * half + j), True) == steps
        for e in range(16):
            dve.wait_ge(w_used, 4 * (U_ALL - GC) + e + 5)
            x2 = halves(xT[:, e, :])
            tt(x2, pair(4 + 2 * (e % 2)), x2, add).then_inc(s("d_add"), 1)
            if e:
                read_y(dve, e - 1)
        read_y(dve, 15)

    @block.gpsimd
    def _(pool):
        link = Chain(pool, chain_p)
        link(nc.gpsimd.memset(ident[:], 0.0))
        link(nc.gpsimd.affine_select(out=ident[:], in_=ident[:], compare_op=ALU.not_equal, fill=1.0, base=0,
                                     pattern=[[-1, P]], channel_multiplier=1))
        link(nc.gpsimd.memset(band[:], 0.0))
        link(nc.gpsimd.memset(band[:, 3:4], 1.0))
        nc.gpsimd.memset(ones[:], 1.0).then_inc(const_made, 1)
        pool.wait_ge(const_made, 1)
        nc.gpsimd.memset(whi[:].rearrange("p q c n -> p (q c n)").bitcast(F32), 0.0).then_inc(ring_zero, 1)
        nc.gpsimd.memset(wlo[:].rearrange("p q c n -> p (q c n)").bitcast(F32), 0.0).then_inc(ring_zero, 1)
        link(nc.gpsimd.memset(pairones[:], 0.0))
        for q in range(2):
            link(nc.gpsimd.memset(pairones[64 * q:64 * q + 64, 64 * q:64 * q + 64], 1.0))
        link(nc.gpsimd.memset(causal[:], 0.0))
        link(nc.gpsimd.affine_select(out=causal[:], in_=causal[:], compare_op=ALU.is_ge, fill=NEG, base=0,
                                     pattern=[[1, P]], channel_multiplier=-1))
        for h in range(4):
            link(nc.gpsimd.tensor_copy(sel[:, h, :], ident[0:4, h:h + 1].broadcast_to([4, P])))
        pool.wait_ge(wg_hi, 1)
        pool.wait_ge(ring_zero, 2)
        gates = wg_raw[:].rearrange("p (c k) n -> p k c n", k=4)
        for rows in (0, 32):
            from_col = rows // 8
            g = nc.gpsimd.tensor_tensor(wlo[:, :, :, rows:rows + 4], gates[:, :, :, from_col:from_col + 4],
                                        whi[:, :, :, rows:rows + 4].bitcast(F32), ALU.subtract)
        g.then_inc(wg_lo, 1)

        def split_pairs(first, last):
            with pool.Fori(first, last) as i:
                for u in range(2):
                    for k in range(4):
                        pool.wait_ge(w_hi, i * 8 + (4 * u + k + 1))
                        nc.gpsimd.tensor_tensor(wlo[:, k, :, :], rawq(k, u), whi[:, k, :, :].bitcast(F32),
                                                ALU.subtract).then_inc(w_lo, 1)

        split_pairs(0, Z_N // 2)
        pool.wait_ge(s("a_wt_read"), 1)
        nc.gpsimd.affine_select(out=wst[:], in_=wst[:], compare_op=ALU.is_ge, fill=0.0, base=0,
                                pattern=[[0, 4], [1, P]], channel_multiplier=-1).then_inc(s("a_wst"), 1)
        barrier(pool, 1)
        split_pairs(Z_N // 2, U_ALL // 2)

    @block.sync
    def _(sp):
        for i in range(NB):
            sp.dma_start(xtok[:, i, :], io["x_prompt"][0, i * P:(i + 1) * P, :]).then_inc(x_in[i], 16)
        sp.dma_start(xtok[0:S, 4, :], io["x_sample"].rearrange("b t d -> (b t) d")).then_inc(x_in[4], 16)

        sp.dma_start(wg_raw[:], w_in[:, COL_G:COL_G + 8].rearrange("(c p) n -> p c n", p=P)).then_inc(wg_in, 16)

        def load_pair(sources, split, down=False):
            for u in range(2):
                if split is not None:
                    sp.wait_ge(w_lo, split + 4 * u)
                sp.dma_start(unit_dst(u, down), sources[u]).then_inc(raw_in[u], 16)

        sp.wait_ge(x_in[2], 16)
        load_pair([cols_of(w_in, COL_C), cols_of(w_in, COL_C + P)], None)
        sp.dma_start(rel33[0:32, :], io["rel_bias"]).then_inc(s("rel_in"), 16)
        sp.dma_start(hot[:], io["bucket_table"]).then_inc(s("rel_in"), 16)
        cgb = io["c_gate_bias"].rearrange("l g -> g l")
        sp.dma_start(gbi[:], cgb[0:4]).then_inc(misc_in, 16)
        sp.dma_start(gbf[32:36, :], cgb[4:8]).then_inc(misc_in, 16)
        sp.dma_start(m0[:], io["state_mlstm_m"].rearrange("l b h -> h (l b)")).then_inc(misc_in, 16)
        for q in range(2):
            sp.dma_start(ns[64 * q:64 * q + 64, :],
                          io["state_mlstm_n"].rearrange("l b (k two) d -> two d (l b k)", two=2)[q]).then_inc(s("n_in"), 16)
        sp.dma_start(io["ffn_conv_sample"][0, :, 0, :], io["state_ffn_conv"][0, :, 1, :]).then_inc(s("conv_moved"), 16)

        load_pair([cols_of(w_in, COL_C + 2 * P), cols_of(w_in, COL_C + 3 * P)], 4)
        sp.wait_ge(x_ev_a, 8)
        sp.wait_ge(x_ev_v, 9)
        sp.dma_start(spill, xT[:].rearrange("p c n -> p (c n)")).then_inc(spilled, 16)
        for a, b, col, unit in ((2, 6, COL_C, Z_CQ), (6, 8, COL_AV, Z_AV), (8, 9, COL_BK, Z_BK),
                                (9, 13, COL_BQ, Z_BQ), (13, 15, COL_AU, Z_AU)):
            with sp.Fori(a, b) as i:
                load_pair([cols_of(w_in, i * (2 * P) + (col + (u - unit) * P)) for u in range(2)], i * 8 - 4)
        load_pair([cols_of(w_out, 0), cols_of(w_out, P)], 4 * Z_N - 4)
        sp.wait_ge(w_used, USED_IN)
        sp.wait_ge(s("rel_out"), 16)
        for n, u in enumerate((0, 1, 4, 5, 2, 3, 6, 7)):
            if n >= 2:
                sp.wait_ge(s("b_sc_free"), 4 * n - 2)
            sp.dma_start(bst[:, u % 2, :, :], bass.AP(tensor=bias_rows.tensor, offset=P - 1 + 2 * u * BIAS_PITCH,
                                                       ap=[[383, P], [BIAS_PITCH, 2], [1, 256]])).then_inc(bias_in[u % 2], 16)
        sp.wait_ge(stage, 4)
        sp.dma_start(xT[:].rearrange("p c n -> p (c n)"), spill).then_inc(spilled, 16)
        with sp.Fori(U_OUT // 2 + 1, U_FFN // 2) as i:
            load_pair([cols_of(w_out, i * (2 * P) + (u - U_OUT) * P) for u in range(2)], i * 8 - 4)

        def params_of(name, col):
            flat = {"state_ffn_conv": "l b j f -> (l b j) f", "ffn_conv_w": "l j f -> (l j) f", "ffn_conv_b": "l f -> l f"}
            return io[name].rearrange(flat[name]).rearrange("r (h f) -> r h f", h=2)[:, :, bass.ds(col, GC * P)]

        def load_group(grp, col, split, with_down):
            def up(j):
                return [cols_of(w_up, col + j * P), cols_of(w_up, col + (FF + j * P))]

            if not with_down:
                load_pair(up(0), split)
                sp.wait_ge(w_used, USED_OUT)
            else:
                sp.wait_ge(s("par_turn"), grp)
            for rows, name in (((0, 16), "state_ffn_conv"), ((16, 19), "ffn_conv_w"), ((19, 20), "ffn_conv_b")):
                sp.dma_start(par_rows[rows[0]:rows[1], :, :], params_of(name, col)).then_inc(s("par_in"), 16)
            if with_down:
                load_pair(up(0), split)
                load_pair([down_of(col - GC * P, m) for m in (0, 1)], split + 8, True)
                load_pair([down_of(col - GC * P, m) for m in (2, 3)], split + 16, True)
            for j in range(1, GC):
                load_pair(up(j), split + 8 * (j + (2 if with_down else 0)))

        load_group(0, 0, 4 * U_FFN - 4, False)
        with sp.Fori(1, NG) as i:
            load_group(i, i * (GC * P), i * 48 + 4 * (U_FFN + U_GRP - 12) - 4, True)
        for m in (0, 2):
            load_pair([down_of((NG - 1) * GC * P, mm) for mm in (m, m + 1)],
                      4 * (U_ALL - GC + m) - 4, True)
        for q in range(4):
            if q == 3:
                sp.wait_ge(s("t_read"), FC // 2)
                store(sp, io["ffn_conv_prompt"][0, 0], trow[0:2, :])
                store(sp, io["ffn_conv_sample"][0, :, 1, :], trow[2:2 + S, :])
            sp.wait_ge(s("y_read"), 4 * q + 4)
            store(sp, io["y_prompt"][0, :, q * 512:(q + 1) * 512].rearrange("(j p) d -> p j d", p=P),
                  ytok[:, :, q * 512:(q + 1) * 512])
        sp.wait_ge(s("y8_read"), 1)
        store(sp, io["y_sample"].rearrange("b t d -> (b t) d"), ytok8[:])
        sp.wait_ge(out_done, out_count[0])
        sp.wait_ge(s("conv_moved"), 16)

    ctx.close()


_INS = ["x_prompt", "x_sample", "cache_swa_k", "cache_swa_v", "state_mlstm_C", "state_mlstm_n", "state_mlstm_m",
        "state_ffn_conv", "rel_bias", "norm1", "w_in", "a_v_gain", "a_spatial_w", "a_spatial_b", "b_q_gain",
        "b_k_gain", "b_sinks", "c_gate_bias", "c_h_gain", "w_out", "norm2", "w_up", "ffn_conv_w", "ffn_conv_b",
        "w_down"]
_OUTS = [("y_prompt", (1, T, D)), ("y_sample", (S, 1, D)),
         ("k_prompt", (1, 1, WINDOW, 2, 64)), ("v_prompt", (1, 1, WINDOW, 2, 64)),
         ("k_sample", (1, S, 1, 2, 64)), ("v_sample", (1, S, 1, 2, 64)),
         ("C_prompt", (1, 1, 4, 64, 128)), ("n_prompt", (1, 1, 4, 64)), ("m_prompt", (1, 1, 4)),
         ("C_sample", (1, S, 4, 64, 128)), ("n_sample", (1, S, 4, 64)), ("m_sample", (1, S, 4)),
         ("ffn_conv_prompt", (1, 1, 2, F2)), ("ffn_conv_sample", (1, S, 2, F2)), ("chunk_v", (1, S, 1, 512))]


def kernel(**inputs):
    import concourse.bacc as bacc
    from concourse.bass_utils import run_bass_kernel_spmd

    nc = bacc.Bacc("TRN2", target_bir_lowering=False, num_devices=1)
    arrays = {f"in_{n}": np.ascontiguousarray(inputs[n]) for n in _INS}
    arrays["in_bucket_table"] = bucket_table()
    io = {n[3:]: nc.dram_tensor(n, a.shape, F32, kind="ExternalInput").ap() for n, a in arrays.items()}
    for n in ("w_in", "w_out", "w_up", "w_down"):
        io[n] = io[n][0]
    for n, shape in _OUTS:
        io[n] = nc.dram_tensor(f"out_{n}", shape, F32, kind="ExternalOutput").ap()
    hybrid_layer(nc, io)
    r = run_bass_kernel_spmd(nc, [arrays], core_ids=[0])
    return tuple(r.results[0][f"out_{n}"] for n, _ in _OUTS)
```
